# Optimizing a Trainium2 kernel written in Bass

```python
import jax
import jax.numpy as jnp
from jax import lax
import numpy as np

D_MODEL = 1024
BATCH = 1
SEQ = 512
DEPTH = 1
DEC_BATCH = 8
DEC_SEQ = 16
PAST_LEN = 1024

CHUNK = 64
N_PAST_CHUNKS = 8
BAND_CHUNKS = N_PAST_CHUNKS + 1
BAND = BAND_CHUNKS * CHUNK
A_HEADS = 8
A_HEAD_DIM = 64
A_WIDTH = A_HEADS * A_HEAD_DIM
REL_CLIP = 128
G_HEADS = 4
G_DK = 64
G_DV = 128
G_WIDTH = G_HEADS * G_DV
G_GATE_RANK = 16
G_GATE_NORM = 16.0
G_BLOCK = 16
MIX_WIDTH = A_WIDTH + G_WIDTH
N_MEM = 256
X_HEADS = 4
X_HEAD_DIM = D_MODEL // X_HEADS
X_WIDTH = X_HEADS * X_HEAD_DIM
P_HEADS = 8
P_NKEYS = 128
P_EXPERTS = P_NKEYS * P_NKEYS
P_QDIM = 256
P_HALF = P_QDIM // 2
P_TOPK = 16
P_TOKEN_BLOCK = 128
EPS = 1e-6
IN_WIDTH = 3 * A_WIDTH + 2 * G_HEADS * G_DK + G_WIDTH + G_GATE_RANK + G_WIDTH
SPLITS = (A_WIDTH, 2 * A_WIDTH, 3 * A_WIDTH,
          3 * A_WIDTH + G_HEADS * G_DK,
          3 * A_WIDTH + 2 * G_HEADS * G_DK,
          3 * A_WIDTH + 2 * G_HEADS * G_DK + G_WIDTH,
          3 * A_WIDTH + 2 * G_HEADS * G_DK + G_WIDTH + G_GATE_RANK)

kernel_name = 'hymba_style_chunkband_gla_peer_stream_step'

def rmsnorm(x, g):
    xf = x.astype(jnp.float32)
    y = xf * lax.rsqrt(jnp.mean(xf * xf, axis=-1, keepdims=True) + EPS)
    return (y * g.astype(jnp.float32)).astype(x.dtype)

def mixer_inputs(x, g_mix, w_in, g_q, g_k, w_gate2, b_gate2):
    b, t, _ = x.shape
    z = rmsnorm(x, g_mix) @ w_in
    qa, ka, va, qg, kg, vg, gl, r = jnp.split(z, SPLITS, axis=-1)
    qa = rmsnorm(qa.reshape(b, t, A_HEADS, A_HEAD_DIM), g_q)
    ka = rmsnorm(ka.reshape(b, t, A_HEADS, A_HEAD_DIM), g_k)
    va = va.reshape(b, t, A_HEADS, A_HEAD_DIM)
    qg = qg.reshape(b, t, G_HEADS, G_DK) * (G_DK ** -0.5)
    kg = kg.reshape(b, t, G_HEADS, G_DK)
    vg = vg.reshape(b, t, G_HEADS, G_DV)
    log_a = jax.nn.log_sigmoid((gl @ w_gate2 + b_gate2).astype(jnp.float32)) / G_GATE_NORM
    log_a = log_a.reshape(b, t, G_HEADS, G_DK)
    return qa, ka, va, qg, kg, vg, log_a, r

def rel_bias_lookup(rel_bias, rel):
    return rel_bias[:, jnp.clip(rel, -REL_CLIP, REL_CLIP) + REL_CLIP].astype(jnp.float32)

def chunk_band_attention_prompt(q, k, v, rel_bias):
    b, s, h, dh = q.shape
    nc = s // CHUNK
    qc = q.reshape(b, nc, CHUNK, h, dh)
    padw = ((0, 0), (N_PAST_CHUNKS, 0), (0, 0), (0, 0), (0, 0))
    kc = jnp.pad(k.reshape(b, nc, CHUNK, h, dh), padw)
    vc = jnp.pad(v.reshape(b, nc, CHUNK, h, dh), padw)
    k_band = jnp.concatenate([kc[:, i:i + nc] for i in range(BAND_CHUNKS)], axis=2)
    v_band = jnp.concatenate([vc[:, i:i + nc] for i in range(BAND_CHUNKS)], axis=2)
    qi = jnp.arange(CHUNK)
    kj = jnp.arange(BAND)
    bias = rel_bias_lookup(rel_bias, N_PAST_CHUNKS * CHUNK + qi[:, None] - kj[None, :])
    key_pos = (jnp.arange(nc)[:, None] - N_PAST_CHUNKS) * CHUNK + kj[None, :]
    valid = (key_pos >= 0)[None, :, None, None, :]
    scores = jnp.einsum('bnqhd,bnkhd->bnhqk', qc, k_band).astype(jnp.float32) * (dh ** -0.5) + bias[None, None]
    scores = jnp.where(valid, scores, -1e30)
    p = jax.nn.softmax(scores, axis=-1).astype(v.dtype)
    o = jnp.einsum('bnhqk,bnkhd->bnqhd', p, v_band)
    return o.reshape(b, s, h * dh)

def chunk_band_attention_sample(q, k_new, v_new, k_cache, v_cache, rel_bias):
    b, t, h, dh = q.shape
    r = k_cache.shape[1]
    q_pos = PAST_LEN + jnp.arange(t)
    k_pos = jnp.concatenate([PAST_LEN - r + jnp.arange(r), q_pos])
    k_all = jnp.concatenate([k_cache.astype(k_new.dtype), k_new], axis=1)
    v_all = jnp.concatenate([v_cache.astype(v_new.dtype), v_new], axis=1)
    bias = rel_bias_lookup(rel_bias, q_pos[:, None] - k_pos[None, :])
    qch = q_pos[:, None] // CHUNK
    kch = k_pos[None, :] // CHUNK
    valid = (kch <= qch) & (kch >= qch - N_PAST_CHUNKS)
    scores = jnp.einsum('bqhd,bkhd->bhqk', q, k_all).astype(jnp.float32) * (dh ** -0.5) + bias[None]
    scores = jnp.where(valid[None, None], scores, -1e30)
    p = jax.nn.softmax(scores, axis=-1).astype(v_all.dtype)
    o = jnp.einsum('bhqk,bkhd->bqhd', p, v_all)
    return o.reshape(b, t, h * dh)

def gla_scan(q, k, v, log_a, s0):
    b, t, h, dk = q.shape
    pad = (-t) % G_BLOCK
    padw = ((0, 0), (0, pad), (0, 0), (0, 0))
    q, k, v, log_a = [jnp.pad(a.astype(jnp.float32), padw) for a in (q, k, v, log_a)]
    nb = (t + pad) // G_BLOCK

    def blocks(a):
        return jnp.moveaxis(a.reshape(b, nb, G_BLOCK, h, a.shape[-1]), 1, 0)

    causal = jnp.tril(jnp.ones((G_BLOCK, G_BLOCK), dtype=bool))[None, :, :, None, None]

    def step(state, inp):
        qb, kb, vb, lab = inp
        cum = jnp.cumsum(lab, axis=1)
        o_inter = jnp.einsum('blhk,bhkv->blhv', qb * jnp.exp(cum), state)
        diff = cum[:, :, None] - cum[:, None, :]
        decay = jnp.exp(jnp.where(causal, diff, -jnp.inf))
        att = jnp.einsum('bqhk,bshk,bqshk->bhqs', qb, kb, decay)
        o_intra = jnp.einsum('bhqs,bshv->bqhv', att, vb)
        last = cum[:, -1]
        k_dec = kb * jnp.exp(last[:, None] - cum)
        state = jnp.exp(last)[..., None] * state + jnp.einsum('bshk,bshv->bhkv', k_dec, vb)
        return state, o_inter + o_intra

    s_final, o = lax.scan(step, s0.astype(jnp.float32), (blocks(q), blocks(k), blocks(v), blocks(log_a)))
    o = jnp.moveaxis(o, 0, 1).reshape(b, nb * G_BLOCK, h, -1)[:, :t]
    return o, s_final

def mixer_output(oa, og, r, g_gla_out, w_out):
    b, t = oa.shape[:2]
    og = rmsnorm(og.astype(r.dtype), g_gla_out).reshape(b, t, G_WIDTH) * jax.nn.silu(r)
    return jnp.concatenate([oa.astype(r.dtype), og], axis=-1) @ w_out

def mem_kv(mem, g_mem, w_ck, w_cv, g_ck):
    m = rmsnorm(mem, g_mem)
    b, n, _ = m.shape
    k = rmsnorm((m @ w_ck).reshape(b, n, X_HEADS, X_HEAD_DIM), g_ck)
    v = (m @ w_cv).reshape(b, n, X_HEADS, X_HEAD_DIM)
    return k, v

def cross_attend(h, mem_k, mem_v, w_cq, g_cq, w_co):
    b, t, _ = h.shape
    q = rmsnorm((h @ w_cq).reshape(b, t, X_HEADS, X_HEAD_DIM), g_cq)
    s = jnp.einsum('bqhd,bkhd->bhqk', q, mem_k.astype(q.dtype)).astype(jnp.float32) * (X_HEAD_DIM ** -0.5)
    p = jax.nn.softmax(s, axis=-1).astype(q.dtype)
    o = jnp.einsum('bhqk,bkhd->bqhd', p, mem_v.astype(q.dtype)).reshape(b, t, X_WIDTH)
    return o @ w_co

def peer_ffn(h, w_pq, sub_keys1, sub_keys2, expert_u, expert_v):
    lead = h.shape[:-1]
    xt = h.reshape(-1, D_MODEL)
    n = xt.shape[0]
    qry = (xt @ w_pq).reshape(n, P_HEADS, 2, P_HALF).astype(jnp.float32)
    s1 = jnp.einsum('nhd,kd->nhk', qry[:, :, 0], sub_keys1.astype(jnp.float32))
    s2 = jnp.einsum('nhd,kd->nhk', qry[:, :, 1], sub_keys2.astype(jnp.float32))
    v1, i1 = lax.top_k(s1, P_TOPK)
    v2, i2 = lax.top_k(s2, P_TOPK)
    cand = (v1[..., :, None] + v2[..., None, :]).reshape(n, P_HEADS, P_TOPK * P_TOPK)
    cand_idx = (i1[..., :, None] * P_NKEYS + i2[..., None, :]).reshape(n, P_HEADS, P_TOPK * P_TOPK)
    top_s, top_pos = lax.top_k(cand, P_TOPK)
    idx = jnp.take_along_axis(cand_idx, top_pos, axis=-1).reshape(n, P_HEADS * P_TOPK)
    gate = jax.nn.softmax(top_s, axis=-1).reshape(n, P_HEADS * P_TOPK).astype(xt.dtype)
    pad = (-n) % P_TOKEN_BLOCK
    xb = jnp.pad(xt, ((0, pad), (0, 0))).reshape(-1, P_TOKEN_BLOCK, D_MODEL)
    ib = jnp.pad(idx, ((0, pad), (0, 0))).reshape(-1, P_TOKEN_BLOCK, P_HEADS * P_TOPK)
    gb = jnp.pad(gate, ((0, pad), (0, 0))).reshape(-1, P_TOKEN_BLOCK, P_HEADS * P_TOPK)

    def block(args):
        xblk, iblk, gblk = args
        act = jax.nn.gelu(jnp.einsum('td,tkd->tk', xblk, expert_u[iblk]), approximate=False) * gblk
        return jnp.einsum('tk,tkd->td', act, expert_v[iblk])

    out = lax.map(block, (xb, ib, gb)).reshape(-1, D_MODEL)[:n]
    return out.reshape(*lead, D_MODEL)

def layer_tail(x, mem_k, mem_v, g_cross, w_cq, g_cq, w_co, g_ffn, w_pq, sub_keys1, sub_keys2, expert_u, expert_v):
    x = x + cross_attend(rmsnorm(x, g_cross), mem_k, mem_v, w_cq, g_cq, w_co)
    return x + peer_ffn(rmsnorm(x, g_ffn), w_pq, sub_keys1, sub_keys2, expert_u, expert_v)

def setup_inputs(seed: int = 0) -> dict:
    key = jax.random.key(seed)
    ks = iter(jax.random.split(key, 40))
    nrm = lambda shape, scale: jax.random.normal(next(ks), shape, jnp.float32) * scale
    gain = lambda shape: 1.0 + 0.02 * jax.random.normal(next(ks), shape, jnp.float32)
    r_cache = min(BAND, PAST_LEN)
    return {
        'x_prompt': nrm((BATCH, SEQ, D_MODEL), 1.0),
        'x_sample': nrm((DEC_BATCH, DEC_SEQ, D_MODEL), 1.0),
        'cache_att_k': nrm((DEPTH, DEC_BATCH, r_cache, A_HEADS, A_HEAD_DIM), 1.0),
        'cache_att_v': nrm((DEPTH, DEC_BATCH, r_cache, A_HEADS, A_HEAD_DIM), 1.0),
        'state_gla': nrm((DEPTH, DEC_BATCH, G_HEADS, G_DK, G_DV), 1.0),
        'cache_mem_k': nrm((DEPTH, DEC_BATCH, N_MEM, X_HEADS, X_HEAD_DIM), 1.0),
        'cache_mem_v': nrm((DEPTH, DEC_BATCH, N_MEM, X_HEADS, X_HEAD_DIM), 1.0),
        'mem_prompt': nrm((BATCH, N_MEM, D_MODEL), 1.0),
        'g_mix': gain((DEPTH, D_MODEL)),
        'w_in': nrm((DEPTH, D_MODEL, IN_WIDTH), D_MODEL ** -0.5),
        'g_q': gain((DEPTH, A_HEAD_DIM)),
        'g_k': gain((DEPTH, A_HEAD_DIM)),
        'rel_bias': nrm((DEPTH, A_HEADS, 2 * REL_CLIP + 1), 0.5),
        'w_gate2': nrm((DEPTH, G_GATE_RANK, G_HEADS * G_DK), G_GATE_RANK ** -0.5),
        'b_gate2': nrm((DEPTH, G_HEADS * G_DK), 0.1),
        'g_gla_out': gain((DEPTH, G_DV)),
        'w_out': nrm((DEPTH, MIX_WIDTH, D_MODEL), MIX_WIDTH ** -0.5),
        'g_cross': gain((DEPTH, D_MODEL)),
        'g_mem': gain((DEPTH, D_MODEL)),
        'w_cq': nrm((DEPTH, D_MODEL, X_WIDTH), D_MODEL ** -0.5),
        'w_ck': nrm((DEPTH, D_MODEL, X_WIDTH), D_MODEL ** -0.5),
        'w_cv': nrm((DEPTH, D_MODEL, X_WIDTH), D_MODEL ** -0.5),
        'g_cq': gain((DEPTH, X_HEAD_DIM)),
        'g_ck': gain((DEPTH, X_HEAD_DIM)),
        'w_co': nrm((DEPTH, X_WIDTH, D_MODEL), X_WIDTH ** -0.5),
        'g_ffn': gain((DEPTH, D_MODEL)),
        'w_pq': nrm((DEPTH, D_MODEL, P_HEADS * P_QDIM), D_MODEL ** -0.5),
        'sub_keys1': nrm((DEPTH, P_NKEYS, P_HALF), P_HALF ** -0.5),
        'sub_keys2': nrm((DEPTH, P_NKEYS, P_HALF), P_HALF ** -0.5),
        'expert_u': nrm((DEPTH, P_EXPERTS, D_MODEL), D_MODEL ** -0.5),
        'expert_v': nrm((DEPTH, P_EXPERTS, D_MODEL), P_HEADS ** -0.5),
    }

def reference(x_prompt, x_sample, cache_att_k, cache_att_v, state_gla, cache_mem_k, cache_mem_v, mem_prompt,
              g_mix, w_in, g_q, g_k, rel_bias, w_gate2, b_gate2, g_gla_out, w_out,
              g_cross, g_mem, w_cq, w_ck, w_cv, g_cq, g_ck, w_co,
              g_ffn, w_pq, sub_keys1, sub_keys2, expert_u, expert_v):
    xp = x_prompt
    xs = x_sample
    keep = min(BAND, xp.shape[1])
    p_k, p_v, p_g, p_mk, p_mv, s_k, s_v, s_g = [], [], [], [], [], [], [], []
    for l in range(DEPTH):
        qa, ka, va, qg, kg, vg, la, r = mixer_inputs(xp, g_mix[l], w_in[l], g_q[l], g_k[l], w_gate2[l], b_gate2[l])
        oa = chunk_band_attention_prompt(qa, ka, va, rel_bias[l])
        s0 = jnp.zeros((xp.shape[0], G_HEADS, G_DK, G_DV), jnp.float32)
        og, gp = gla_scan(qg, kg, vg, la, s0)
        xp = xp + mixer_output(oa, og, r, g_gla_out[l], w_out[l])
        mk, mv = mem_kv(mem_prompt, g_mem[l], w_ck[l], w_cv[l], g_ck[l])
        xp = layer_tail(xp, mk, mv, g_cross[l], w_cq[l], g_cq[l], w_co[l],
                        g_ffn[l], w_pq[l], sub_keys1[l], sub_keys2[l], expert_u[l], expert_v[l])
        p_k.append(ka[:, -keep:])
        p_v.append(va[:, -keep:])
        p_g.append(gp.astype(xp.dtype))
        p_mk.append(mk)
        p_mv.append(mv)
        qa, ka, va, qg, kg, vg, la, r = mixer_inputs(xs, g_mix[l], w_in[l], g_q[l], g_k[l], w_gate2[l], b_gate2[l])
        oa = chunk_band_attention_sample(qa, ka, va, cache_att_k[l], cache_att_v[l], rel_bias[l])
        og, gs = gla_scan(qg, kg, vg, la, state_gla[l])
        xs = xs + mixer_output(oa, og, r, g_gla_out[l], w_out[l])
        xs = layer_tail(xs, cache_mem_k[l], cache_mem_v[l], g_cross[l], w_cq[l], g_cq[l], w_co[l],
                        g_ffn[l], w_pq[l], sub_keys1[l], sub_keys2[l], expert_u[l], expert_v[l])
        s_k.append(ka)
        s_v.append(va)
        s_g.append(gs.astype(state_gla.dtype))
    return (xp, xs, jnp.stack(p_k), jnp.stack(p_v), jnp.stack(p_g), jnp.stack(p_mk), jnp.stack(p_mv),
            jnp.stack(s_k), jnp.stack(s_v), jnp.stack(s_g))


_drawn_inputs = setup_inputs


def setup_inputs(seed=0):
    import zlib

    import numpy as np

    out = dict(_drawn_inputs(seed))
    spreads = {}
    factors = {'g_q': 7.463,
     'g_k': 2.741,
     'g_gla_out': 3.234,
     'g_cross': 6.86,
     'g_mem': 2.909,
     'g_cq': 7.216,
     'g_ck': 2.718,
     'g_ffn': 4.074}
    for name, (base, spread) in spreads.items():
        noise = np.random.default_rng([zlib.crc32(name.encode()), seed]).standard_normal(out[name].shape)
        drawn = base * np.exp(spread * noise) if base else spread * noise
        out[name] = jnp.asarray(drawn.astype(out[name].dtype))
    for name, factor in factors.items():
        out[name] = (out[name] * factor).astype(out[name].dtype)
    return out
```

```python
from contextlib import ExitStack

import concourse.bass as bass
from concourse import mybir

F32 = mybir.dt.float32
F16 = mybir.dt.float16
U32 = mybir.dt.uint32
ALU = mybir.AluOpType
ACT = mybir.ActivationFunctionType
AX = mybir.AxisListType

P = 128
D = 1024
KT = D // P
SEQ, DEC_B, DEC_T = 512, 8, 16
T = SEQ + DEC_B * DEC_T
NT = T // P
PT_TILES = SEQ // P
AH, AD = 8, 64
GH, GK, GV = 4, 64, 128
CHUNK = 64
BANDK = 512
NEWK = BANDK + DEC_T
XH, XD, NMEM = 4, 256, 256
NK = 128
TOPK = 16
PH = 8
EPS = 1e-6
UNIT = 512
WSLOTS = 2
EB = 4
NBLK = NK // EB
TG = 32
NTG = T // TG
USCALE = 1024.0
NEG = -3.0e38
CREDIT = 16


def peer_stream_step(nc, x_in, mem_in, w_in, w_gl, w_out, w_cq, w_ck, w_cv, w_co, w_pq, wg2, gcols, grows,
                     bias_p, bias_s, kc_t, v_c, state_in, mk_c, mv_c, keys_t, u_t, v_t, consts,
                     y_out, k_out, v_out, gp_out, gs_out, mk_out, mv_out, w_dram):
    ctx = ExitStack()
    with ctx:
        def sem(name):
            return ctx.enter_context(nc.semaphore(name))

        AR = ctx.enter_context(nc.sbuf_tensor("arena", [P, 53200], F32))
        PS = ctx.enter_context(nc.psum_tensor("banks", [P, 8, 512], F32))

        def at(off, *shape):
            n = 1
            for s in shape:
                n *= s
            v = AR[:, off:off + n]
            if len(shape) == 2:
                v = v.rearrange("p (a b) -> p a b", a=shape[0])
            elif len(shape) == 3:
                v = v.rearrange("p (a b c) -> p a b c", a=shape[0], b=shape[1])
            elif len(shape) == 4:
                v = v.rearrange("p (a b c d) -> p a b c d", a=shape[0], b=shape[1], c=shape[2])
            return v

        X = at(0, NT, D)
        CB = 5120
        cons = at(CB, 128 * 5 + 130 + 136 + 8)
        ident = AR[:, CB:CB + 128]
        iota = AR[:, CB + 128:CB + 256]
        maskp = AR[:, CB + 256:CB + 384]
        masks = AR[:, CB + 384:CB + 512]
        trip = AR[:, CB + 512:CB + 642]
        tris = AR[:, CB + 642:CB + 778]
        bmask = AR[:, CB + 778:CB + 786]
        NCONST = 786
        gc_sb = at(CB + 786, 4, KT)
        gr_sb = AR[:, CB + 818:CB + 818 + 768]
        wg2_sb = AR[0:17, CB + 1586:CB + 1842]
        bs_sb = AR[:, CB + 1842:CB + 1842 + NEWK]
        eps_sb = AR[:, CB + 2370:CB + 2371]
        gq, gk, ggla = gr_sb[:, 0:64], gr_sb[:, 64:128], gr_sb[:, 128:256]
        gcq, gck = gr_sb[:, 256:512], gr_sb[:, 512:768]
        MM = 7500
        mv_tm = at(MM, 2, D)
        mkT = at(MM + 2048, 2 * XH, NMEM)
        BI = MM + 4096
        bias_ring = at(BI, 2, 512)
        smid_p = at(BI, 4, 2, P)
        H16 = MM
        hhi = AR[:, H16:H16 + 2560].bitcast(F16).rearrange("p (k t) -> p k t", k=KT)
        hlo = AR[:, H16 + 2560:H16 + 5120].bitcast(F16).rearrange("p (k t) -> p k t", k=KT)
        TA = 12620
        hT = at(TA, KT, T)
        memT = at(TA, KT, NMEM)
        mk_tm = at(TA + 2048, 2, D)
        glT = AR[0:17, TA + 4096:TA + 4096 + T]
        QZ = at(TA, 2, DEC_B, P)
        zz = at(TA + 2048, 2, 256)
        ll = at(TA + 2560, 2, 256)
        eplus = at(TA + 3072, 2, 2, 136)
        eminus = at(TA + 4736, 2, P)
        TB = 17740
        q_tm = at(TB, NT, 512)
        k_tm = at(TB + 2560, NT, 512)
        mixT = at(TB, KT, T)
        cq_tm = at(TB, NT, D)
        qry = at(TB, 8, T)
        V5 = 22860
        v_tm = at(V5, NT, 512)
        selT = at(V5, 3, T)
        G3 = V5 + 2560
        qk_tm = at(G3, NT, 512)
        vg = at(G3 + 2560, NT, 512)
        rr = at(G3 + 5120, NT, 512)
        smid_s = at(G3, DEC_B, 2, P)
        st_s = at(G3 + 2560, DEC_B, 2, P)
        khm = at(G3 + 5120, DEC_B, 256)
        kc_ring = at(G3, 2, 4, 512)
        vc_ring = at(G3 + 4096, 2, 4, 512)
        mkc_ring = at(G3, 2, 2 * XH, NMEM)
        mvc_ring = at(G3 + 4096, 2, 2, D)
        s_ring = at(G3, 2, NT, 4 * NK)
        top_v = at(G3 + 5120, NT, 2 * PH, TOPK)
        top_i = at(G3 + 6400, NT, 2 * PH * TOPK).bitcast(U32)
        QK = G3 + 8192
        qT = at(QK, 4, T)
        kT = at(QK + 2560, 4, T)
        cqT = at(QK, KT, T)
        cand = at(QK, PH, 256)
        eq = at(QK + 2048, P, TOPK)
        ts = at(QK + 4096, PH, TOPK)
        tp = AR[:, QK + 4224:QK + 4352].bitcast(U32)
        jf = at(QK + 4352, 2, P)
        ji = at(QK + 4608, 2, P).bitcast(U32)
        WR = QK + 5120
        ring = at(WR, WSLOTS, KT, UNIT)
        TM = WR + WSLOTS * 4096
        xn = at(TM, 2, D)
        junk = AR[:, TM + 2048:TM + 3072]
        er = at(TM + 3072, 2, 512)
        sq = at(TM + 4400, 2, 512)
        ATm = at(TM, 2, 2, P)
        kh_tm = at(TM + 1024, 2, 256)
        hats = at(TM + 2048, 2, 4, P)
        og = at(TM + 3072, 2, 512)
        S_sb = at(TM, 2, NEWK)
        PT_sb = at(TM + 1056, 2, 5, P)
        QB = at(TM + 2336, 4, DEC_B, 32)
        vn = at(TM + 3360, 2, 512)
        QX = at(TM + 2336, KT, DEC_B, 32)
        topif = at(TM, 2, PH, TOPK)
        wgl_sb = at(TM + 4096, KT, 16)
        sg = at(TM + 512, P)
        gsum = at(TM + 640, PH)
        srep = AR[:, TM + 1024:TM + 1280]
        keys_sb = at(TM + 4096, 2, NK)
        ST = TM + 5424
        hn_ss = at(ST, 2, 8)
        hn_rs = at(ST + 16, 2, 8)
        nrm_ss = at(ST + 32, 2, 1)
        nrm_rs = at(ST + 34, 2, 1)
        sm_nm = at(ST + 40, 2, 2)
        sm_sum = at(ST + 44, 2, 2)
        sm_inv = at(ST + 48, 2, 2)
        sm_max = at(ST + 52, 2, 2)
        S_p = at(TM + 6020, 2, P)
        R1, R2 = TA, G3 - 640
        ust = at(R1, 4, KT, P)
        u16 = AR[:, R1 + 4096:R1 + 8192].bitcast(F16).rearrange("p (s x k e) -> p s x k e", s=4, x=2, k=KT)
        gel = at(R1 + 8192, 2, T)
        vst = at(R2, 4, D)
        v16 = AR[:, R2 + 4096:R2 + 12288].bitcast(F16).rearrange("p (s x d) -> p s x d", s=2 * EB, x=2)
        a16 = AR[:, R2 + 12288:R2 + 17408].bitcast(F16).rearrange("p (s x t) -> p s x t", s=2 * EB, x=2)
        W_sb = at(R2 + 17408, 2, NTG, EB, TG)
        a32 = at(R2 + 22528, 2, T)
        stage = at(R2 + 12288, 2, NK, TG)
        A_oh = at(R2 + 23808, 16, NK)
        B_oh = at(R2 + 25856, 16, NK)

        bank_full = [sem(f"bank_full{b}") for b in range(8)]
        bank_free = [sem(f"bank_free{b}") for b in range(8)]
        x_in_s = sem("x_loaded")
        c_in = sem("consts_loaded")
        mem_in_s = [sem(f"mem_loaded{i}") for i in range(2)]
        w_in_s = [sem(f"weights_loaded{i}") for i in range(WSLOTS)]
        bias_s_ = [sem(f"bias_loaded{i}") for i in range(2)]
        kc_s = [sem(f"cache_k_loaded{i}") for i in range(2)]
        vc_s = [sem(f"cache_v_loaded{i}") for i in range(2)]
        vn_s = [sem(f"newv_loaded{i}") for i in range(2)]
        mkc_s = [sem(f"memcache_k_loaded{i}") for i in range(2)]
        mvc_s = [sem(f"memcache_v_loaded{i}") for i in range(2)]
        st_s_s = sem("states_loaded")
        keys_s = sem("keys_loaded")
        outs = {n: sem(f"{n}_stored") for n in ("v", "mk", "mv", "gp", "gs")}
        kout_s = sem("k_stored")
        y_s = sem("y_stored")
        dve_step = sem("dve_step")
        act_step = sem("act_step")
        zero_s = sem("tiles_cleared")
        nrm = {n: (sem(f"{n}_rstd"), sem(f"{n}_scaled")) for n in ("mix", "mem", "cross", "ffn")}
        hn = {n: tuple(sem(f"{n}_{w}") for w in ("squares", "sums", "rstd", "normed")) for n in ("qk", "mk", "gla", "cq")}
        r_exp = sem("r_exp")
        r_silu = sem("r_silu")
        g_l = sem("gate_log")
        g_la = sem("log_a")
        g_hat = sem("hats_ready")
        g_smid = sem("state_scaled")
        g_st = sem("state_updated")
        g_khm = sem("khat_masked")
        qb_s = sem("blockq_ready")
        sm = {n: tuple(sem(f"{n}_{w}") for w in ("max", "exp", "prob")) for n in ("att", "xat")}
        qx_s = sem("padded_q_ready")
        x_mix = sem("x_after_mix")
        x_cross = sem("x_after_cross")
        h_split = sem("h_split")
        tk_exp_in = sem("topk_shifted")
        tk_exp = sem("topk_exp")
        tk_done = sem("topk_selected")
        a_oh_s = sem("gate_onehots")
        b_oh_s = sem("key_onehots")
        wg_mm = sem("gate_mm_done")
        wg_ev = sem("gate_evacuated")
        wst_s = [sem(f"gate_stored{i}") for i in range(2)]
        u_in = [sem(f"u_loaded{i}") for i in range(4)]
        v_in = [sem(f"v_loaded{i}") for i in range(4)]
        W_in = [sem(f"gates_loaded{i}") for i in range(2)]
        u_hi = sem("u_high")
        u_sp = sem("u_split")
        v_hi = sem("v_high")
        v_sp = sem("v_split")
        z_mm = sem("z_done")
        z_ge = sem("gelu_done")
        a_mul = sem("act_gated")
        a_hi = sem("act_high")
        a_sp = sem("act_split")
        y_mm = sem("y_done")
        y_ev = sem("y_added")

        groups = {}
        uses = [0] * 8

        def open_group(pe, key):
            b = len(groups) % 8
            if uses[b]:
                pe.wait_ge(bank_free[b], uses[b])
            uses[b] += 1
            groups[key] = (b, uses[b])
            return PS[:, b, :], bank_full[b]

        def full(eng, *key):
            b, n = groups[key]
            eng.wait_ge(bank_full[b], n)
            return PS[:, b, :], bank_free[b]

        def drained(eng, *key):
            b, n = groups[key]
            eng.wait_ge(bank_free[b], n)

        count = {}

        def link(eng, ins, s):
            count[id(s)] = count.get(id(s), 0) + 1
            ins.then_inc(s, 1)
            eng.wait_ge(s, count[id(s)])

        UNITS = ([("in", w_in, c) for c in (0, 512, 1024, 1536, 2048, 2576)]
                 + [("ck", w_ck, c) for c in (0, 512)] + [("cv", w_cv, c) for c in (0, 512)]
                 + [("wo", w_out, c) for c in (0, 512)] + [("cq", w_cq, c) for c in (0, 512)]
                 + [("co", w_co, c) for c in (0, 512)] + [("pq", w_pq, c) for c in (0, 512, 1024, 1536)])
        unit_last = {}
        SMU = [("p", h, qt) for qt in range(PT_TILES) for h in range(AH)] + [("s", b, 0) for b in range(DEC_B)]
        XU = [("p", hp, qt) for qt in range(PT_TILES) for hp in range(2)] + [("s", b, 0) for b in range(DEC_B)]

        NORMS = {"mix": (0, NT, lambda t: X[:, t, :], lambda t, g: hT[:, 4 * g:4 * g + 4, t * P:(t + 1) * P]),
                 "mem": (1, 2, lambda t: mk_tm[:, t, :], lambda t, g: memT[:, 4 * g:4 * g + 4, t * P:(t + 1) * P]),
                 "cross": (2, NT, lambda t: X[:, t, :], lambda t, g: hT[:, 4 * g:4 * g + 4, t * P:(t + 1) * P]),
                 "ffn": (3, NT, lambda t: X[:, t, :], lambda t, g: hT[:, 4 * g:4 * g + 4, t * P:(t + 1) * P])}

        block = ctx.enter_context(nc.Block())

        @block.tensor
        def _(pe):
            def norm_transposes(name):
                for t in range(NORMS[name][1]):
                    pe.wait_ge(nrm[name][1], t + 1)
                    for g in range(2):
                        ps, done = open_group(pe, ("T" + name, t, g))
                        for j in range(4):
                            mm = pe.transpose(ps[:, j * P:(j + 1) * P], xn[:, t % 2, (4 * g + j) * P:(4 * g + j + 1) * P],
                                              ident)
                        mm.then_inc(done, 1)

            def project(u, srcT, name, t, rows=P):
                slot = u % WSLOTS
                pe.wait_ge(w_in_s[slot], 16 * (u // WSLOTS + 1))
                ps, done = open_group(pe, (name, u, t))
                for k in range(KT):
                    mm = pe.matmul(ps, srcT[:, k, t * P:(t + 1) * P], ring[:, slot, k, :],
                                   start=(k == 0), stop=(k == KT - 1))
                mm.then_inc(done, 1)
                unit_last[u] = (name, u, t)

            pe.wait_ge(c_in, 16 * 7)
            norm_transposes("mix")
            for u in range(6):
                for t in range(NT):
                    if u == 0:
                        for g in range(2):
                            drained(pe, "Tmix", t, g)
                    project(u, hT, "z", t)
            for i in range(2):
                ps, done = open_group(pe, ("gl", i))
                for k in range(KT):
                    mm = pe.matmul(ps[0:16, 0:320], wgl_sb[:, k, :], hT[:, k, 320 * i:320 * i + 320],
                                   start=(k == 0), stop=(k == KT - 1))
                mm.then_inc(done, 1)
            norm_transposes("mem")
            for u in range(6, 10):
                for t in range(2):
                    if u == 6:
                        for g in range(2):
                            drained(pe, "Tmem", t, g)
                    project(u, memT, "m", t)
            for t in range(NT):
                for which, tm in (("q", q_tm), ("k", k_tm)):
                    pe.wait_ge(hn["qk"][3], 2 * NT if which == "k" else NT + 1)
                    ps, done = open_group(pe, (which + "T", t))
                    for c in range(4):
                        mm = pe.transpose(ps[:, c * P:(c + 1) * P], tm[:, t, c * P:(c + 1) * P], ident)
                    mm.then_inc(done, 1)
            for t in range(2):
                pe.wait_ge(hn["mk"][3], 4)
                for g in range(2):
                    ps, done = open_group(pe, ("mkT", t, g))
                    for j in range(4):
                        mm = pe.transpose(ps[:, j * P:(j + 1) * P], mk_tm[:, t, (4 * g + j) * P:(4 * g + j + 1) * P],
                                          ident)
                    mm.then_inc(done, 1)

            def gla_gate(t):
                drained(pe, "gl", 0)
                drained(pe, "gl", 1)
                ps, done = open_group(pe, ("z2", t))
                pe.matmul(ps[:, 0:256], glT[:, t * P:(t + 1) * P], wg2_sb, start=True, stop=True).then_inc(done, 1)

            def gla_tile(t):
                tri = trip if t < PT_TILES else tris
                W = 130 if t < PT_TILES else 136
                ps, done = open_group(pe, ("gT", t))
                for c in range(4):
                    mm = pe.transpose(ps[:, c * P:(c + 1) * P], qk_tm[:, t, c * P:(c + 1) * P], ident)
                mm.then_inc(done, 1)
                pe.wait_ge(g_la, t + 1)
                ps, done = open_group(pe, ("cum", t))
                for p in range(2):
                    mm = pe.matmul(ps[:, 256 * p:256 * p + W], zz[:, t % 2, p * P:(p + 1) * P], tri,
                                   start=True, stop=True)
                mm.then_inc(done, 1)
                qh = hats[:, t % 2, 0:2, :]
                kh = hats[:, t % 2, 2:4, :]
                pe.wait_ge(g_hat, t + 1)
                ps, done = open_group(pe, ("kh", t))
                for p in range(2):
                    mm = pe.transpose(ps[:, p * P:(p + 1) * P], kh[:, p, :], ident)
                mm.then_inc(done, 1)
                for par in range(2):
                    o = 64 * par
                    ps, done = open_group(pe, ("A", t, par))
                    for p in range(2):
                        mm = pe.matmul(ps[:, p * P:(p + 1) * P], kh[o:o + 64, p, :], qh[o:o + 64, p, :],
                                       start=True, stop=True)
                    mm.then_inc(done, 1)
                drained(pe, "kh", t)
                if t < PT_TILES:
                    for c in range(2):
                        ps, done = open_group(pe, ("KV", t, c))
                        for h in range(GH):
                            o = 64 * (h % 2)
                            mm = pe.matmul(ps[o:o + 64, (h // 2) * P:(h // 2 + 1) * P],
                                           kh_tm[64 * c:64 * c + 64, t % 2, h * 64:h * 64 + 64],
                                           vg[64 * c:64 * c + 64, t, h * P:(h + 1) * P], start=True, stop=True)
                        mm.then_inc(done, 1)
                else:
                    pe.wait_ge(g_khm, 1)
                    for c in range(4):
                        ps, done = open_group(pe, ("KV", t, c))
                        for i in range(2):
                            for h in range(GH):
                                o = 64 * (h % 2)
                                mm = pe.matmul(ps[o:o + 64, i * 256 + (h // 2) * P:i * 256 + (h // 2 + 1) * P],
                                               khm[:, 2 * c + i, h * 64:h * 64 + 64],
                                               vg[:, t, h * P:(h + 1) * P], start=True, stop=True)
                        mm.then_inc(done, 1)
                drained(pe, "A", t, 0)
                drained(pe, "A", t, 1)
                pe.wait_ge(g_smid, 2 * t + 2 if t < PT_TILES else 2 * t + 1)
                for par in range(2):
                    o = 64 * par
                    ps, done = open_group(pe, ("go", t, par))
                    for p in range(2):
                        out = ps[:, p * P:(p + 1) * P]
                        h = 2 * p + par
                        pe.matmul(out, ATm[:, par, p, :], vg[:, t, h * P:(h + 1) * P], start=True, stop=False)
                        if t < PT_TILES:
                            for c in range(2):
                                mm = pe.matmul(out[64 * c:64 * c + 64, :], qh[o:o + 64, p, 64 * c:64 * c + 64],
                                               smid_p[o:o + 64, 2 * (t % 2) + c, p, :], start=False, stop=True)
                        else:
                            for b in range(DEC_B):
                                mm = pe.matmul(out, QZ[o:o + 64, p, b, :], smid_s[o:o + 64, b, p, :],
                                               start=False, stop=(b == DEC_B - 1))
                    mm.then_inc(done, 1)

            def gla_out(t):
                pe.wait_ge(hn["gla"][3], t + 1)
                ps, done = open_group(pe, ("ogT", t))
                for c in range(4):
                    mm = pe.transpose(ps[:, c * P:(c + 1) * P], og[:, t % 2, c * P:(c + 1) * P], ident)
                mm.then_inc(done, 1)

            gla_gate(0)
            for t in range(NT):
                if t + 1 < NT:
                    gla_gate(t + 1)
                gla_tile(t)
                if t:
                    gla_out(t - 1)
            gla_out(NT - 1)

            def att_scores(m):
                kind, a, qt = SMU[m]
                if kind == "p":
                    for t in range(qt + 1):
                        drained(pe, "qT", t)
                        drained(pe, "kT", t)
                    o, n = 64 * (a % 2), (qt + 1) * P
                    ps, done = open_group(pe, ("s", m))
                    pe.matmul(ps[:, 0:n], qT[o:o + 64, a // 2, qt * P:(qt + 1) * P], kT[o:o + 64, a // 2, 0:n],
                              start=True, stop=True).then_inc(done, 1)
                else:
                    pe.wait_ge(qb_s, 1)
                    pe.wait_ge(kc_s[a % 2], 16 * (a // 2 + 1))
                    for part in range(2):
                        ps, done = open_group(pe, ("s", m) if part == 0 else ("s2", m))
                        for p in range(4):
                            rhs = (kc_ring[:, a % 2, p, :] if part == 0
                                   else kT[:, p, SEQ + DEC_T * a:SEQ + DEC_T * (a + 1)])
                            out = ps[32 * p:32 * p + 32, 0:BANDK if part == 0 else DEC_T]
                            mm = pe.matmul(out, QB[:, p, a, :], rhs, start=True, stop=True,
                                           tile_position=(0, 32 * p))
                        mm.then_inc(done, 1)

            def att_probs(m):
                kind, a, qt = SMU[m]
                pe.wait_ge(sm["att"][2], m + 1)
                ps, done = open_group(pe, ("PT", m))
                for k in range(qt + 1 if kind == "p" else 4):
                    mm = pe.transpose(ps[:, k * P:(k + 1) * P], S_sb[:, m % 2, k * P:(k + 1) * P], ident)
                mm.then_inc(done, 1)
                if kind == "s":
                    ps, done = open_group(pe, ("PT2", m))
                    pe.transpose(ps[0:DEC_T, 0:P], S_sb[:, m % 2, BANDK:NEWK], ident).then_inc(done, 1)

            def att_values(m):
                kind, a, qt = SMU[m]
                drained(pe, "PT", m)
                if kind == "p":
                    o = 64 * (a % 2)
                    ps, done = open_group(pe, ("o", m))
                    for k in range(qt + 1):
                        mm = pe.matmul(ps[o:o + 64, 0:P], v_tm[:, k, a * 64:(a + 1) * 64], PT_sb[:, m % 2, k, :],
                                       start=(k == 0), stop=(k == qt))
                    mm.then_inc(done, 1)
                else:
                    drained(pe, "PT2", m)
                    pe.wait_ge(vc_s[a % 2], 16 * (a // 2 + 1))
                    pe.wait_ge(vn_s[a % 2], 16 * (a // 2 + 1))
                    ps, done = open_group(pe, ("o", m))
                    for h in range(AH):
                        o = 64 * (h % 2)
                        out = ps[o:o + 64, (h // 2) * DEC_T:(h // 2 + 1) * DEC_T]
                        for k in range(4):
                            pe.matmul(out, vc_ring[:, a % 2, k, h * 64:(h + 1) * 64],
                                      PT_sb[:, m % 2, k, DEC_T * h:DEC_T * (h + 1)], start=(k == 0), stop=False)
                        mm = pe.matmul(out, vn[0:DEC_T, a % 2, h * 64:(h + 1) * 64],
                                       PT_sb[0:DEC_T, m % 2, 4, DEC_T * h:DEC_T * (h + 1)], start=False, stop=True)
                    mm.then_inc(done, 1)

            for m in range(len(SMU) + 3):
                if m < len(SMU):
                    att_scores(m)
                if 2 <= m < len(SMU) + 2:
                    att_probs(m - 2)
                if m >= 3:
                    att_values(m - 3)
            for t in range(NT):
                for u in range(10, 12):
                    if u == 10:
                        drained(pe, "ogT", t)
                        for m, (kind, a, qt) in enumerate(SMU):
                            if (qt == t and kind == "p") or (kind == "s" and t == NT - 1):
                                drained(pe, "o", m)
                    project(u, mixT, "w", t)
            norm_transposes("cross")
            for u in range(12, 14):
                for t in range(NT):
                    if u == 12:
                        for g in range(2):
                            drained(pe, "Tcross", t, g)
                    project(u, hT, "cq", t)
            for t in range(NT):
                pe.wait_ge(hn["cq"][3], NT + t + 1)
                for g in range(2):
                    ps, done = open_group(pe, ("cqT", t, g))
                    for j in range(4):
                        mm = pe.transpose(ps[:, j * P:(j + 1) * P], cq_tm[:, t, (4 * g + j) * P:(4 * g + j + 1) * P],
                                          ident)
                    mm.then_inc(done, 1)

            def x_scores(m):
                kind, a, qt = XU[m]
                ps, done = open_group(pe, ("xs", m))
                if kind == "p":
                    drained(pe, "cqT", qt, a)
                    if m == 0:
                        for t in range(2):
                            for g in range(2):
                                drained(pe, "mkT", t, g)
                    for i in range(2):
                        for d in range(2):
                            mm = pe.matmul(ps[:, i * NMEM:(i + 1) * NMEM], cqT[:, 4 * a + 2 * i + d, qt * P:(qt + 1) * P],
                                           mkT[:, 4 * a + 2 * i + d, :], start=(d == 0), stop=(d == 1))
                else:
                    pe.wait_ge(qx_s, 1)
                    pe.wait_ge(mkc_s[a % 2], 16 * (a // 2 + 1))
                    for h in range(XH):
                        for d in range(2):
                            mm = pe.matmul(ps[32 * h:32 * h + 32, 0:NMEM], QX[:, 2 * h + d, a, :],
                                           mkc_ring[:, a % 2, 2 * h + d, :], start=(d == 0), stop=(d == 1),
                                           tile_position=(0, 32 * h))
                mm.then_inc(done, 1)

            def x_probs(m):
                kind, a, qt = XU[m]
                pe.wait_ge(sm["xat"][2], m + 1)
                ps, done = open_group(pe, ("xPT", m))
                for k in range(4 if kind == "p" else 2):
                    mm = pe.transpose(ps[:, k * P:(k + 1) * P], S_sb[:, m % 2, k * P:(k + 1) * P], ident)
                mm.then_inc(done, 1)

            def x_values(m):
                kind, a, qt = XU[m]
                drained(pe, "xPT", m)
                ps, done = open_group(pe, ("xo", m))
                if kind == "p":
                    if m == 0:
                        for u in range(8, 10):
                            for t in range(2):
                                drained(pe, "m", u, t)
                    for i in range(2):
                        for d in range(2):
                            c = (4 * a + 2 * i + d) * P
                            for k in range(2):
                                mm = pe.matmul(ps[:, (2 * i + d) * P:(2 * i + d + 1) * P], mv_tm[:, k, c:c + P],
                                               PT_sb[:, m % 2, 2 * i + k, :], start=(k == 0), stop=(k == 1))
                else:
                    pe.wait_ge(mvc_s[a % 2], 16 * (a // 2 + 1))
                    for j in range(2 * XH):
                        for k in range(2):
                            mm = pe.matmul(ps[:, j * DEC_T:(j + 1) * DEC_T], mvc_ring[:, a % 2, k, j * P:(j + 1) * P],
                                           PT_sb[:, m % 2, k, 32 * (j // 2):32 * (j // 2) + DEC_T],
                                           start=(k == 0), stop=(k == 1))
                mm.then_inc(done, 1)

            for m in range(len(XU) + 3):
                if m < len(XU):
                    x_scores(m)
                if 2 <= m < len(XU) + 2:
                    x_probs(m - 2)
                if m >= 3:
                    x_values(m - 3)
            for t in range(NT):
                for u in range(14, 16):
                    if u == 14:
                        for m, (kind, a, qt) in enumerate(XU):
                            if (qt == t and kind == "p") or (kind == "s" and t == NT - 1):
                                drained(pe, "xo", m)
                    project(u, hT, "co", t)
            norm_transposes("ffn")
            pe.wait_ge(keys_s, 32)
            for u in range(16, 20):
                slot = u % WSLOTS
                pe.wait_ge(w_in_s[slot], 16 * (u // WSLOTS + 1))
                for j in range(4):
                    for i in range(2):
                        if u == 16 and j == 0:
                            for t in range(NT if i else 3):
                                for g in range(2):
                                    drained(pe, "Tffn", t, g)
                        ps, done = open_group(pe, ("pq", u, j, i))
                        for k in range(KT):
                            mm = pe.matmul(ps[:, 0:320], ring[:, slot, k, j * P:(j + 1) * P],
                                           hT[:, k, 320 * i:320 * i + 320], start=(k == 0), stop=(k == KT - 1))
                        mm.then_inc(done, 1)
                        unit_last[u] = ("pq", u, j, i)
                for j in range(4):
                    for i in range(2):
                        drained(pe, "pq", u, j, i)
                for t in range(NT):
                    ps, done = open_group(pe, ("sc", u, t))
                    for j in range(4):
                        mm = pe.matmul(ps[:, j * NK:(j + 1) * NK], qry[:, 4 * (u % 2) + j, t * P:(t + 1) * P],
                                       keys_sb[:, j % 2, :], start=True, stop=True)
                    mm.then_inc(done, 1)
            for t in range(NT):
                pe.wait_ge(tk_done, t + 1)
                ps, done = open_group(pe, ("sel", t))
                pe.transpose(ps[:, 0:P], sg, ident)
                pe.transpose(ps[:, P:2 * P], jf[:, 0, :], ident)
                pe.transpose(ps[:, 2 * P:3 * P], jf[:, 1, :], ident).then_inc(done, 1)

            for b in range(8):
                pe.wait_ge(bank_free[b], uses[b])
            pe.sem_inc(wg_mm, CREDIT)
            with pe.Fori(0, NTG // 2) as i:
                for s in range(2):
                    for q in range(8):
                        n = i * 16 + (8 * s + q)
                        pe.wait_ge(a_oh_s, n + 1)
                        pe.wait_ge(b_oh_s, n + 1)
                        pe.wait_ge(wg_ev, i * 16 + (CREDIT if s == 0 else CREDIT + q + 1))
                        for j in range(4):
                            slot = (4 * q + j) % 16
                            mm = pe.matmul(PS[:, q, j * P:(j + 1) * P], A_oh[:, slot, :], B_oh[:, slot, :],
                                           start=True, stop=True)
                        mm.then_inc(wg_mm, 1)

            pe.wait_ge(wg_ev, CREDIT + NTG * 8)

            def z_tile(k, n, first):
                pe.wait_ge(u_sp, n + 1)
                if not first:
                    pe.wait_ge(z_ge, n - 1)
                for i in range(2):
                    for kk in range(KT):
                        for x, (a, b) in enumerate(((0, hhi), (0, hlo), (1, hhi))):
                            mm = pe.matmul(PS[:, 2 * (k % 2) + i, 0:320], u16[:, k % 4, a, kk, :],
                                           b[:, kk, 320 * i:320 * i + 320], start=(kk == 0 and x == 0),
                                           stop=(kk == KT - 1 and x == 2))
                mm.then_inc(z_mm, 1)

            def y_block(par, B, first):
                pe.wait_ge(a_sp, B * EB + EB)
                pe.wait_ge(v_sp, B * EB + EB)
                for g in range(2 * NT):
                    if not (first and g < 4):
                        pe.wait_ge(y_ev, B * (2 * NT) + (g - 3))
                    t, half = g // 2, g % 2
                    bank = 4 + (par * 2 * NT + g) % 4
                    for e in range(EB):
                        s = EB * par + e
                        for x, (a, b) in enumerate(((0, 0), (0, 1), (1, 0))):
                            mm = pe.matmul(PS[:, bank, :], a16[:, s, a, t * P:(t + 1) * P],
                                           v16[:, s, b, half * 512:(half + 1) * 512], start=(e == 0 and x == 0),
                                           stop=(e == EB - 1 and x == 2))
                    mm.then_inc(y_mm, 1)

            pe.wait_ge(h_split, NT)
            for k in range(EB):
                z_tile(k, k, k < 2)
            for k in range(EB):
                z_tile(k, EB + k, False)
            y_block(0, 0, True)
            with pe.Fori(0, NBLK // 2 - 1) as i:
                for s in range(2):
                    for k in range(EB):
                        z_tile(k, i * (2 * EB) + (EB * (2 + s) + k), False)
                    y_block((1 + s) % 2, i * 2 + (1 + s), False)
            y_block(1, NBLK - 1, False)

        @block.sync
        def _(sp):
            def unit(u):
                name, w, c = UNITS[u]
                if u >= WSLOTS:
                    full(sp, *unit_last[u - WSLOTS])
                sp.dma_start(ring[:, u % WSLOTS, :, :], w.rearrange("(k p) n -> p k n", p=P)[:, :, c:c + UNIT])\
                  .then_inc(w_in_s[u % WSLOTS], 16)

            sp.dma_start(X[:, 0, :], x_in[0:P, :]).then_inc(x_in_s, 16)
            sp.dma_start(X[:, 1:NT, :], x_in[P:T, :].rearrange("(t p) d -> p t d", p=P)).then_inc(x_in_s, 16)
            sp.dma_start(AR[:, CB:CB + NCONST], consts).then_inc(c_in, 16)
            sp.dma_start(gc_sb, gcols).then_inc(c_in, 16)
            sp.dma_start(gr_sb, grows).then_inc(c_in, 16)
            sp.dma_start(wg2_sb, wg2).then_inc(c_in, 16)
            sp.dma_start(bs_sb, bias_s).then_inc(c_in, 16)
            sp.dma_start(wgl_sb, w_gl.rearrange("(k p) n -> p k n", p=P)).then_inc(c_in, 16)
            for u in range(len(UNITS)):
                unit(u)
                if u == 6:
                    for b in range(2):
                        if b == 0:
                            full(sp, "gl", 1)
                        sp.dma_start(mk_tm[:, b, :], mem_in[b * P:(b + 1) * P, :]).then_inc(mem_in_s[b], 16)
            for s in range(2):
                sp.sem_inc(wst_s[s], CREDIT)
            with sp.Fori(0, NTG // 2) as i:
                for s in range(2):
                    sp.wait_ge(wg_ev, i * 16 + (CREDIT + 8 * (s + 1)))
                    sp.dma_start(w_dram[:, :, bass.ds(i * 2 + s, 1), :].rearrange("b p g n -> p b (g n)"),
                                 stage[:, s, :, :].rearrange("p (b e) t -> p b (e t)", e=EB))\
                      .then_inc(wst_s[s], 16)

            def load_w(par, B):
                sp.dma_start(W_sb[:, par, :, :, :], w_dram[bass.ds(B, 1)].rearrange("b p g n -> p (b g n)"))\
                  .then_inc(W_in[par], 16)

            def load_uv(k, n, first):
                if not first:
                    sp.wait_ge(u_sp, n - 3)
                sp.dma_start(ust[:, k % 4, :, :], u_t[bass.ds(n, 1)].rearrange("e p n -> p (e n)"))\
                  .then_inc(u_in[k % 4], 16)
                if not first:
                    sp.wait_ge(v_sp, n - 3)
                sp.dma_start(vst[:, k % 4, :], v_t[bass.ds(n, 1)].rearrange("e p n -> p (e n)"))\
                  .then_inc(v_in[k % 4], 16)

            full(sp, "sel", NT - 1)
            for s in range(2):
                sp.wait_ge(wst_s[s], CREDIT + 16 * (NTG // 2))
            load_w(0, 0)
            load_w(1, 1)
            for k in range(EB):
                load_uv(k, k, True)
            with sp.Fori(0, NBLK // 2 - 1) as i:
                for s in range(2):
                    for k in range(EB):
                        load_uv(k, i * (2 * EB) + (EB * (1 + s) + k), False)
                    sp.wait_ge(a_mul, i * (2 * EB) + EB * (1 + s))
                    load_w(s, i * 2 + (2 + s))
            for k in range(EB):
                load_uv(k, NK - EB + k, False)
            for t in range(NT):
                sp.wait_ge(y_ev, (NBLK - 1) * 2 * NT + 2 * (t + 1))
                sp.dma_start(y_out[t * P:(t + 1) * P, :], X[:, t, :]).then_inc(y_s, 16)
            sp.wait_ge(y_s, 16 * NT)
            sp.wait_ge(kout_s, 16)
            for stored in outs.values():
                sp.wait_ge(stored, 16)

        @block.gpsimd
        def _(pool):
            pool.wait_ge(hn["qk"][3], 2 * NT)
            pool.dma_start(k_out.rearrange("(t p) n -> p t n", p=P), k_tm).then_inc(kout_s, 16)
            for t in range(NT):
                drained(pool, "z", 2, t)
            pool.dma_start(v_out.rearrange("(t p) n -> p t n", p=P), v_tm).then_inc(outs["v"], 16)
            pool.wait_ge(hn["mk"][3], 4)
            pool.dma_start(mk_out.rearrange("(t p) n -> p t n", p=P), mk_tm).then_inc(outs["mk"], 16)
            for u in range(8, 10):
                for t in range(2):
                    drained(pool, "m", u, t)
            pool.dma_start(mv_out.rearrange("(t p) n -> p t n", p=P), mv_tm).then_inc(outs["mv"], 16)
            full(pool, "go", PT_TILES - 1, 1)
            pool.dma_start(st_s, state_in.rearrange("b g p v -> p b g v")).then_inc(st_s_s, 16)
            pool.wait_ge(g_st, 2 * PT_TILES)
            pool.dma_start(gp_out.rearrange("g p v -> p g v"), S_p).then_inc(outs["gp"], 16)
            full(pool, "go", NT - 1, 1)
            def load_bias(h, n):
                pool.dma_start(bias_ring[:, n % 2, :], bias_p[h]).then_inc(bias_s_[n % 2], 16)

            def load_keys(b):
                pool.dma_start(kc_ring[:, b % 2, :, :], kc_t[b]).then_inc(kc_s[b % 2], 16)

            def load_values(b):
                pool.dma_start(vc_ring[:, b % 2, :, :], v_c[b]).then_inc(vc_s[b % 2], 16)
                pool.dma_start(vn[0:DEC_T, b % 2, :], v_tm[DEC_T * b:DEC_T * (b + 1), NT - 1, :])\
                    .then_inc(vn_s[b % 2], 16)

            load_bias(0, 0)
            load_bias(1, 1)
            pool.wait_ge(g_st, 2 * PT_TILES + 4)
            pool.dma_start(gs_out.rearrange("b g p v -> p b g v"), st_s).then_inc(outs["gs"], 16)
            pool.wait_ge(outs["gs"], 16)
            pool.wait_ge(hn["gla"][3], NT)
            drained(pool, "ogT", NT - 1)
            full(pool, "ogT", NT - 1)
            for b in range(2):
                load_keys(b)
                load_values(b)
            for m in range(2, PT_TILES * AH):
                pool.wait_ge(sm["att"][0], m - 1)
                load_bias(SMU[m][1], m)
            for b in range(2, DEC_B + 1):
                if b < DEC_B:
                    full(pool, "s", PT_TILES * AH + b - 2)
                    load_keys(b)
                if b >= 3:
                    full(pool, "o", PT_TILES * AH + b - 3)
                    load_values(b - 1)

            def load_memkeys(b):
                pool.dma_start(mkc_ring[:, b % 2, :, :], mk_c[b]).then_inc(mkc_s[b % 2], 16)

            def load_memvalues(b):
                pool.dma_start(mvc_ring[:, b % 2, :, :], mv_c[b]).then_inc(mvc_s[b % 2], 16)

            for b in range(2):
                full(pool, "o", PT_TILES * AH + DEC_B - 2 + b)
                load_memkeys(b)
                load_memvalues(b)
            for b in range(2, DEC_B + 1):
                if b < DEC_B:
                    full(pool, "xs", 2 * PT_TILES + b - 2)
                    load_memkeys(b)
                if b >= 3:
                    full(pool, "xo", 2 * PT_TILES + b - 3)
                    load_memvalues(b - 1)
            drained(pool, "cqT", NT - 1, 1)
            for i in range(2):
                pool.dma_start(keys_sb[:, i, :], keys_t[i]).then_inc(keys_s, 16)
            drained(pool, "sel", NT - 1)
            for q in range(T // 4):
                if q >= 4:
                    pool.wait_ge(wg_mm, CREDIT + q - 3)
                for j in range(4):
                    ins = pool.tensor_scalar(B_oh[:, (4 * q + j) % 16, :], iota, selT[:, 2, 4 * q + j:4 * q + j + 1],
                                             None, ALU.is_equal)
                ins.then_inc(b_oh_s, 1)

        @block.scalar
        def _(act):
            def norm_stats(name, ready):
                _, n, src, _ = NORMS[name]
                for t in range(n):
                    ready(t)
                    link(act, act.activation(junk, src(t), ACT.Square, accum_out=nrm_ss[:, t % 2, :]), act_step)
                    if t >= 2:
                        act.wait_ge(nrm[name][1], t - 1)
                    link(act, act.activation(nrm_rs[:, t % 2, :], nrm_ss[:, t % 2, :], ACT.Ln, scale=1.0 / D,
                                             bias=eps_sb), act_step)
                    act.activation(nrm_rs[:, t % 2, :], nrm_rs[:, t % 2, :], ACT.Exp, scale=-0.5)\
                       .then_inc(nrm[name][0], 1)

            def head_norm(name, items, heads, width):
                sqs, sums, rstd, _ = hn[name]
                for m in range(len(items) + 1):
                    if m < len(items):
                        key, dst, slot_free = items[m]
                        ps, free = full(act, *key)
                        slot_free()
                        act.activation(dst, ps, ACT.Copy).then_inc(free, 1)
                        drained(act, *key)
                        if m >= 2:
                            act.wait_ge(sums, m - 1)
                        act.activation(sq[:, m % 2, :], dst, ACT.Square).then_inc(sqs, 1)
                    if m:
                        act.wait_ge(sums, m)
                        s = (m - 1) % 2
                        link(act, act.activation(hn_rs[:, s, 0:heads], hn_ss[:, s, 0:heads], ACT.Ln,
                                                 scale=1.0 / width, bias=eps_sb), act_step)
                        act.activation(hn_rs[:, s, 0:heads], hn_rs[:, s, 0:heads], ACT.Exp, scale=-0.5)\
                           .then_inc(rstd, 1)

            def copy_out(dst, *key):
                ps, free = full(act, *key)
                n = 1
                for s in dst.shape[1:]:
                    n *= s
                if len(dst.shape) == 3:
                    ps = ps[0:dst.shape[0], 0:n].rearrange("p (a b) -> p a b", a=dst.shape[1])
                else:
                    ps = ps[0:dst.shape[0], 0:n]
                act.activation(dst, ps, ACT.Copy).then_inc(free, 1)

            act.wait_ge(c_in, 16 * 7)
            norm_stats("mix", lambda t: act.wait_ge(x_in_s, 16 if t == 0 else 32) if t else act.wait_ge(x_in_s, 32))
            nothing = lambda: None
            head_norm("qk", [(("z", u, t), (q_tm, k_tm)[u][:, t, :], nothing) for u in range(2) for t in range(NT)], 8, 64)
            for u, dst in ((2, v_tm), (3, qk_tm), (4, vg)):
                for t in range(NT):
                    copy_out(dst[:, t, :], "z", u, t)
            for t in range(NT):
                ps, free = full(act, "z", 5, t)
                link(act, act.activation(rr[:, t, :], ps, ACT.Copy), act_step)
                if t >= 2:
                    act.wait_ge(r_silu, t - 1)
                act.activation(er[:, t % 2, :], ps, ACT.Exp, scale=-1.0).then_inc(free, 1)
            act.wait_ge(zero_s, 1)
            for i in range(2):
                copy_out(glT[0:16, 320 * i:320 * i + 320], "gl", i)
            norm_stats("mem", lambda t: act.wait_ge(mem_in_s[t], 16))
            def mk_free():
                act.wait_ge(nrm["mem"][1], 2)
            head_norm("mk", [(("m", u, t), mk_tm[:, t, (u - 6) * 512:(u - 5) * 512], mk_free)
                             for u in range(6, 8) for t in range(2)], 2, 256)
            for u in range(8, 10):
                for t in range(2):
                    copy_out(mv_tm[:, t, (u - 8) * 512:(u - 7) * 512], "m", u, t)
            for t in range(NT):
                for which, dst in (("q", qT), ("k", kT)):
                    copy_out(dst[:, :, t * P:(t + 1) * P], which + "T", t)
            for t in range(2):
                for g in range(2):
                    copy_out(mkT[:, 4 * g:4 * g + 4, t * P:(t + 1) * P], "mkT", t, g)
            act.wait_ge(outs["mk"], 16)
            def gate(t):
                ps, free = full(act, "z2", t)
                s = t % 2
                if t >= 2:
                    full(act, "cum", t - 2)
                act.activation(zz[:, s, :], ps[:, 0:256], ACT.Copy).then_inc(free, 1)
                drained(act, "z2", t)
                link(act, act.activation(ll[:, s, :], zz[:, s, :], ACT.Abs), act_step)
                link(act, act.activation(ll[:, s, :], ll[:, s, :], ACT.Exp, scale=-1.0), act_step)
                act.activation(ll[:, s, :], ll[:, s, :], ACT.Ln, bias=1.0).then_inc(g_l, 1)

            gate(0)
            for t in range(NT):
                W = 130 if t < PT_TILES else 136
                if t + 1 < NT:
                    gate(t + 1)
                ps, free = full(act, "cum", t)
                psv = ps.rearrange("p (a b) -> p a b", a=2)
                link(act, act.activation(eplus[:, t % 2, :, 0:W], psv[:, :, 0:W], ACT.Exp), act_step)
                if t:
                    act.wait_ge(g_hat, t)
                act.activation(eminus, psv[:, :, 0:P], ACT.Exp, scale=-1.0).then_inc(free, 1)
                copy_out(kh_tm[:, t % 2, :], "kh", t)
                sqs, sums, rstd, done = hn["gla"]
                if t >= 2:
                    full(act, "ogT", t - 2)
                if t == 0:
                    act.wait_ge(r_silu, NT)
                for par in range(2):
                    ps, free = full(act, "go", t, par)
                    act.activation(og[:, t % 2, :].rearrange("p (g par d) -> p g par d", g=2, par=2)[:, :, par, :],
                                   ps[:, 0:256].rearrange("p (g d) -> p g d", g=2), ACT.Copy).then_inc(free, 1)
                for par in range(2):
                    drained(act, "go", t, par)
                act.activation(sq[:, t % 2, :], og[:, t % 2, :], ACT.Square).then_inc(sqs, 1)
                act.wait_ge(sums, t + 1)
                link(act, act.activation(hn_rs[:, t % 2, 0:4], hn_ss[:, t % 2, 0:4], ACT.Ln, scale=1.0 / GV,
                                         bias=eps_sb), act_step)
                act.activation(hn_rs[:, t % 2, 0:4], hn_rs[:, t % 2, 0:4], ACT.Exp, scale=-0.5).then_inc(rstd, 1)
                if t == 0:
                    act.wait_ge(kout_s, 16)
                if t:
                    copy_out(mixT[:, 4:8, (t - 1) * P:t * P], "ogT", t - 1)
            copy_out(mixT[:, 4:8, (NT - 1) * P:NT * P], "ogT", NT - 1)

            def softmax_exp(m):
                kind, a, qt = SMU[m]
                n = (qt + 1) * P if kind == "p" else NEWK
                act.wait_ge(sm["att"][0], m + 1)
                act.activation(S_sb[:, m % 2, 0:n], S_sb[:, m % 2, 0:n], ACT.Exp, bias=sm_nm[:, m % 2, 0:1],
                               accum_out=sm_sum[:, m % 2, 0:1]).then_inc(sm["att"][1], 1)

            def probs_out(m):
                kind, a, qt = SMU[m]
                if m >= 2:
                    full(act, "o", m - 2)
                copy_out(PT_sb[:, m % 2, 0:(qt + 1 if kind == "p" else 4), :], "PT", m)
                if kind == "s":
                    copy_out(PT_sb[0:DEC_T, m % 2, 4, :], "PT2", m)

            for m in range(len(SMU) + 2):
                if m < len(SMU):
                    softmax_exp(m)
                if m >= 2:
                    probs_out(m - 2)
            norm_stats("cross", lambda t: act.wait_ge(x_mix, 2 * t + 2))
            def cq_free():
                full(act, "w", 11, NT - 1)
            head_norm("cq", [(("cq", u, t), cq_tm[:, t, (u - 12) * 512:(u - 11) * 512], cq_free)
                             for u in range(12, 14) for t in range(NT)], 2, 256)
            for t in range(NT):
                for g in range(2):
                    copy_out(cqT[:, 4 * g:4 * g + 4, t * P:(t + 1) * P], "cqT", t, g)

            def x_exp(m):
                kind, a, qt = XU[m]
                ps, free = full(act, "xs", m)
                act.wait_ge(sm["xat"][0], m + 1)
                if m >= 2:
                    full(act, "xPT", m - 2)
                for i in range(2 if kind == "p" else 1):
                    ins = act.activation(S_sb[:, m % 2, i * NMEM:(i + 1) * NMEM], ps[:, i * NMEM:(i + 1) * NMEM],
                                         ACT.Exp, bias=sm_nm[:, m % 2, i:i + 1], scale=1.0 / 16,
                                         accum_out=sm_sum[:, m % 2, i:i + 1])
                    if kind == "p" and i == 0:
                        link(act, ins, act_step)
                ins.then_inc(free, 1)

            for m in range(len(XU) + 2):
                if m < len(XU):
                    x_exp(m)
                if m >= 2:
                    if m >= 4:
                        full(act, "xo", m - 4)
                    copy_out(PT_sb[:, m % 2, 0:(4 if XU[m - 2][0] == "p" else 2), :], "xPT", m - 2)
            norm_stats("ffn", lambda t: act.wait_ge(x_cross, 2 * t + 2))
            for u in range(16, 20):
                for j in range(4):
                    for i in range(2):
                        if u >= 18 and j == 0 and i == 0:
                            full(act, "sc", u - 2, NT - 1)
                        copy_out(qry[:, 4 * (u % 2) + j, 320 * i:320 * i + 320], "pq", u, j, i)
            for t in range(NT):
                act.wait_ge(tk_exp_in, t + 1)
                act.activation(sg, sg, ACT.Exp).then_inc(tk_exp, 1)
            act.sem_inc(wg_ev, CREDIT)
            with act.Fori(0, NTG // 2) as i:
                for s in range(2):
                    act.wait_ge(wst_s[s], i * 16 + CREDIT)
                    for q in range(8):
                        act.wait_ge(wg_mm, i * 16 + (CREDIT + 8 * s + q + 1))
                        act.activation(stage[:, s, :, 4 * q:4 * q + 4].rearrange("p e t -> p t e"),
                                       PS[:, q, :].rearrange("p (t e) -> p t e", t=4), ACT.Copy).then_inc(wg_ev, 1)

            def u_high(k, n, i_loads, first):
                act.wait_ge(u_in[k], i_loads)
                if not first:
                    act.wait_ge(z_mm, n - 3)
                act.activation(u16[:, k, 0, :, :], ust[:, k, :, :], ACT.Copy, scale=USCALE).then_inc(u_hi, 1)

            def v_high(k, par, B, i_loads, first):
                act.wait_ge(v_in[k], i_loads)
                if not first:
                    act.wait_ge(y_mm, (B - 1) * (2 * NT))
                act.activation(v16[:, EB * par + k, 0, :], vst[:, k, :], ACT.Copy).then_inc(v_hi, 1)

            def gelu(k, par, n, first):
                act.wait_ge(z_mm, n + 1)
                if not first:
                    act.wait_ge(a_mul, n - 1)
                act.activation(gel[:, k % 2, :].rearrange("p (i t) -> p i t", i=2),
                               PS[:, 2 * (k % 2):2 * (k % 2) + 2, 0:320], ACT.Gelu, scale=1.0 / USCALE)\
                   .then_inc(z_ge, 1)
                act.wait_ge(a_mul, n + 1)
                act.activation(a16[:, EB * par + k, 0, :], a32[:, k % 2, :], ACT.Copy).then_inc(a_hi, 1)

            def z_steps(par, B, i_loads, first):
                for k in range(EB):
                    v_high(k, par, B, i_loads, first)
                    gelu(k, par, B * EB + k, first and k < 2 and par == 0)

            for k in range(EB):
                u_high(k, k, 16, True)
            z_steps(0, 0, 16, True)
            for k in range(EB):
                u_high(k, EB + k, 32, False)
            z_steps(1, 1, 32, True)
            with act.Fori(0, NBLK // 2 - 1) as i:
                for s in range(2):
                    B = i * 2 + (2 + s)
                    for k in range(EB):
                        u_high(k, i * (2 * EB) + (EB * (2 + s) + k), i * 32 + 16 * (3 + s), False)
                    z_steps(s, B, i * 32 + 16 * (3 + s), False)

        @block.vector
        def _(dve):
            link(dve, dve.memset(eps_sb, EPS), dve_step)
            dve.sem_inc(c_in, 16)

            def norm_scale(name):
                gi, n, src, dst = NORMS[name]
                for t in range(n + 1):
                    if t < n:
                        dve.wait_ge(nrm[name][0], t + 1)
                        dve.tensor_scalar(xn[:, t % 2, :], src(t), nrm_rs[:, t % 2, :], None, ALU.mult)\
                           .then_inc(nrm[name][1], 1)
                    if t:
                        for g in range(2):
                            ps, free = full(dve, "T" + name, t - 1, g)
                            ins = dve.tensor_tensor(dst(t - 1, g), ps.rearrange("p (a b) -> p a b", a=4),
                                                    gc_sb[:, gi, 4 * g:4 * g + 4].unsqueeze(2).to_broadcast([P, 4, P]),
                                                    ALU.mult)
                            ins.then_inc(free, 1)

            def head_norm(name, items, heads, width):
                sqs, sums, rstd, done = hn[name]
                for m in range(len(items) + 1):
                    if m < len(items):
                        dve.wait_ge(sqs, m + 1)
                        dve.tensor_reduce(hn_ss[:, m % 2, 0:heads],
                                          sq[:, m % 2, :].rearrange("p (h d) -> p h d", h=heads), AX.X, ALU.add)\
                           .then_inc(sums, 1)
                    if m:
                        dst, gain = items[m - 1]
                        v = dst.rearrange("p (h d) -> p h d", h=heads)
                        dve.wait_ge(rstd, m)
                        rs = hn_rs[:, (m - 1) % 2, 0:heads].unsqueeze(2).to_broadcast([P, heads, width])
                        link(dve, dve.tensor_tensor(v, v, rs, ALU.mult), dve_step)
                        dve.tensor_tensor(v, v, gain.unsqueeze(1).to_broadcast([P, heads, width]), ALU.mult)\
                           .then_inc(done, 1)

            norm_scale("mix")
            head_norm("qk", [((q_tm, k_tm)[u][:, t, :], (gq, gk)[u]) for u in range(2) for t in range(NT)], 8, 64)
            for t in range(NT):
                drained(dve, "z", 5, t)
                s = t % 2
                link(dve, dve.tensor_scalar(er[:, s, :], er[:, s, :], 1.0, None, ALU.add), dve_step)
                link(dve, dve.reciprocal(er[:, s, :], er[:, s, :]), dve_step)
                dve.tensor_tensor(rr[:, t, :], rr[:, t, :], er[:, s, :], ALU.mult).then_inc(r_silu, 1)
            full(dve, "gl", 1)
            dve.memset(glT, 1.0).then_inc(zero_s, 1)
            norm_scale("mem")
            head_norm("mk", [(mk_tm[:, t, (u - 6) * 512:(u - 5) * 512], gck) for u in range(6, 8) for t in range(2)],
                      2, 256)
            dve.wait_ge(outs["mk"], 16)
            full(dve, "mkT", 1, 1)
            link(dve, dve.memset(QZ, 0.0), dve_step)
            link(dve, dve.memset(S_p, 0.0), dve_step)

            def gate(t):
                dve.wait_ge(g_l, t + 1)
                s = t % 2
                dve.scalar_tensor_tensor(out=zz[:, s, :], in0=zz[:, s, :], scalar=0.0, in1=ll[:, s, :],
                                         op0=ALU.min, op1=ALU.subtract).then_inc(g_la, 1)

            def scaled(dst, src, t, col, inc):
                for p in range(2):
                    ins = dve.tensor_scalar(dst[:, p, :], src[:, p, :], eplus[:, t % 2, p, col:col + 1], None, ALU.mult)
                    if p == 0:
                        ins.then_inc(dve_step, 1)
                        count[id(dve_step)] += 1
                ins.then_inc(inc, 1)

            gate(0)
            for t in range(NT):
                s = t % 2
                if t + 1 < NT:
                    gate(t + 1)
                ps, free = full(dve, "gT", t)
                psv = ps.rearrange("p (a b) -> p a b", a=4)
                drained(dve, "cum", t)
                link(dve, dve.scalar_tensor_tensor(out=hats[:, s, 0:2, :], in0=psv[:, 0:2, :], scalar=GK ** -0.5,
                                                   in1=eplus[:, s, :, 0:P], op0=ALU.mult, op1=ALU.mult), dve_step)
                dve.tensor_tensor(hats[:, s, 2:4, :], psv[:, 2:4, :], eminus, ALU.mult).then_inc(free, 1)
                drained(dve, "gT", t)
                if t == NT - 1:
                    for b in range(DEC_B):
                        link(dve, dve.tensor_copy(QZ[:, :, b, DEC_T * b:DEC_T * (b + 1)],
                                                  hats[:, s, 0:2, DEC_T * b:DEC_T * (b + 1)]), dve_step)
                dve.sem_inc(g_hat, 1)
                mask = maskp if t < PT_TILES else masks
                if t:
                    full(dve, "go", t - 1, 1)
                for par in range(2):
                    ps, free = full(dve, "A", t, par)
                    dve.tensor_tensor(ATm[:, par], ps[:, 0:256].rearrange("p (h t) -> p h t", h=2),
                                      mask.unsqueeze(1).to_broadcast([P, 2, P]), ALU.mult).then_inc(free, 1)
                if t < PT_TILES:
                    for c in range(2):
                        scaled(smid_p[:, 2 * s + c], S_p, t, P + c, g_smid)
                        dve.wait_ge(g_smid, 2 * t + c + 1)
                        ps, free = full(dve, "KV", t, c)
                        dve.tensor_tensor(S_p, smid_p[:, 2 * s + c], ps[:, 0:256].rearrange("p (a b) -> p a b", a=2),
                                          ALU.add).then_inc(free, 1)
                        drained(dve, "KV", t, c)
                        scaled(S_p, S_p, t, 64 * c + 63, g_st)
                        dve.wait_ge(g_st, 2 * t + c + 1)
                else:
                    drained(dve, "kh", t)
                    dve.tensor_tensor(khm, kh_tm[:, s, :].unsqueeze(1).to_broadcast([P, DEC_B, 256]),
                                      bmask.unsqueeze(2).to_broadcast([P, DEC_B, 256]), ALU.mult).then_inc(g_khm, 1)
                    dve.wait_ge(st_s_s, 16)
                    for p in range(2):
                        ins = dve.tensor_tensor(smid_s[:, :, p, :], st_s[:, :, p, :],
                                                eplus[:, s, p, P:P + 8].unsqueeze(2).to_broadcast([P, DEC_B, P]),
                                                ALU.mult)
                        if p == 0:
                            link(dve, ins, dve_step)
                    ins.then_inc(g_smid, 1)
                    dve.wait_ge(g_smid, 2 * t + 1)
                    for c in range(4):
                        ps, free = full(dve, "KV", t, c)
                        dve.tensor_tensor(st_s[:, 2 * c:2 * c + 2, :, :].rearrange("p b g v -> p (b g v)"),
                                          smid_s[:, 2 * c:2 * c + 2, :, :].rearrange("p b g v -> p (b g v)"),
                                          ps, ALU.add).then_inc(free, 1)
                        drained(dve, "KV", t, c)
                        for i in range(2):
                            for p in range(2):
                                b = 2 * c + i
                                ins = dve.tensor_scalar(st_s[:, b, p, :], st_s[:, b, p, :],
                                                        eplus[:, s, p, DEC_T * b + 15:DEC_T * b + 16], None, ALU.mult)
                                if i + p < 2:
                                    link(dve, ins, dve_step)
                        ins.then_inc(g_st, 1)
                sqs, sums, rstd, done = hn["gla"]
                dve.wait_ge(sqs, t + 1)
                dve.tensor_reduce(hn_ss[:, s, 0:4], sq[:, s, :].rearrange("p (h d) -> p h d", h=GH), AX.X, ALU.add)\
                   .then_inc(sums, 1)
                v = og[:, s, :].rearrange("p (h d) -> p h d", h=GH)
                dve.wait_ge(rstd, t + 1)
                link(dve, dve.tensor_tensor(v, v, hn_rs[:, s, 0:4].unsqueeze(2).to_broadcast([P, GH, GV]), ALU.mult),
                     dve_step)
                link(dve, dve.tensor_tensor(v, v, ggla.unsqueeze(1).to_broadcast([P, GH, GV]), ALU.mult), dve_step)
                dve.tensor_tensor(og[:, s, :], og[:, s, :], rr[:, t, :], ALU.mult).then_inc(done, 1)

            full(dve, "ogT", NT - 1)
            for t in range(NT):
                drained(dve, "qT", t)
            link(dve, dve.memset(QB, 0.0), dve_step)
            for o in (0, 64):
                ins = dve.tensor_copy(QB[o:o + 64, :, :, o // 4:o // 4 + DEC_T],
                                      qT[o:o + 64, :, SEQ:T].rearrange("p c (b t) -> p c b t", b=DEC_B))
                if o == 0:
                    link(dve, ins, dve_step)
            ins.then_inc(qb_s, 1)

            def att_max(m):
                kind, a, qt = SMU[m]
                s = m % 2
                if m >= 2:
                    full(dve, "PT" if SMU[m - 2][0] == "p" else "PT2", m - 2)
                ps, free = full(dve, "s", m)
                if kind == "p":
                    n = (qt + 1) * P
                    dve.wait_ge(bias_s_[s], 16 * (m // 2 + 1))
                    dve.scalar_tensor_tensor(out=S_sb[:, s, 0:n], in0=ps[:, 0:n], scalar=AD ** -0.5,
                                             in1=bias_ring[:, s, 512 - n:512], op0=ALU.mult, op1=ALU.add)\
                       .then_inc(free, 1)
                    drained(dve, "s", m)
                else:
                    n = NEWK
                    dve.scalar_tensor_tensor(out=S_sb[:, s, 0:BANDK], in0=ps, scalar=AD ** -0.5,
                                             in1=bs_sb[:, 0:BANDK], op0=ALU.mult, op1=ALU.add).then_inc(free, 1)
                    ps, free = full(dve, "s2", m)
                    dve.scalar_tensor_tensor(out=S_sb[:, s, BANDK:NEWK], in0=ps[:, 0:DEC_T], scalar=AD ** -0.5,
                                             in1=bs_sb[:, BANDK:NEWK], op0=ALU.mult, op1=ALU.add).then_inc(free, 1)
                    drained(dve, "s", m)
                    drained(dve, "s2", m)
                dve.tensor_reduce(sm_nm[:, s, 0:1], S_sb[:, s, 0:n], AX.X, ALU.max, negate=True)\
                   .then_inc(sm["att"][0], 1)

            def att_norm(m):
                kind, a, qt = SMU[m]
                n = (qt + 1) * P if kind == "p" else NEWK
                s = m % 2
                dve.wait_ge(sm["att"][1], m + 1)
                link(dve, dve.reciprocal(sm_inv[:, s, 0:1], sm_sum[:, s, 0:1]), dve_step)
                dve.tensor_scalar(S_sb[:, s, 0:n], S_sb[:, s, 0:n], sm_inv[:, s, 0:1], None, ALU.mult)\
                   .then_inc(sm["att"][2], 1)

            def att_out(m):
                kind, a, qt = SMU[m]
                ps, free = full(dve, "o", m)
                if kind == "p":
                    o = 64 * (a % 2)
                    dve.tensor_copy(mixT[o:o + 64, a // 2, qt * P:(qt + 1) * P], ps[o:o + 64, 0:P]).then_inc(free, 1)
                else:
                    dve.tensor_copy(mixT[:, 0:4, SEQ + DEC_T * a:SEQ + DEC_T * (a + 1)],
                                    ps[:, 0:64].rearrange("p (c t) -> p c t", c=4)).then_inc(free, 1)

            for m in range(len(SMU) + 3):
                if m < len(SMU):
                    att_max(m)
                if 1 <= m < len(SMU) + 1:
                    att_norm(m - 1)
                if m >= 3:
                    att_out(m - 3)

            def residual(name, u0, ready):
                for t in range(NT):
                    for u in (u0, u0 + 1):
                        ps, free = full(dve, name, u, t)
                        c = (u - u0) * 512
                        ins = dve.tensor_tensor(X[:, t, c:c + 512], X[:, t, c:c + 512], ps, ALU.add)
                        ins.then_inc(free, 1)
                        drained(dve, name, u, t)
                        dve.sem_inc(ready, 1)

            residual("w", 10, x_mix)
            norm_scale("cross")
            head_norm("cq", [(cq_tm[:, t, (u - 12) * 512:(u - 11) * 512], gcq) for u in range(12, 14) for t in range(NT)],
                      2, 256)
            for g in range(2):
                drained(dve, "cqT", NT - 1, g)
            link(dve, dve.memset(QX, 0.0), dve_step)
            dve.tensor_copy(QX[:, :, :, 0:DEC_T], cqT[:, :, SEQ:T].rearrange("p c (b t) -> p c b t", b=DEC_B))\
               .then_inc(qx_s, 1)

            def x_max(m):
                kind, a, qt = XU[m]
                ps, _ = full(dve, "xs", m)
                h = 2 if kind == "p" else 1
                s = m % 2
                link(dve, dve.tensor_reduce(sm_max[:, s, 0:h], ps[:, 0:h * NMEM].rearrange("p (h k) -> p h k", h=h),
                                            AX.X, ALU.max), dve_step)
                dve.tensor_scalar(sm_nm[:, s, 0:h], sm_max[:, s, 0:h], -1.0 / 16, None, ALU.mult)\
                   .then_inc(sm["xat"][0], 1)

            def x_norm(m):
                kind, a, qt = XU[m]
                h = 2 if kind == "p" else 1
                s = m % 2
                drained(dve, "xs", m)
                link(dve, dve.reciprocal(sm_inv[:, s, 0:h], sm_sum[:, s, 0:h]), dve_step)
                v = S_sb[:, s, 0:h * NMEM].rearrange("p (h k) -> p h k", h=h)
                dve.tensor_tensor(v, v, sm_inv[:, s, 0:h].unsqueeze(2).to_broadcast([P, h, NMEM]), ALU.mult)\
                   .then_inc(sm["xat"][2], 1)

            def x_out(m):
                kind, a, qt = XU[m]
                ps, free = full(dve, "xo", m)
                if kind == "p":
                    dve.tensor_copy(hT[:, 4 * a:4 * a + 4, qt * P:(qt + 1) * P], ps.rearrange("p (c t) -> p c t", c=4))\
                       .then_inc(free, 1)
                else:
                    dve.tensor_copy(hT[:, :, SEQ + DEC_T * a:SEQ + DEC_T * (a + 1)],
                                    ps[:, 0:P].rearrange("p (c t) -> p c t", c=8)).then_inc(free, 1)

            for m in range(len(XU) + 3):
                if m < len(XU):
                    x_max(m)
                if 1 <= m < len(XU) + 1:
                    x_norm(m - 1)
                if m >= 3:
                    x_out(m - 3)
            residual("co", 14, x_cross)
            norm_scale("ffn")
            for t in range(NT):
                c = slice(t * P, (t + 1) * P)
                for g in range(2):
                    drained(dve, "Tffn", t, g)
                link(dve, dve.tensor_copy(hhi[:, :, c], hT[:, :, c]), dve_step)
                dve.tensor_tensor(hlo[:, :, c], hT[:, :, c], hhi[:, :, c], ALU.subtract).then_inc(h_split, 1)

            def top16(vals, idx, src, n):
                link(dve, dve.max(vals[:, 0:8], src), dve_step)
                dve.max_index(idx[:, 0:8], vals[:, 0:8], src)
                link(dve, dve.match_replace(srep[:, 0:n], vals[:, 0:8], src, NEG), dve_step)
                link(dve, dve.max(vals[:, 8:16], srep[:, 0:n]), dve_step)
                link(dve, dve.max_index(idx[:, 8:16], vals[:, 8:16], srep[:, 0:n]), dve_step)

            for u in range(16, 20):
                for t in range(NT):
                    ps, free = full(dve, "sc", u, t)
                    dve.tensor_copy(s_ring[:, u % 2, t, :], ps).then_inc(free, 1)
                    drained(dve, "sc", u, t)
                for t in range(NT):
                    for j in range(4):
                        jj = 4 * (u - 16) + j
                        top16(top_v[:, t, jj, :], top_i[:, t, jj * TOPK:(jj + 1) * TOPK],
                              s_ring[:, u % 2, t, j * NK:(j + 1) * NK], NK)
            for t in range(NT):
                v = top_v[:, t].rearrange("p (h two) k -> p h two k", two=2)
                for h in range(PH):
                    link(dve, dve.tensor_tensor(cand[:, h, :].rearrange("p (a b) -> p a b", a=TOPK),
                                                v[:, h, 0, :].unsqueeze(2).to_broadcast([P, TOPK, TOPK]),
                                                v[:, h, 1, :].unsqueeze(1).to_broadcast([P, TOPK, TOPK]), ALU.add),
                         dve_step)
                for h in range(PH):
                    top16(ts[:, h, :], tp[:, h * TOPK:(h + 1) * TOPK], cand[:, h, :], 256)
                if t:
                    full(dve, "sel", t - 1)
                link(dve, dve.tensor_tensor(sg.rearrange("p (h k) -> p h k", h=PH), ts,
                                            ts[:, :, 0:1].to_broadcast([P, PH, TOPK]), ALU.subtract), dve_step)
                dve.sem_inc(tk_exp_in, 1)
                link(dve, dve.tensor_scalar(ji[:, 0, :], tp, 4, None, ALU.logical_shift_right), dve_step)
                link(dve, dve.tensor_scalar(ji[:, 1, :], tp, 15, None, ALU.bitwise_and), dve_step)
                link(dve, dve.tensor_copy(jf, ji), dve_step)
                for half in range(2):
                    link(dve, dve.tensor_copy(topif[:, half], top_i[:, t, :].rearrange(
                        "p (h two k) -> p h two k", two=2, k=TOPK)[:, :, half, :]), dve_step)
                for half in range(2):
                    link(dve, dve.tensor_tensor(eq, jf[:, half, :].unsqueeze(2).to_broadcast([P, P, TOPK]),
                                                iota[:, 0:TOPK].unsqueeze(1).to_broadcast([P, P, TOPK]), ALU.is_equal),
                         dve_step)
                    e4 = eq.rearrange("p (h k) j -> p h k j", h=PH)
                    link(dve, dve.tensor_tensor(e4, e4, topif[:, half].unsqueeze(2).to_broadcast([P, PH, TOPK, TOPK]),
                                                ALU.mult), dve_step)
                    link(dve, dve.tensor_reduce(jf[:, half, :], eq, AX.X, ALU.add), dve_step)
                dve.wait_ge(tk_exp, t + 1)
                g = sg.rearrange("p (h k) -> p h k", h=PH)
                link(dve, dve.tensor_reduce(gsum, g, AX.X, ALU.add), dve_step)
                link(dve, dve.reciprocal(gsum, gsum), dve_step)
                dve.tensor_tensor(g, g, gsum.unsqueeze(2).to_broadcast([P, PH, TOPK]), ALU.mult).then_inc(tk_done, 1)
                ps, free = full(dve, "sel", t)
                dve.tensor_copy(selT[:, :, t * P:(t + 1) * P], ps[:, 0:3 * P].rearrange("p (a b) -> p a b", a=3))\
                   .then_inc(free, 1)
            drained(dve, "sel", NT - 1)
            with dve.Fori(0, NTG // 2) as i:
                for s in range(2):
                    for q in range(8):
                        dve.wait_ge(wg_mm, i * 16 + (CREDIT + max(8 * s + q - 3, 0)))
                        for j in range(4):
                            tok = i * (2 * TG) + (TG * s + 4 * q + j)
                            ins = dve.tensor_scalar(A_oh[:, (4 * q + j) % 16, :], iota, selT[:, 1, bass.ds(tok, 1)],
                                                    selT[:, 0, bass.ds(tok, 1)], ALU.is_equal, ALU.mult)
                        ins.then_inc(a_oh_s, 1)

            def u_low(k, n):
                dve.wait_ge(u_hi, n + 1)
                dve.scalar_tensor_tensor(out=u16[:, k, 1, :, :], in0=ust[:, k, :, :], scalar=USCALE,
                                         in1=u16[:, k, 0, :, :], op0=ALU.mult, op1=ALU.subtract).then_inc(u_sp, 1)

            def v_low(k, par, n):
                dve.wait_ge(v_hi, n + 1)
                dve.tensor_tensor(v16[:, EB * par + k, 1, :], vst[:, k, :], v16[:, EB * par + k, 0, :],
                                  ALU.subtract).then_inc(v_sp, 1)

            def gated(k, par, n, loads):
                dve.wait_ge(z_ge, n + 1)
                if k == 0:
                    dve.wait_ge(W_in[par], loads)
                dve.tensor_tensor(a32[:, k % 2, :].rearrange("p (g t) -> p g t", g=NTG),
                                  gel[:, k % 2, :].rearrange("p (g t) -> p g t", g=NTG), W_sb[:, par, :, k, :],
                                  ALU.mult).then_inc(a_mul, 1)
                dve.wait_ge(a_hi, n + 1)
                dve.tensor_tensor(a16[:, EB * par + k, 1, :], a32[:, k % 2, :], a16[:, EB * par + k, 0, :],
                                  ALU.subtract).then_inc(a_sp, 1)

            def z_steps(par, n0, loads):
                for k in range(EB):
                    v_low(k, par, n0 + k)
                    gated(k, par, n0 + k, loads)

            def y_add(par, B, g):
                t, half = g // 2, g % 2
                dve.wait_ge(y_mm, B * (2 * NT) + (g + 1))
                c = slice(half * 512, half * 512 + 512)
                dve.tensor_tensor(X[:, t, c], X[:, t, c], PS[:, 4 + (par * 2 * NT + g) % 4, :], ALU.add)\
                   .then_inc(y_ev, 1)

            for k in range(EB):
                u_low(k, k)
            z_steps(0, 0, 16)
            for k in range(EB):
                u_low(k, EB + k)
            z_steps(1, EB, 16)
            with dve.Fori(0, NBLK // 2 - 1) as i:
                for s in range(2):
                    for g in range(2 * NT):
                        if g % 2 == 0 and g < 2 * EB:
                            u_low(g // 2, i * (2 * EB) + (EB * (2 + s) + g // 2))
                        y_add(s, i * 2 + s, g)
                    z_steps(s, i * (2 * EB) + EB * (2 + s), i * 16 + 32)
            for B in (NBLK - 2, NBLK - 1):
                for g in range(2 * NT):
                    y_add(B % 2, B, g)


def kernel(**inputs):
    import numpy as np
    import concourse.bacc as _bacc
    from concourse import mybir as _mybir
    from concourse.bass_utils import run_bass_kernel_spmd as _run

    a = {k: np.asarray(v) for k, v in inputs.items()}
    f = np.float32
    x = np.concatenate([a["x_prompt"][0], a["x_sample"].reshape(128, 1024)], axis=0)
    w_in = a["w_in"][0]
    q, m = np.arange(128)[:, None], np.arange(512)[None, :]
    rb = a["rel_bias"][0]
    bias_p = rb[:, np.clip(q + 384 - m, -128, 128) + 128]
    blocked = np.broadcast_to((q < 64) & (m >= 448), bias_p.shape)
    bias_p = np.where(blocked, f(-1e30), bias_p).astype(f)
    i, j = np.arange(16)[:, None], np.arange(528)[None, :]
    bias_s = rb[:, np.clip(512 + i - j, -128, 128) + 128].reshape(128, 528)
    kc = a["cache_att_k"][0][:, 64:].reshape(8, 512, 4, 128).transpose(0, 3, 2, 1)
    vc = a["cache_att_v"][0][:, 64:].reshape(8, 4, 128, 512).transpose(0, 2, 1, 3)
    mkc = a["cache_mem_k"][0].reshape(8, 256, 8, 128).transpose(0, 3, 2, 1)
    mvc = a["cache_mem_v"][0].reshape(8, 2, 128, 1024).transpose(0, 2, 1, 3)
    state = a["state_gla"][0].reshape(8, 2, 128, 128)
    u_t = a["expert_u"][0].reshape(128, 128, 8, 128).transpose(1, 3, 2, 0).reshape(128, 128, 1024)
    v_t = a["expert_v"][0].reshape(128, 128, 1024).transpose(1, 0, 2)
    gcols = np.stack([a[n][0].reshape(8, 128).T for n in ("g_mix", "g_mem", "g_cross", "g_ffn")], axis=1)
    grow = np.concatenate([a[n][0] for n in ("g_q", "g_k", "g_gla_out", "g_cq", "g_ck")])
    grows = np.broadcast_to(grow, (128, 768))
    wg2 = np.concatenate([a["w_gate2"][0], a["b_gate2"]], axis=0)
    keys = np.stack([a["sub_keys1"][0].T, a["sub_keys2"][0].T])
    s, t = np.arange(128)[:, None], np.arange(128)[None, :]

    def tri(L):
        same = (s // L) == (t // L)
        mid = (s // L) * L + L // 2 - 1
        centred = (same & (s <= t)).astype(f) - (same & (s <= mid)).astype(f)
        mids = ((s // L) == np.arange(128 // L)[None, :]).astype(f) * (s <= mid)
        return np.concatenate([centred, mids], axis=1) / 16.0

    def causal(L):
        return (((s // L) == (t // L)) & (s <= t)).astype(f)

    consts = np.concatenate([np.eye(128), np.broadcast_to(np.arange(128), (128, 128)), causal(64), causal(16),
                             tri(64), tri(16), (s // 16) == np.arange(8)[None, :]], axis=1).astype(f)
    arrays = {"x_in": x, "mem_in": a["mem_prompt"][0], "w_in": w_in, "w_gl": w_in[:, 2560:2576], "w_out": a["w_out"][0],
              "w_cq": a["w_cq"][0], "w_ck": a["w_ck"][0], "w_cv": a["w_cv"][0], "w_co": a["w_co"][0],
              "w_pq": a["w_pq"][0], "wg2": wg2, "gcols": gcols, "grows": grows, "bias_p": bias_p, "bias_s": bias_s,
              "kc_t": kc, "v_c": vc, "state_in": state, "mk_c": mkc, "mv_c": mvc, "keys_t": keys, "u_t": u_t,
              "v_t": v_t, "consts": consts}
    arrays = {k: np.ascontiguousarray(v) for k, v in arrays.items()}
    outs = {"y_out": (640, 1024), "k_out": (640, 512), "v_out": (640, 512), "gp_out": (2, 128, 128),
            "gs_out": (8, 2, 128, 128), "mk_out": (256, 1024), "mv_out": (256, 1024)}

    nc = _bacc.Bacc("TRN2", target_bir_lowering=False, num_devices=1)
    F = _mybir.dt.float32
    aps = {k: nc.dram_tensor(k, v.shape, F, kind="ExternalInput").ap() for k, v in arrays.items()}
    aps |= {k: nc.dram_tensor(k, v, F, kind="ExternalOutput").ap() for k, v in outs.items()}
    w_dram = nc.dram_tensor("w_dram", (NBLK, P, NTG, EB * TG), F).ap()
    peer_stream_step(nc, w_dram=w_dram, **aps)
    r = _run(nc, [arrays], core_ids=[0]).results[0]
    y, k, v = r["y_out"], r["k_out"], r["v_out"]
    return (y[:512].reshape(1, 512, 1024), y[512:].reshape(8, 16, 1024),
            k[:512].reshape(1, 1, 512, 8, 64), v[:512].reshape(1, 1, 512, 8, 64),
            r["gp_out"].reshape(1, 1, 4, 64, 128),
            r["mk_out"].reshape(1, 1, 256, 4, 256), r["mv_out"].reshape(1, 1, 256, 4, 256),
            k[512:].reshape(1, 8, 16, 8, 64), v[512:].reshape(1, 8, 16, 8, 64),
            r["gs_out"].reshape(1, 8, 4, 64, 128))
```

```python
from contextlib import ExitStack

import concourse.bass as bass
from concourse import mybir

F32 = mybir.dt.float32
F16 = mybir.dt.float16
U32 = mybir.dt.uint32
ALU = mybir.AluOpType
ACT = mybir.ActivationFunctionType
AX = mybir.AxisListType

P = 128
D = 1024
KT = D // P
SEQ, DEC_B, DEC_T = 512, 8, 16
T = SEQ + DEC_B * DEC_T
NT = T // P
PT_TILES = SEQ // P
AH, AD = 8, 64
GH, GK, GV = 4, 64, 128
CHUNK = 64
BANDK = 512
NEWK = BANDK + DEC_T
XH, XD, NMEM = 4, 256, 256
NK = 128
TOPK = 16
PH = 8
EPS = 1e-6
UNIT = 512
WSLOTS = 2
BSLOTS = 4
EB = 4
NBLK = NK // EB
TG = 32
NTG = T // TG
USCALE = 1024.0
OHB = 16
AHEAD = 16
NA = AHEAD * EB
NEG = -3.0e38
CREDIT = 16


def peer_stream_step(nc, x_in, mem_in, w_in, w_gl, w_out, w_cq, w_ck, w_cv, w_co, w_pq, wg2, gcols, grows,
                     bias_p, bias_s, kc_t, v_c, state_in, mk_c, mv_c, keys_t, u_t, v_t, consts,
                     y_out, k_out, v_out, gp_out, gs_out, mk_out, mv_out, w_dram, g_dram):
    ctx = ExitStack()
    with ctx:
        def sem(name):
            return ctx.enter_context(nc.semaphore(name))

        AR = ctx.enter_context(nc.sbuf_tensor("arena", [P, 53200], F32))
        PS = ctx.enter_context(nc.psum_tensor("banks", [P, 8, 512], F32))

        def at(off, *shape):
            n = 1
            for s in shape:
                n *= s
            v = AR[:, off:off + n]
            if len(shape) == 2:
                v = v.rearrange("p (a b) -> p a b", a=shape[0])
            elif len(shape) == 3:
                v = v.rearrange("p (a b c) -> p a b c", a=shape[0], b=shape[1])
            elif len(shape) == 4:
                v = v.rearrange("p (a b c d) -> p a b c d", a=shape[0], b=shape[1], c=shape[2])
            return v

        X = at(0, NT, D)
        CB = 5120
        cons = at(CB, 128 * 5 + 130 + 136 + 8)
        ident = AR[:, CB:CB + 128]
        iota = AR[:, CB + 128:CB + 256]
        maskp = AR[:, CB + 256:CB + 384]
        masks = AR[:, CB + 384:CB + 512]
        trip = AR[:, CB + 512:CB + 642]
        tris = AR[:, CB + 642:CB + 778]
        bmask = AR[:, CB + 778:CB + 786]
        NCONST = 786
        gc_sb = at(CB + 786, 4, KT)
        gr_sb = AR[:, CB + 818:CB + 818 + 768]
        wg2_sb = AR[0:17, CB + 1586:CB + 1842]
        bs_sb = AR[:, CB + 1842:CB + 1842 + NEWK]
        eps_sb = AR[:, CB + 2370:CB + 2371]
        gq, gk, ggla = gr_sb[:, 0:64], gr_sb[:, 64:128], gr_sb[:, 128:256]
        gcq, gck = gr_sb[:, 256:512], gr_sb[:, 512:768]
        MM = 7500
        mv_tm = at(MM, 2, D)
        mkT = at(MM + 2048, 2 * XH, NMEM)
        BI = MM + 4096
        smid_p = at(BI, 4, 2, P)
        H16 = MM
        hhi = AR[:, H16:H16 + 2560].bitcast(F16).rearrange("p (k t) -> p k t", k=KT)
        hlo = AR[:, H16 + 2560:H16 + 5120].bitcast(F16).rearrange("p (k t) -> p k t", k=KT)
        TA = 12620
        hT = at(TA, KT, T)
        memT = at(TA, KT, NMEM)
        mk_tm = at(TA + 2048, 2, D)
        glT = AR[0:17, TA + 4096:TA + 4096 + T]
        QZ = at(TA, 2, DEC_B, P)
        bias_ring = at(TA, BSLOTS, 512)
        zz = at(TA + 2048, 2, 256)
        ll = at(TA + 2560, 2, 256)
        eplus = at(TA + 3072, 2, 2, 136)
        eminus = at(TA + 4736, 2, P)
        TB = 17740
        q_tm = at(TB, NT, 512)
        k_tm = at(TB + 2560, NT, 512)
        mixT = at(TB, KT, T)
        cq_tm = at(TB, NT, D)
        qry = at(TB, 8, T)
        V5 = 22860
        v_tm = at(V5, NT, 512)
        sel16 = AR[:, V5:V5 + 1280].bitcast(F16).rearrange("p (x t) -> p x t", x=4)
        G3 = V5 + 2560
        qk_tm = at(G3, NT, 512)
        vg = at(G3 + 2560, NT, 512)
        rr = at(G3 + 5120, NT, 512)
        smid_s = at(G3, DEC_B, 2, P)
        st_s = at(G3 + 2560, DEC_B, 2, P)
        khm = at(G3 + 5120, DEC_B, 256)
        kc_ring = at(G3, 2, 4, 512)
        vc_ring = at(G3 + 4096, 2, 4, 512)
        mkc_ring = at(G3, 2, 2 * XH, NMEM)
        mvc_ring = at(G3 + 4096, 2, 2, D)
        s_ring = at(G3, 2, NT, 4 * NK)
        QK = G3 + 8192
        qT = at(QK, 4, T)
        kT = at(QK + 2560, 4, T)
        cqT = at(QK, KT, T)
        cand = at(QK, PH, 256)
        eq = at(QK + 2048, P, TOPK)
        ts = at(QK + 4096, PH, TOPK)
        tp = AR[:, QK + 4224:QK + 4352].bitcast(U32)
        jf = at(QK + 4352, 2, P)
        ji = at(QK + 4608, 2, P).bitcast(U32)
        WR = QK + 5120
        ring = at(WR, WSLOTS, KT, UNIT)
        TM = WR + WSLOTS * 4096
        xn = at(TM, 2, D)
        junk = AR[:, TM + 2048:TM + 3072]
        er = at(TM + 3072, 2, 512)
        sq = at(TM + 4400, 2, 512)
        ATm = at(TM, 2, 2, P)
        kh_tm = at(TM + 1024, 2, 256)
        hats = at(TM + 2048, 2, 4, P)
        og = at(TM + 3072, 2, 512)
        S_sb = at(TM, 2, NEWK)
        PT_sb = at(TM + 1056, 2, 5, P)
        QB = at(TM + 2336, 4, DEC_B, 32)
        vn = at(TM + 3360, 2, 512)
        QX = at(TM + 2336, KT, DEC_B, 32)
        topif = at(TM, 2, PH, TOPK)
        top_v = at(TM + 1280, NT, 2 * PH, TOPK)
        top_i = at(TM + 2560, NT, 2 * PH * TOPK).bitcast(U32)
        iota16 = AR[:, V5 + 1280:V5 + 2304].bitcast(F16).rearrange("p (i t) -> p i t", t=OHB)
        oh = AR[:, G3:G3 + 6144].bitcast(F16).rearrange("p (s x i t) -> p s x i t", s=2, x=3, t=OHB)
        eqa = AR[:, G3 + 6144:G3 + 7168].bitcast(F16).rearrange("p (i t) -> p i t", t=OHB)
        stage = at(WR, 2, NK, TG)
        wgl_sb = at(TM + 4096, KT, 16)
        sg = at(TM + 512, P)
        gsum = at(TM + 640, PH)
        srep = AR[:, TM + 1024:TM + 1280]
        keys_sb = at(TM + 4096, 2, NK)
        ST = TM + 5424
        hn_ss = at(ST, 2, 8)
        hn_rs = at(ST + 16, 2, 8)
        nrm_ss = at(ST + 32, 2, 1)
        nrm_rs = at(ST + 34, 2, 1)
        sm_nm = at(ST + 40, 2, 2)
        sm_sum = at(ST + 44, 2, 2)
        sm_inv = at(ST + 48, 2, 2)
        sm_max = at(ST + 52, 2, 2)
        S_p = at(TM + 6020, 2, P)
        R1, R2 = TA, G3 - 640
        ust = at(R1, 4, KT, P)
        u16 = AR[:, R1 + 4096:R1 + 8192].bitcast(F16).rearrange("p (s x k e) -> p s x k e", s=4, x=2, k=KT)
        gel = at(R1 + 8192, 2, T)
        vst = at(R2, 4, D)
        v16 = AR[:, R2 + 4096:R2 + 12288].bitcast(F16).rearrange("p (s x d) -> p s x d", s=2 * EB, x=2)
        a16 = AR[:, R2 + 12288:R2 + 17408].bitcast(F16).rearrange("p (s x t) -> p s x t", s=2 * EB, x=2)
        W_sb = at(R2 + 17408, 2, NTG, EB, TG)
        a32 = at(R2 + 22528, 2, T)

        bank_full = [sem(f"bank_full{b}") for b in range(8)]
        bank_free = [sem(f"bank_free{b}") for b in range(8)]
        x_in_s = sem("x_loaded")
        c_in = sem("consts_loaded")
        mem_in_s = [sem(f"mem_loaded{i}") for i in range(2)]
        w_in_s = [sem(f"weights_loaded{i}") for i in range(WSLOTS)]
        bias_s_ = [sem(f"bias_loaded{i}") for i in range(BSLOTS)]
        kc_s = [sem(f"cache_k_loaded{i}") for i in range(2)]
        vc_s = [sem(f"cache_v_loaded{i}") for i in range(2)]
        vn_s = [sem(f"newv_loaded{i}") for i in range(2)]
        mkc_s = [sem(f"memcache_k_loaded{i}") for i in range(2)]
        mvc_s = [sem(f"memcache_v_loaded{i}") for i in range(2)]
        st_s_s = sem("states_loaded")
        keys_s = sem("keys_loaded")
        outs = {n: sem(f"{n}_stored") for n in ("v", "mk", "mv", "gp", "gs")}
        kout_s = sem("k_stored")
        y_s = sem("y_stored")
        dve_step = sem("dve_step")
        act_step = sem("act_step")
        zero_s = sem("tiles_cleared")
        nrm = {n: (sem(f"{n}_rstd"), sem(f"{n}_scaled")) for n in ("mix", "mem", "cross", "ffn")}
        hn = {n: tuple(sem(f"{n}_{w}") for w in ("squares", "sums", "rstd", "normed")) for n in ("qk", "mk", "gla", "cq")}
        r_exp = sem("r_exp")
        r_silu = sem("r_silu")
        g_l = sem("gate_log")
        g_la = sem("log_a")
        g_hat = sem("hats_ready")
        g_smid = sem("state_scaled")
        g_st = sem("state_updated")
        g_khm = sem("khat_masked")
        qb_s = sem("blockq_ready")
        sm = {n: tuple(sem(f"{n}_{w}") for w in ("max", "exp", "prob")) for n in ("att", "xat")}
        qx_s = sem("padded_q_ready")
        x_mix = sem("x_after_mix")
        x_cross = sem("x_after_cross")
        h_split = sem("h_split")
        tk_exp_in = sem("topk_shifted")
        tk_exp = sem("topk_exp")
        tk_done = sem("topk_selected")
        sel_mm = sem("choices_transposed")
        oh_s = sem("onehots_ready")
        gst = [sem(f"gelu_stored{i}") for i in range(2)]
        g_in = [sem(f"gelu_loaded{i}") for i in range(2)]
        wg_mm = sem("gate_mm_done")
        wg_ev = sem("gate_evacuated")
        wst_s = [sem(f"gate_stored{i}") for i in range(2)]
        u_in = [sem(f"u_loaded{i}") for i in range(4)]
        v_in = [sem(f"v_loaded{i}") for i in range(4)]
        W_in = [sem(f"gates_loaded{i}") for i in range(2)]
        u_hi0 = sem("u_high_only")
        u_hi = sem("u_high")
        u_sp = sem("u_split")
        v_hi = sem("v_high")
        v_sp = sem("v_split")
        z_mm = sem("z_done")
        z_ge = sem("gelu_done")
        a_mul = sem("act_gated")
        a_hi = sem("act_high")
        a_sp = sem("act_split")
        y_mm = sem("y_done")
        y_ev = sem("y_added")

        groups = {}
        uses = [0] * 8

        def open_group(pe, key):
            b = len(groups) % 8
            if uses[b]:
                pe.wait_ge(bank_free[b], uses[b])
            uses[b] += 1
            groups[key] = (b, uses[b])
            return PS[:, b, :], bank_full[b]

        def full(eng, *key):
            b, n = groups[key]
            eng.wait_ge(bank_full[b], n)
            return PS[:, b, :], bank_free[b]

        def drained(eng, *key):
            b, n = groups[key]
            eng.wait_ge(bank_free[b], n)

        count = {}

        def link(eng, ins, s):
            count[id(s)] = count.get(id(s), 0) + 1
            ins.then_inc(s, 1)
            eng.wait_ge(s, count[id(s)])

        UNITS = ([("in", w_in, c) for c in (0, 512, 1024, 1536, 2048, 2576)]
                 + [("ck", w_ck, c) for c in (0, 512)] + [("cv", w_cv, c) for c in (0, 512)]
                 + [("wo", w_out, c) for c in (0, 512)] + [("cq", w_cq, c) for c in (0, 512)]
                 + [("co", w_co, c) for c in (0, 512)] + [("pq", w_pq, c) for c in (0, 512, 1024, 1536)])
        unit_last = {}

        def spread(prompt):
            each = len(prompt) // DEC_B
            order = []
            for b in range(DEC_B):
                order += prompt[b * each:(b + 1) * each] + [("s", b, 0)]
            return order

        SMU = spread([("p", h, qt) for qt in range(PT_TILES) for h in range(AH)])
        XU = spread([("p", hp, qt) for qt in range(PT_TILES) for hp in range(2)])
        bias_use = {m: n for n, m in enumerate(m for m, unit in enumerate(SMU) if unit[0] == "p")}

        NORMS = {"mix": (0, NT, lambda t: X[:, t, :], lambda t, g: hT[:, 4 * g:4 * g + 4, t * P:(t + 1) * P]),
                 "mem": (1, 2, lambda t: mk_tm[:, t, :], lambda t, g: memT[:, 4 * g:4 * g + 4, t * P:(t + 1) * P]),
                 "cross": (2, NT, lambda t: X[:, t, :], lambda t, g: hT[:, 4 * g:4 * g + 4, t * P:(t + 1) * P]),
                 "ffn": (3, NT, lambda t: X[:, t, :], lambda t, g: hT[:, 4 * g:4 * g + 4, t * P:(t + 1) * P])}

        block = ctx.enter_context(nc.Block())

        @block.tensor
        def _(pe):
            def norm_transposes(name):
                for t in range(NORMS[name][1]):
                    pe.wait_ge(nrm[name][1], t + 1)
                    for g in range(2):
                        ps, done = open_group(pe, ("T" + name, t, g))
                        for j in range(4):
                            mm = pe.transpose(ps[:, j * P:(j + 1) * P], xn[:, t % 2, (4 * g + j) * P:(4 * g + j + 1) * P],
                                              ident)
                        mm.then_inc(done, 1)

            def project(u, srcT, name, t, rows=P):
                slot = u % WSLOTS
                pe.wait_ge(w_in_s[slot], 16 * (u // WSLOTS + 1))
                ps, done = open_group(pe, (name, u, t))
                for k in range(KT):
                    mm = pe.matmul(ps, srcT[:, k, t * P:(t + 1) * P], ring[:, slot, k, :],
                                   start=(k == 0), stop=(k == KT - 1))
                mm.then_inc(done, 1)
                unit_last[u] = (name, u, t)

            pe.wait_ge(c_in, 16 * 7)
            norm_transposes("mix")
            for u in range(6):
                for t in range(NT):
                    if u == 0:
                        for g in range(2):
                            drained(pe, "Tmix", t, g)
                    project(u, hT, "z", t)
            for i in range(2):
                ps, done = open_group(pe, ("gl", i))
                for k in range(KT):
                    mm = pe.matmul(ps[0:16, 0:320], wgl_sb[:, k, :], hT[:, k, 320 * i:320 * i + 320],
                                   start=(k == 0), stop=(k == KT - 1))
                mm.then_inc(done, 1)
            norm_transposes("mem")
            for u in range(6, 10):
                for t in range(2):
                    if u == 6:
                        for g in range(2):
                            drained(pe, "Tmem", t, g)
                    project(u, memT, "m", t)
            for t in range(NT):
                for which, tm in (("q", q_tm), ("k", k_tm)):
                    pe.wait_ge(hn["qk"][3], 2 * NT if which == "k" else NT + 1)
                    ps, done = open_group(pe, (which + "T", t))
                    for c in range(4):
                        mm = pe.transpose(ps[:, c * P:(c + 1) * P], tm[:, t, c * P:(c + 1) * P], ident)
                    mm.then_inc(done, 1)
            for t in range(2):
                pe.wait_ge(hn["mk"][3], 4)
                for g in range(2):
                    ps, done = open_group(pe, ("mkT", t, g))
                    for j in range(4):
                        mm = pe.transpose(ps[:, j * P:(j + 1) * P], mk_tm[:, t, (4 * g + j) * P:(4 * g + j + 1) * P],
                                          ident)
                    mm.then_inc(done, 1)

            def gla_gate(t):
                drained(pe, "gl", 0)
                drained(pe, "gl", 1)
                ps, done = open_group(pe, ("z2", t))
                pe.matmul(ps[:, 0:256], glT[:, t * P:(t + 1) * P], wg2_sb, start=True, stop=True).then_inc(done, 1)

            def gla_tile(t):
                tri = trip if t < PT_TILES else tris
                W = 130 if t < PT_TILES else 136
                ps, done = open_group(pe, ("gT", t))
                for c in range(4):
                    mm = pe.transpose(ps[:, c * P:(c + 1) * P], qk_tm[:, t, c * P:(c + 1) * P], ident)
                mm.then_inc(done, 1)
                pe.wait_ge(g_la, t + 1)
                ps, done = open_group(pe, ("cum", t))
                for p in range(2):
                    mm = pe.matmul(ps[:, 256 * p:256 * p + W], zz[:, t % 2, p * P:(p + 1) * P], tri,
                                   start=True, stop=True)
                mm.then_inc(done, 1)
                qh = hats[:, t % 2, 0:2, :]
                kh = hats[:, t % 2, 2:4, :]
                pe.wait_ge(g_hat, t + 1)
                ps, done = open_group(pe, ("kh", t))
                for p in range(2):
                    mm = pe.transpose(ps[:, p * P:(p + 1) * P], kh[:, p, :], ident)
                mm.then_inc(done, 1)
                for par in range(2):
                    o = 64 * par
                    ps, done = open_group(pe, ("A", t, par))
                    for p in range(2):
                        mm = pe.matmul(ps[:, p * P:(p + 1) * P], kh[o:o + 64, p, :], qh[o:o + 64, p, :],
                                       start=True, stop=True)
                    mm.then_inc(done, 1)
                drained(pe, "kh", t)
                if t < PT_TILES:
                    for c in range(2):
                        ps, done = open_group(pe, ("KV", t, c))
                        for h in range(GH):
                            o = 64 * (h % 2)
                            mm = pe.matmul(ps[o:o + 64, (h // 2) * P:(h // 2 + 1) * P],
                                           kh_tm[64 * c:64 * c + 64, t % 2, h * 64:h * 64 + 64],
                                           vg[64 * c:64 * c + 64, t, h * P:(h + 1) * P], start=True, stop=True)
                        mm.then_inc(done, 1)
                else:
                    pe.wait_ge(g_khm, 1)
                    for c in range(4):
                        ps, done = open_group(pe, ("KV", t, c))
                        for i in range(2):
                            for h in range(GH):
                                o = 64 * (h % 2)
                                mm = pe.matmul(ps[o:o + 64, i * 256 + (h // 2) * P:i * 256 + (h // 2 + 1) * P],
                                               khm[:, 2 * c + i, h * 64:h * 64 + 64],
                                               vg[:, t, h * P:(h + 1) * P], start=True, stop=True)
                        mm.then_inc(done, 1)
                drained(pe, "A", t, 0)
                drained(pe, "A", t, 1)
                pe.wait_ge(g_smid, 2 * t + 2 if t < PT_TILES else 2 * t + 1)
                for par in range(2):
                    o = 64 * par
                    ps, done = open_group(pe, ("go", t, par))
                    for p in range(2):
                        out = ps[:, p * P:(p + 1) * P]
                        h = 2 * p + par
                        pe.matmul(out, ATm[:, par, p, :], vg[:, t, h * P:(h + 1) * P], start=True, stop=False)
                        if t < PT_TILES:
                            for c in range(2):
                                mm = pe.matmul(out[64 * c:64 * c + 64, :], qh[o:o + 64, p, 64 * c:64 * c + 64],
                                               smid_p[o:o + 64, 2 * (t % 2) + c, p, :], start=False, stop=True)
                        else:
                            for b in range(DEC_B):
                                mm = pe.matmul(out, QZ[o:o + 64, p, b, :], smid_s[o:o + 64, b, p, :],
                                               start=False, stop=(b == DEC_B - 1))
                    mm.then_inc(done, 1)

            def gla_out(t):
                pe.wait_ge(hn["gla"][3], t + 1)
                ps, done = open_group(pe, ("ogT", t))
                for c in range(4):
                    mm = pe.transpose(ps[:, c * P:(c + 1) * P], og[:, t % 2, c * P:(c + 1) * P], ident)
                mm.then_inc(done, 1)

            gla_gate(0)
            for t in range(NT):
                if t + 1 < NT:
                    gla_gate(t + 1)
                gla_tile(t)
                if t:
                    gla_out(t - 1)
            gla_out(NT - 1)

            def att_scores(m):
                kind, a, qt = SMU[m]
                if kind == "p":
                    for t in range(qt + 1):
                        drained(pe, "qT", t)
                        drained(pe, "kT", t)
                    o, n = 64 * (a % 2), (qt + 1) * P
                    ps, done = open_group(pe, ("s", m))
                    pe.matmul(ps[:, 0:n], qT[o:o + 64, a // 2, qt * P:(qt + 1) * P], kT[o:o + 64, a // 2, 0:n],
                              start=True, stop=True).then_inc(done, 1)
                else:
                    pe.wait_ge(qb_s, 1)
                    drained(pe, "kT", NT - 1)
                    pe.wait_ge(kc_s[a % 2], 16 * (a // 2 + 1))
                    for part in range(2):
                        ps, done = open_group(pe, ("s", m) if part == 0 else ("s2", m))
                        for p in range(4):
                            rhs = (kc_ring[:, a % 2, p, :] if part == 0
                                   else kT[:, p, SEQ + DEC_T * a:SEQ + DEC_T * (a + 1)])
                            out = ps[32 * p:32 * p + 32, 0:BANDK if part == 0 else DEC_T]
                            mm = pe.matmul(out, QB[:, p, a, :], rhs, start=True, stop=True,
                                           tile_position=(0, 32 * p))
                        mm.then_inc(done, 1)

            def att_probs(m):
                kind, a, qt = SMU[m]
                pe.wait_ge(sm["att"][2], m + 1)
                ps, done = open_group(pe, ("PT", m))
                for k in range(qt + 1 if kind == "p" else 4):
                    mm = pe.transpose(ps[:, k * P:(k + 1) * P], S_sb[:, m % 2, k * P:(k + 1) * P], ident)
                mm.then_inc(done, 1)
                if kind == "s":
                    ps, done = open_group(pe, ("PT2", m))
                    pe.transpose(ps[0:DEC_T, 0:P], S_sb[:, m % 2, BANDK:NEWK], ident).then_inc(done, 1)

            def att_values(m):
                kind, a, qt = SMU[m]
                drained(pe, "PT", m)
                if kind == "p":
                    o = 64 * (a % 2)
                    ps, done = open_group(pe, ("o", m))
                    for k in range(qt + 1):
                        mm = pe.matmul(ps[o:o + 64, 0:P], v_tm[:, k, a * 64:(a + 1) * 64], PT_sb[:, m % 2, k, :],
                                       start=(k == 0), stop=(k == qt))
                    mm.then_inc(done, 1)
                else:
                    drained(pe, "PT2", m)
                    pe.wait_ge(vc_s[a % 2], 16 * (a // 2 + 1))
                    pe.wait_ge(vn_s[a % 2], 16 * (a // 2 + 1))
                    ps, done = open_group(pe, ("o", m))
                    for h in range(AH):
                        o = 64 * (h % 2)
                        out = ps[o:o + 64, (h // 2) * DEC_T:(h // 2 + 1) * DEC_T]
                        for k in range(4):
                            pe.matmul(out, vc_ring[:, a % 2, k, h * 64:(h + 1) * 64],
                                      PT_sb[:, m % 2, k, DEC_T * h:DEC_T * (h + 1)], start=(k == 0), stop=False)
                        mm = pe.matmul(out, vn[0:DEC_T, a % 2, h * 64:(h + 1) * 64],
                                       PT_sb[0:DEC_T, m % 2, 4, DEC_T * h:DEC_T * (h + 1)], start=False, stop=True)
                    mm.then_inc(done, 1)

            for m in range(len(SMU) + 3):
                if m < len(SMU):
                    att_scores(m)
                if 2 <= m < len(SMU) + 2:
                    att_probs(m - 2)
                if m >= 3:
                    att_values(m - 3)
            for t in range(NT):
                for u in range(10, 12):
                    if u == 10:
                        drained(pe, "ogT", t)
                        for m, (kind, a, qt) in enumerate(SMU):
                            if (qt == t and kind == "p") or (kind == "s" and t == NT - 1):
                                drained(pe, "o", m)
                    project(u, mixT, "w", t)
            norm_transposes("cross")
            for u in range(12, 14):
                for t in range(NT):
                    if u == 12:
                        for g in range(2):
                            drained(pe, "Tcross", t, g)
                    project(u, hT, "cq", t)
            for t in range(NT):
                pe.wait_ge(hn["cq"][3], NT + t + 1)
                for g in range(2):
                    ps, done = open_group(pe, ("cqT", t, g))
                    for j in range(4):
                        mm = pe.transpose(ps[:, j * P:(j + 1) * P], cq_tm[:, t, (4 * g + j) * P:(4 * g + j + 1) * P],
                                          ident)
                    mm.then_inc(done, 1)

            def x_scores(m):
                kind, a, qt = XU[m]
                ps, done = open_group(pe, ("xs", m))
                if kind == "p":
                    drained(pe, "cqT", qt, a)
                    if m == 0:
                        for t in range(2):
                            for g in range(2):
                                drained(pe, "mkT", t, g)
                    for i in range(2):
                        for d in range(2):
                            mm = pe.matmul(ps[:, i * NMEM:(i + 1) * NMEM], cqT[:, 4 * a + 2 * i + d, qt * P:(qt + 1) * P],
                                           mkT[:, 4 * a + 2 * i + d, :], start=(d == 0), stop=(d == 1))
                else:
                    pe.wait_ge(qx_s, 1)
                    pe.wait_ge(mkc_s[a % 2], 16 * (a // 2 + 1))
                    for h in range(XH):
                        for d in range(2):
                            mm = pe.matmul(ps[32 * h:32 * h + 32, 0:NMEM], QX[:, 2 * h + d, a, :],
                                           mkc_ring[:, a % 2, 2 * h + d, :], start=(d == 0), stop=(d == 1),
                                           tile_position=(0, 32 * h))
                mm.then_inc(done, 1)

            def x_probs(m):
                kind, a, qt = XU[m]
                pe.wait_ge(sm["xat"][2], m + 1)
                ps, done = open_group(pe, ("xPT", m))
                for k in range(4 if kind == "p" else 2):
                    mm = pe.transpose(ps[:, k * P:(k + 1) * P], S_sb[:, m % 2, k * P:(k + 1) * P], ident)
                mm.then_inc(done, 1)

            def x_values(m):
                kind, a, qt = XU[m]
                drained(pe, "xPT", m)
                ps, done = open_group(pe, ("xo", m))
                if kind == "p":
                    if m == 0:
                        for u in range(8, 10):
                            for t in range(2):
                                drained(pe, "m", u, t)
                    for i in range(2):
                        for d in range(2):
                            c = (4 * a + 2 * i + d) * P
                            for k in range(2):
                                mm = pe.matmul(ps[:, (2 * i + d) * P:(2 * i + d + 1) * P], mv_tm[:, k, c:c + P],
                                               PT_sb[:, m % 2, 2 * i + k, :], start=(k == 0), stop=(k == 1))
                else:
                    pe.wait_ge(mvc_s[a % 2], 16 * (a // 2 + 1))
                    for j in range(2 * XH):
                        for k in range(2):
                            mm = pe.matmul(ps[:, j * DEC_T:(j + 1) * DEC_T], mvc_ring[:, a % 2, k, j * P:(j + 1) * P],
                                           PT_sb[:, m % 2, k, 32 * (j // 2):32 * (j // 2) + DEC_T],
                                           start=(k == 0), stop=(k == 1))
                mm.then_inc(done, 1)

            for m in range(len(XU) + 3):
                if m < len(XU):
                    x_scores(m)
                if 2 <= m < len(XU) + 2:
                    x_probs(m - 2)
                if m >= 3:
                    x_values(m - 3)
            for t in range(NT):
                for u in range(14, 16):
                    if u == 14:
                        for m, (kind, a, qt) in enumerate(XU):
                            if (qt == t and kind == "p") or (kind == "s" and t == NT - 1):
                                drained(pe, "xo", m)
                    project(u, hT, "co", t)
            norm_transposes("ffn")
            pe.wait_ge(keys_s, 32)
            for u in range(16, 20):
                slot = u % WSLOTS
                pe.wait_ge(w_in_s[slot], 16 * (u // WSLOTS + 1))
                for j in range(4):
                    for i in range(2):
                        if u == 16 and j == 0:
                            for t in range(NT if i else 3):
                                for g in range(2):
                                    drained(pe, "Tffn", t, g)
                        ps, done = open_group(pe, ("pq", u, j, i))
                        for k in range(KT):
                            mm = pe.matmul(ps[:, 0:320], ring[:, slot, k, j * P:(j + 1) * P],
                                           hT[:, k, 320 * i:320 * i + 320], start=(k == 0), stop=(k == KT - 1))
                        mm.then_inc(done, 1)
                        unit_last[u] = ("pq", u, j, i)
                for j in range(4):
                    for i in range(2):
                        drained(pe, "pq", u, j, i)
                for t in range(NT):
                    ps, done = open_group(pe, ("sc", u, t))
                    for j in range(4):
                        mm = pe.matmul(ps[:, j * NK:(j + 1) * NK], qry[:, 4 * (u % 2) + j, t * P:(t + 1) * P],
                                       keys_sb[:, j % 2, :], start=True, stop=True)
                    mm.then_inc(done, 1)

            for b in range(8):
                pe.wait_ge(bank_free[b], uses[b])

            def z_tile(k, n, first=False):
                pe.wait_ge(u_sp, n + 1)
                if not first:
                    pe.wait_ge(z_ge, n - 1)
                for i in range(2):
                    for kk in range(KT):
                        for x, (a, b) in enumerate(((0, hhi), (0, hlo), (1, hhi))):
                            mm = pe.matmul(PS[:, 2 * (k % 2) + i, 0:320], u16[:, k % 4, a, kk, :],
                                           b[:, kk, 320 * i:320 * i + 320], start=(kk == 0 and x == 0),
                                           stop=(kk == KT - 1 and x == 2))
                mm.then_inc(z_mm, 1)

            def y_block(par, B, first=False):
                pe.wait_ge(a_sp, B * EB + EB)
                pe.wait_ge(v_sp, B * EB + EB)
                for g in range(2 * NT):
                    if not (first and g < 4):
                        pe.wait_ge(y_ev, B * (2 * NT) + (g - 3))
                    t, half = g // 2, g % 2
                    bank = 4 + (par * 2 * NT + g) % 4
                    for e in range(EB):
                        s = EB * par + e
                        for x, (a, b) in enumerate(((0, 0), (0, 1), (1, 0))):
                            mm = pe.matmul(PS[:, bank, :], a16[:, s, a, t * P:(t + 1) * P],
                                           v16[:, s, b, half * 512:(half + 1) * 512], start=(e == 0 and x == 0),
                                           stop=(e == EB - 1 and x == 2))
                    mm.then_inc(y_mm, 1)

            def gate_batch(slot, n):
                pe.wait_ge(oh_s, n + 1)
                for q in range(4):
                    pe.wait_ge(wg_ev, n * 4 + (CREDIT + q - 3))
                    for j in range(4):
                        for x in range(2):
                            mm = pe.matmul(PS[:, 4 + q, j * P:(j + 1) * P], oh[:, slot, x, :, 4 * q + j],
                                           oh[:, slot, 2, :, 4 * q + j], start=(x == 0), stop=(x == 1))
                    mm.then_inc(wg_mm, 1)

            pe.wait_ge(h_split, NT)
            for k in range(EB):
                z_tile(k, k, k < 2)
            with pe.Fori(0, NT) as i:
                for k in range(12):
                    z_tile(k % 4, i * 12 + (4 + k))
                    if k == 3:
                        pe.wait_ge(tk_done, i + 1)
                        pe.wait_ge(wg_ev, i * 32 + CREDIT)
                        pe.transpose(PS[:, 4, 0:P], sg, ident)
                        pe.transpose(PS[:, 4, P:2 * P], jf[:, 0, :], ident)
                        pe.transpose(PS[:, 4, 2 * P:3 * P], jf[:, 1, :], ident).then_inc(sel_mm, 1)
                    if k >= 4:
                        gate_batch(k % 2, i * 8 + (k - 4))
            pe.wait_ge(wg_ev, CREDIT + T // 4)
            y_block(0, 0, True)
            with pe.Fori(0, AHEAD // 2 - 1) as i:
                for s in range(2):
                    y_block(1 - s, i * 2 + (1 + s))
            for k in range(EB):
                z_tile(k, NA + k)
            with pe.Fori(0, (NBLK - AHEAD) // 2 - 1) as i:
                for s in range(2):
                    y_block(1 - s, i * 2 + (AHEAD - 1 + s))
                    for k in range(EB):
                        z_tile(k, i * (2 * EB) + (EB * (AHEAD + 1 + s) + k))
            y_block(1, NBLK - 3)
            for k in range(EB):
                z_tile(k, NK - EB + k)
            y_block(0, NBLK - 2)
            y_block(1, NBLK - 1)

        @block.sync
        def _(sp):
            def unit(u):
                name, w, c = UNITS[u]
                if u >= WSLOTS:
                    full(sp, *unit_last[u - WSLOTS])
                sp.dma_start(ring[:, u % WSLOTS, :, :], w.rearrange("(k p) n -> p k n", p=P)[:, :, c:c + UNIT])\
                  .then_inc(w_in_s[u % WSLOTS], 16)

            sp.dma_start(X[:, 0, :], x_in[0:P, :]).then_inc(x_in_s, 16)
            sp.dma_start(X[:, 1:NT, :], x_in[P:T, :].rearrange("(t p) d -> p t d", p=P)).then_inc(x_in_s, 16)
            sp.dma_start(AR[:, CB:CB + NCONST], consts).then_inc(c_in, 16)
            sp.dma_start(gc_sb, gcols).then_inc(c_in, 16)
            sp.dma_start(gr_sb, grows).then_inc(c_in, 16)
            sp.dma_start(wg2_sb, wg2).then_inc(c_in, 16)
            sp.dma_start(bs_sb, bias_s).then_inc(c_in, 16)
            sp.dma_start(wgl_sb, w_gl.rearrange("(k p) n -> p k n", p=P)).then_inc(c_in, 16)
            for u in range(len(UNITS)):
                unit(u)
                if u == 6:
                    for b in range(2):
                        if b == 0:
                            full(sp, "gl", 1)
                        sp.dma_start(mk_tm[:, b, :], mem_in[b * P:(b + 1) * P, :]).then_inc(mem_in_s[b], 16)

            def load_u(k, n, first=False):
                if not first:
                    sp.wait_ge(u_sp, n - 3)
                sp.dma_start(ust[:, k % 4, :, :], u_t[bass.ds(n, 1)].rearrange("e p n -> p (e n)"))\
                  .then_inc(u_in[k % 4], 16)

            def load_v(k, n, first=False):
                if not first:
                    sp.wait_ge(v_sp, n - 3)
                sp.dma_start(vst[:, k % 4, :], v_t[bass.ds(n, 1)].rearrange("e p n -> p (e n)"))\
                  .then_inc(v_in[k % 4], 16)

            def load_gelu(k, n, first=False):
                if not first:
                    sp.wait_ge(a_mul, n - 1)
                sp.dma_start(gel[:, k % 2, :], g_dram[bass.ds(n, 1)].rearrange("e p n -> p (e n)"))\
                  .then_inc(g_in[k % 2], 16)

            def load_gates(par, B, first=False):
                if not first:
                    sp.wait_ge(a_mul, B * EB - EB)
                sp.dma_start(W_sb[:, par, :, :, :], w_dram[bass.ds(B, 1)].rearrange("b p g n -> p (b g n)"))\
                  .then_inc(W_in[par], 16)

            def store_gelu(k, n):
                sp.wait_ge(z_ge, n + 1)
                sp.dma_start(g_dram[bass.ds(n, 1)].rearrange("e p n -> p (e n)"), gel[:, k % 2, :])\
                  .then_inc(gst[k % 2], 16)

            full(sp, "sc", 19, NT - 1)
            for k in range(EB):
                load_u(k, k, True)
            for k in range(EB):
                load_u(k, EB + k)
                store_gelu(k, k)
            for s in range(2):
                sp.sem_inc(wst_s[s], CREDIT)
            with sp.Fori(0, NT) as i:
                for k in range(12):
                    load_u(k, i * 12 + (8 + k))
                    store_gelu(k, i * 12 + (4 + k))
                    if k >= 4 and k % 2:
                        j = (k - 4) // 2
                        sp.wait_ge(wg_ev, i * 32 + (CREDIT + 8 * (j + 1)))
                        sp.dma_start(w_dram[:, :, bass.ds(i * 4 + j, 1), :].rearrange("b p g n -> p b (g n)"),
                                     stage[:, j % 2, :, :].rearrange("p (b e) t -> p b (e t)", e=EB))\
                          .then_inc(wst_s[j % 2], 16)
            for s in range(2):
                sp.wait_ge(wst_s[s], CREDIT + 16 * (NTG // 2))
                sp.wait_ge(gst[s], 16 * (NA // 2))
            load_v(0, 0, True)
            load_gates(0, 0, True)
            load_gelu(0, 0, True)
            load_v(1, 1, True)
            load_gelu(1, 1, True)

            def feed_y(par, B, first=False):
                load_gates(1 - par, B + 1, first)
                for k in range(EB):
                    load_v(k + 2, B * EB + (k + 2), first and k < 2)
                    if not (first and k < 2):
                        load_gelu(k, B * EB + k)

            def feed_zy(par, B):
                load_gates(1 - par, B + 1)
                for k in range(EB):
                    load_u(k, B * EB + (k + 4))
                    load_v(k + 2, B * EB + (k + 2))

            feed_y(0, 0, True)
            with sp.Fori(0, AHEAD // 2 - 1) as i:
                for s in range(2):
                    feed_y(1 - s, i * 2 + (1 + s))
            feed_y(1, AHEAD - 1)
            with sp.Fori(0, (NBLK - AHEAD) // 2 - 1) as i:
                for s in range(2):
                    feed_zy(s, i * 2 + (AHEAD + s))
            feed_zy(0, NBLK - 2)
            load_v(2, NK - 2)
            load_v(3, NK - 1)
            for t in range(NT):
                sp.wait_ge(y_ev, (NBLK - 1) * 2 * NT + 2 * (t + 1))
                sp.dma_start(y_out[t * P:(t + 1) * P, :], X[:, t, :]).then_inc(y_s, 16)
            sp.wait_ge(y_s, 16 * NT)
            sp.wait_ge(kout_s, 16)
            for stored in outs.values():
                sp.wait_ge(stored, 16)

        @block.gpsimd
        def _(pool):
            pool.wait_ge(hn["qk"][3], 2 * NT)
            pool.dma_start(k_out.rearrange("(t p) n -> p t n", p=P), k_tm).then_inc(kout_s, 16)
            for t in range(NT):
                drained(pool, "z", 2, t)
            pool.dma_start(v_out.rearrange("(t p) n -> p t n", p=P), v_tm).then_inc(outs["v"], 16)
            pool.wait_ge(hn["mk"][3], 4)
            pool.dma_start(mk_out.rearrange("(t p) n -> p t n", p=P), mk_tm).then_inc(outs["mk"], 16)
            for u in range(8, 10):
                for t in range(2):
                    drained(pool, "m", u, t)
            pool.dma_start(mv_out.rearrange("(t p) n -> p t n", p=P), mv_tm).then_inc(outs["mv"], 16)
            full(pool, "go", PT_TILES - 1, 1)
            pool.dma_start(st_s, state_in.rearrange("b g p v -> p b g v")).then_inc(st_s_s, 16)
            pool.wait_ge(g_st, 2 * PT_TILES)
            pool.dma_start(gp_out.rearrange("g p v -> p g v"), S_p).then_inc(outs["gp"], 16)
            full(pool, "go", NT - 1, 1)
            def load_bias(n):
                h = n % AH
                pool.dma_start(bias_ring[:, n % BSLOTS, :], bias_p[h]).then_inc(bias_s_[n % BSLOTS], 16)

            def load_keys(b):
                pool.dma_start(kc_ring[:, b % 2, :, :], kc_t[b]).then_inc(kc_s[b % 2], 16)

            def load_values(b):
                pool.dma_start(vc_ring[:, b % 2, :, :], v_c[b]).then_inc(vc_s[b % 2], 16)
                pool.dma_start(vn[0:DEC_T, b % 2, :], v_tm[DEC_T * b:DEC_T * (b + 1), NT - 1, :])\
                    .then_inc(vn_s[b % 2], 16)

            for n in range(2):
                load_bias(n)
            pool.wait_ge(g_st, 2 * PT_TILES + 4)
            pool.dma_start(gs_out.rearrange("b g p v -> p b g v"), st_s).then_inc(outs["gs"], 16)
            pool.wait_ge(outs["gs"], 16)
            pool.wait_ge(hn["gla"][3], NT)
            drained(pool, "ogT", NT - 1)
            full(pool, "ogT", NT - 1)
            for b in range(2):
                load_keys(b)
                load_values(b)
            for n in range(2, BSLOTS):
                load_bias(n)
            for m in range(len(SMU) + 3):
                if m < len(SMU):
                    kind, b, _ = SMU[m]
                    if kind == "p" and bias_use[m] + BSLOTS < len(bias_use):
                        pool.wait_ge(sm["att"][0], m + 1)
                        load_bias(bias_use[m] + BSLOTS)
                    if kind == "s" and b + 2 < DEC_B:
                        full(pool, "s", m)
                        load_keys(b + 2)
                if m >= 3 and SMU[m - 3][0] == "s" and SMU[m - 3][1] + 2 < DEC_B:
                    full(pool, "o", m - 3)
                    load_values(SMU[m - 3][1] + 2)

            def load_memkeys(b):
                pool.dma_start(mkc_ring[:, b % 2, :, :], mk_c[b]).then_inc(mkc_s[b % 2], 16)

            def load_memvalues(b):
                pool.dma_start(mvc_ring[:, b % 2, :, :], mv_c[b]).then_inc(mvc_s[b % 2], 16)

            for b in range(2):
                full(pool, "o", SMU.index(("s", DEC_B - 2 + b, 0)))
                load_memkeys(b)
                load_memvalues(b)
            for m in range(len(XU) + 3):
                if m < len(XU) and XU[m][0] == "s" and XU[m][1] + 2 < DEC_B:
                    full(pool, "xs", m)
                    load_memkeys(XU[m][1] + 2)
                if m >= 3 and XU[m - 3][0] == "s" and XU[m - 3][1] + 2 < DEC_B:
                    full(pool, "xo", m - 3)
                    load_memvalues(XU[m - 3][1] + 2)
            full(pool, "xs", len(XU) - 1)
            for i in range(2):
                pool.dma_start(keys_sb[:, i, :], keys_t[i]).then_inc(keys_s, 16)
            def u_low(k, n):
                pool.wait_ge(u_hi, n + 1)
                pool.tensor_tensor(u16[:, k, 1, :, :].rearrange("p k e -> p (k e)"),
                                   ust[:, k, :, :].rearrange("p k e -> p (k e)"),
                                   u16[:, k, 0, :, :].rearrange("p k e -> p (k e)"), ALU.subtract).then_inc(u_sp, 1)

            with pool.Fori(0, AHEAD + 1) as i:
                for k in range(EB):
                    u_low(k, i * EB + k)

        @block.scalar
        def _(act):
            def norm_stats(name, ready):
                _, n, src, _ = NORMS[name]
                for t in range(n):
                    ready(t)
                    link(act, act.activation(junk, src(t), ACT.Square, accum_out=nrm_ss[:, t % 2, :]), act_step)
                    if t >= 2:
                        act.wait_ge(nrm[name][1], t - 1)
                    link(act, act.activation(nrm_rs[:, t % 2, :], nrm_ss[:, t % 2, :], ACT.Ln, scale=1.0 / D,
                                             bias=eps_sb), act_step)
                    act.activation(nrm_rs[:, t % 2, :], nrm_rs[:, t % 2, :], ACT.Exp, scale=-0.5)\
                       .then_inc(nrm[name][0], 1)

            def head_norm(name, items, heads, width):
                sqs, sums, rstd, _ = hn[name]
                for m in range(len(items) + 1):
                    if m < len(items):
                        key, dst, slot_free = items[m]
                        ps, free = full(act, *key)
                        slot_free()
                        act.activation(dst, ps, ACT.Copy).then_inc(free, 1)
                        drained(act, *key)
                        if m >= 2:
                            act.wait_ge(sums, m - 1)
                        act.activation(sq[:, m % 2, :], dst, ACT.Square).then_inc(sqs, 1)
                    if m:
                        act.wait_ge(sums, m)
                        s = (m - 1) % 2
                        link(act, act.activation(hn_rs[:, s, 0:heads], hn_ss[:, s, 0:heads], ACT.Ln,
                                                 scale=1.0 / width, bias=eps_sb), act_step)
                        act.activation(hn_rs[:, s, 0:heads], hn_rs[:, s, 0:heads], ACT.Exp, scale=-0.5)\
                           .then_inc(rstd, 1)

            def copy_out(dst, *key):
                ps, free = full(act, *key)
                n = 1
                for s in dst.shape[1:]:
                    n *= s
                if len(dst.shape) == 3:
                    ps = ps[0:dst.shape[0], 0:n].rearrange("p (a b) -> p a b", a=dst.shape[1])
                else:
                    ps = ps[0:dst.shape[0], 0:n]
                act.activation(dst, ps, ACT.Copy).then_inc(free, 1)

            act.wait_ge(c_in, 16 * 7)
            norm_stats("mix", lambda t: act.wait_ge(x_in_s, 16 if t == 0 else 32) if t else act.wait_ge(x_in_s, 32))
            nothing = lambda: None
            head_norm("qk", [(("z", u, t), (q_tm, k_tm)[u][:, t, :], nothing) for u in range(2) for t in range(NT)], 8, 64)
            for u, dst in ((2, v_tm), (3, qk_tm), (4, vg)):
                for t in range(NT):
                    copy_out(dst[:, t, :], "z", u, t)
            for t in range(NT):
                ps, free = full(act, "z", 5, t)
                link(act, act.activation(rr[:, t, :], ps, ACT.Copy), act_step)
                if t >= 2:
                    act.wait_ge(r_silu, t - 1)
                act.activation(er[:, t % 2, :], ps, ACT.Exp, scale=-1.0).then_inc(free, 1)
            act.wait_ge(zero_s, 1)
            for i in range(2):
                copy_out(glT[0:16, 320 * i:320 * i + 320], "gl", i)
            norm_stats("mem", lambda t: act.wait_ge(mem_in_s[t], 16))
            def mk_free():
                act.wait_ge(nrm["mem"][1], 2)
            head_norm("mk", [(("m", u, t), mk_tm[:, t, (u - 6) * 512:(u - 5) * 512], mk_free)
                             for u in range(6, 8) for t in range(2)], 2, 256)
            for u in range(8, 10):
                for t in range(2):
                    copy_out(mv_tm[:, t, (u - 8) * 512:(u - 7) * 512], "m", u, t)
            for t in range(NT):
                for which, dst in (("q", qT), ("k", kT)):
                    copy_out(dst[:, :, t * P:(t + 1) * P], which + "T", t)
            for t in range(2):
                for g in range(2):
                    copy_out(mkT[:, 4 * g:4 * g + 4, t * P:(t + 1) * P], "mkT", t, g)
            act.wait_ge(outs["mk"], 16)
            def gate(t):
                ps, free = full(act, "z2", t)
                s = t % 2
                if t >= 2:
                    full(act, "cum", t - 2)
                act.activation(zz[:, s, :], ps[:, 0:256], ACT.Copy).then_inc(free, 1)
                drained(act, "z2", t)
                link(act, act.activation(ll[:, s, :], zz[:, s, :], ACT.Abs), act_step)
                link(act, act.activation(ll[:, s, :], ll[:, s, :], ACT.Exp, scale=-1.0), act_step)
                act.activation(ll[:, s, :], ll[:, s, :], ACT.Ln, bias=1.0).then_inc(g_l, 1)

            gate(0)
            for t in range(NT):
                W = 130 if t < PT_TILES else 136
                if t + 1 < NT:
                    gate(t + 1)
                ps, free = full(act, "cum", t)
                psv = ps.rearrange("p (a b) -> p a b", a=2)
                link(act, act.activation(eplus[:, t % 2, :, 0:W], psv[:, :, 0:W], ACT.Exp), act_step)
                if t:
                    act.wait_ge(g_hat, t)
                act.activation(eminus, psv[:, :, 0:P], ACT.Exp, scale=-1.0).then_inc(free, 1)
                copy_out(kh_tm[:, t % 2, :], "kh", t)
                sqs, sums, rstd, done = hn["gla"]
                if t >= 2:
                    full(act, "ogT", t - 2)
                if t == 0:
                    act.wait_ge(r_silu, NT)
                for par in range(2):
                    ps, free = full(act, "go", t, par)
                    act.activation(og[:, t % 2, :].rearrange("p (g par d) -> p g par d", g=2, par=2)[:, :, par, :],
                                   ps[:, 0:256].rearrange("p (g d) -> p g d", g=2), ACT.Copy).then_inc(free, 1)
                for par in range(2):
                    drained(act, "go", t, par)
                act.activation(sq[:, t % 2, :], og[:, t % 2, :], ACT.Square).then_inc(sqs, 1)
                act.wait_ge(sums, t + 1)
                link(act, act.activation(hn_rs[:, t % 2, 0:4], hn_ss[:, t % 2, 0:4], ACT.Ln, scale=1.0 / GV,
                                         bias=eps_sb), act_step)
                act.activation(hn_rs[:, t % 2, 0:4], hn_rs[:, t % 2, 0:4], ACT.Exp, scale=-0.5).then_inc(rstd, 1)
                if t == 0:
                    act.wait_ge(kout_s, 16)
                if t:
                    copy_out(mixT[:, 4:8, (t - 1) * P:t * P], "ogT", t - 1)
            copy_out(mixT[:, 4:8, (NT - 1) * P:NT * P], "ogT", NT - 1)

            def softmax_exp(m):
                kind, a, qt = SMU[m]
                n = (qt + 1) * P if kind == "p" else NEWK
                act.wait_ge(sm["att"][0], m + 1)
                act.activation(S_sb[:, m % 2, 0:n], S_sb[:, m % 2, 0:n], ACT.Exp, bias=sm_nm[:, m % 2, 0:1],
                               accum_out=sm_sum[:, m % 2, 0:1]).then_inc(sm["att"][1], 1)

            def probs_out(m):
                kind, a, qt = SMU[m]
                if m >= 2:
                    full(act, "o", m - 2)
                copy_out(PT_sb[:, m % 2, 0:(qt + 1 if kind == "p" else 4), :], "PT", m)
                if kind == "s":
                    copy_out(PT_sb[0:DEC_T, m % 2, 4, :], "PT2", m)

            for m in range(len(SMU) + 2):
                if m < len(SMU):
                    softmax_exp(m)
                if m >= 2:
                    probs_out(m - 2)
            norm_stats("cross", lambda t: act.wait_ge(x_mix, 2 * t + 2))
            def cq_free():
                full(act, "w", 11, NT - 1)
            head_norm("cq", [(("cq", u, t), cq_tm[:, t, (u - 12) * 512:(u - 11) * 512], cq_free)
                             for u in range(12, 14) for t in range(NT)], 2, 256)
            for t in range(NT):
                for g in range(2):
                    copy_out(cqT[:, 4 * g:4 * g + 4, t * P:(t + 1) * P], "cqT", t, g)

            def x_exp(m):
                kind, a, qt = XU[m]
                ps, free = full(act, "xs", m)
                act.wait_ge(sm["xat"][0], m + 1)
                if m >= 2:
                    full(act, "xPT", m - 2)
                for i in range(2 if kind == "p" else 1):
                    ins = act.activation(S_sb[:, m % 2, i * NMEM:(i + 1) * NMEM], ps[:, i * NMEM:(i + 1) * NMEM],
                                         ACT.Exp, bias=sm_nm[:, m % 2, i:i + 1], scale=1.0 / 16,
                                         accum_out=sm_sum[:, m % 2, i:i + 1])
                    if kind == "p" and i == 0:
                        link(act, ins, act_step)
                ins.then_inc(free, 1)

            for m in range(len(XU) + 2):
                if m < len(XU):
                    x_exp(m)
                if m >= 2:
                    if m >= 4:
                        full(act, "xo", m - 4)
                    copy_out(PT_sb[:, m % 2, 0:(4 if XU[m - 2][0] == "p" else 2), :], "xPT", m - 2)
            norm_stats("ffn", lambda t: act.wait_ge(x_cross, 2 * t + 2))
            for u in range(16, 20):
                for j in range(4):
                    for i in range(2):
                        if u >= 18 and j == 0 and i == 0:
                            full(act, "sc", u - 2, NT - 1)
                        copy_out(qry[:, 4 * (u % 2) + j, 320 * i:320 * i + 320], "pq", u, j, i)

            def v_high(k, par, B, early=False):
                act.wait_ge(v_in[k], B * 16 + 16)
                if not early:
                    act.wait_ge(y_mm, B * (2 * NT) - 2 * NT)
                act.activation(v16[:, EB * par + k, 0, :], vst[:, k, :], ACT.Copy).then_inc(v_hi, 1)

            def gelu(k, n):
                act.activation(gel[:, k % 2, :].rearrange("p (i t) -> p i t", i=2),
                               PS[:, 2 * (k % 2):2 * (k % 2) + 2, 0:320], ACT.Gelu, scale=1.0 / USCALE)\
                   .then_inc(z_ge, 1)

            def gated_high(k, par, n):
                act.wait_ge(a_mul, n + 1)
                act.activation(a16[:, EB * par + k, 0, :], a32[:, k % 2, :], ACT.Copy).then_inc(a_hi, 1)

            for k in range(EB):
                act.wait_ge(u_in[k], 16)
                act.activation(u16[:, k, 0, :, :], ust[:, k, :, :], ACT.Copy, scale=USCALE).then_inc(u_hi0, 1)
                act.wait_ge(u_hi0, k + 1)
                act.activation(ust[:, k, :, :], ust[:, k, :, :], ACT.Copy, scale=USCALE).then_inc(u_hi, 1)

            def early_tile(k, n, stored):
                act.wait_ge(z_mm, n + 1)
                if stored is not None:
                    act.wait_ge(gst[k % 2], stored)
                gelu(k, n)
                act.wait_ge(u_in[k % 4], n * 4 + (32 - 4 * (k % 4)))
                act.activation(u16[:, k % 4, 0, :, :], ust[:, k % 4, :, :], ACT.Copy, scale=USCALE).then_inc(u_hi0, 1)
                act.wait_ge(u_hi0, n + 5)
                act.activation(ust[:, k % 4, :, :], ust[:, k % 4, :, :], ACT.Copy, scale=USCALE).then_inc(u_hi, 1)

            for k in range(EB):
                early_tile(k, k, None if k < 2 else 16)
            act.sem_inc(wg_ev, CREDIT)
            with act.Fori(0, NT) as i:
                for k in range(12):
                    early_tile(k, i * 12 + (4 + k), i * 96 + (32 + 16 * (k // 2)))
                    if k == 3:
                        act.wait_ge(tk_exp_in, i + 1)
                        act.activation(sg, sg, ACT.Exp).then_inc(tk_exp, 1)
                    if k >= 4:
                        j = k - 4
                        if j % 2 == 0:
                            act.wait_ge(wst_s[(j // 2) % 2], i * 32 + (CREDIT + 16 * (j // 4)))
                        for q in range(4):
                            act.wait_ge(wg_mm, i * 32 + (4 * j + q + 1))
                            c = OHB * (j % 2) + 4 * q
                            act.activation(stage[:, (j // 2) % 2, :, c:c + 4].rearrange("p e t -> p t e"),
                                           PS[:, 4 + q, :].rearrange("p (t e) -> p t e", t=4), ACT.Copy,
                                           scale=1.0 / USCALE).then_inc(wg_ev, 1)

            def y_steps(par, B, early=False):
                for k in range(EB):
                    v_high(k, par, B, early)
                    gated_high(k, par, B * EB + k)

            def zy_steps(par, B):
                for k in range(EB):
                    v_high(k, par, B)
                    act.wait_ge(z_mm, B * EB + (k + 1))
                    act.wait_ge(a_mul, B * EB + (k - 1))
                    gelu(k, B * EB + k)
                    gated_high(k, par, B * EB + k)

            def u_steps(B):
                for k in range(EB):
                    act.wait_ge(u_in[k], B * 16 + 16)
                    act.wait_ge(z_mm, B * EB + (k - 3))
                    act.activation(u16[:, k, 0, :, :], ust[:, k, :, :], ACT.Copy, scale=USCALE).then_inc(u_hi, 1)

            y_steps(0, 0, True)
            y_steps(1, 1, True)
            with act.Fori(0, AHEAD // 2 - 1) as i:
                for s in range(2):
                    y_steps(s, i * 2 + (2 + s))
            zy_steps(0, AHEAD)
            with act.Fori(0, (NBLK - AHEAD) // 2 - 1) as i:
                for s in range(2):
                    B = i * 2 + (AHEAD + 1 + s)
                    u_steps(B)
                    zy_steps(1 - s, B)
            u_steps(NBLK - 1)
            zy_steps(1, NBLK - 1)

        @block.vector
        def _(dve):
            link(dve, dve.memset(eps_sb, EPS), dve_step)
            dve.sem_inc(c_in, 16)

            def norm_scale(name):
                gi, n, src, dst = NORMS[name]
                for t in range(n + 1):
                    if t < n:
                        dve.wait_ge(nrm[name][0], t + 1)
                        dve.tensor_scalar(xn[:, t % 2, :], src(t), nrm_rs[:, t % 2, :], None, ALU.mult)\
                           .then_inc(nrm[name][1], 1)
                    if t:
                        for g in range(2):
                            ps, free = full(dve, "T" + name, t - 1, g)
                            ins = dve.tensor_tensor(dst(t - 1, g), ps.rearrange("p (a b) -> p a b", a=4),
                                                    gc_sb[:, gi, 4 * g:4 * g + 4].unsqueeze(2).to_broadcast([P, 4, P]),
                                                    ALU.mult)
                            ins.then_inc(free, 1)

            def head_norm(name, items, heads, width):
                sqs, sums, rstd, done = hn[name]
                for m in range(len(items) + 1):
                    if m < len(items):
                        dve.wait_ge(sqs, m + 1)
                        dve.tensor_reduce(hn_ss[:, m % 2, 0:heads],
                                          sq[:, m % 2, :].rearrange("p (h d) -> p h d", h=heads), AX.X, ALU.add)\
                           .then_inc(sums, 1)
                    if m:
                        dst, gain = items[m - 1]
                        v = dst.rearrange("p (h d) -> p h d", h=heads)
                        dve.wait_ge(rstd, m)
                        rs = hn_rs[:, (m - 1) % 2, 0:heads].unsqueeze(2).to_broadcast([P, heads, width])
                        link(dve, dve.tensor_tensor(v, v, rs, ALU.mult), dve_step)
                        dve.tensor_tensor(v, v, gain.unsqueeze(1).to_broadcast([P, heads, width]), ALU.mult)\
                           .then_inc(done, 1)

            norm_scale("mix")
            head_norm("qk", [((q_tm, k_tm)[u][:, t, :], (gq, gk)[u]) for u in range(2) for t in range(NT)], 8, 64)
            for t in range(NT):
                drained(dve, "z", 5, t)
                s = t % 2
                link(dve, dve.tensor_scalar(er[:, s, :], er[:, s, :], 1.0, None, ALU.add), dve_step)
                link(dve, dve.reciprocal(er[:, s, :], er[:, s, :]), dve_step)
                dve.tensor_tensor(rr[:, t, :], rr[:, t, :], er[:, s, :], ALU.mult).then_inc(r_silu, 1)
            full(dve, "gl", 1)
            dve.memset(glT, 1.0).then_inc(zero_s, 1)
            norm_scale("mem")
            head_norm("mk", [(mk_tm[:, t, (u - 6) * 512:(u - 5) * 512], gck) for u in range(6, 8) for t in range(2)],
                      2, 256)
            dve.wait_ge(outs["mk"], 16)
            full(dve, "mkT", 1, 1)
            link(dve, dve.memset(QZ, 0.0), dve_step)
            link(dve, dve.memset(S_p, 0.0), dve_step)

            def gate(t):
                dve.wait_ge(g_l, t + 1)
                s = t % 2
                dve.scalar_tensor_tensor(out=zz[:, s, :], in0=zz[:, s, :], scalar=0.0, in1=ll[:, s, :],
                                         op0=ALU.min, op1=ALU.subtract).then_inc(g_la, 1)

            def scaled(dst, src, t, col, inc):
                for p in range(2):
                    ins = dve.tensor_scalar(dst[:, p, :], src[:, p, :], eplus[:, t % 2, p, col:col + 1], None, ALU.mult)
                    if p == 0:
                        ins.then_inc(dve_step, 1)
                        count[id(dve_step)] += 1
                ins.then_inc(inc, 1)

            gate(0)
            for t in range(NT):
                s = t % 2
                if t + 1 < NT:
                    gate(t + 1)
                ps, free = full(dve, "gT", t)
                psv = ps.rearrange("p (a b) -> p a b", a=4)
                drained(dve, "cum", t)
                link(dve, dve.scalar_tensor_tensor(out=hats[:, s, 0:2, :], in0=psv[:, 0:2, :], scalar=GK ** -0.5,
                                                   in1=eplus[:, s, :, 0:P], op0=ALU.mult, op1=ALU.mult), dve_step)
                dve.tensor_tensor(hats[:, s, 2:4, :], psv[:, 2:4, :], eminus, ALU.mult).then_inc(free, 1)
                drained(dve, "gT", t)
                if t == NT - 1:
                    for b in range(DEC_B):
                        link(dve, dve.tensor_copy(QZ[:, :, b, DEC_T * b:DEC_T * (b + 1)],
                                                  hats[:, s, 0:2, DEC_T * b:DEC_T * (b + 1)]), dve_step)
                dve.sem_inc(g_hat, 1)
                mask = maskp if t < PT_TILES else masks
                if t:
                    full(dve, "go", t - 1, 1)
                for par in range(2):
                    ps, free = full(dve, "A", t, par)
                    dve.tensor_tensor(ATm[:, par], ps[:, 0:256].rearrange("p (h t) -> p h t", h=2),
                                      mask.unsqueeze(1).to_broadcast([P, 2, P]), ALU.mult).then_inc(free, 1)
                if t < PT_TILES:
                    for c in range(2):
                        scaled(smid_p[:, 2 * s + c], S_p, t, P + c, g_smid)
                        dve.wait_ge(g_smid, 2 * t + c + 1)
                        ps, free = full(dve, "KV", t, c)
                        dve.tensor_tensor(S_p, smid_p[:, 2 * s + c], ps[:, 0:256].rearrange("p (a b) -> p a b", a=2),
                                          ALU.add).then_inc(free, 1)
                        drained(dve, "KV", t, c)
                        scaled(S_p, S_p, t, 64 * c + 63, g_st)
                        dve.wait_ge(g_st, 2 * t + c + 1)
                else:
                    drained(dve, "kh", t)
                    dve.tensor_tensor(khm, kh_tm[:, s, :].unsqueeze(1).to_broadcast([P, DEC_B, 256]),
                                      bmask.unsqueeze(2).to_broadcast([P, DEC_B, 256]), ALU.mult).then_inc(g_khm, 1)
                    dve.wait_ge(st_s_s, 16)
                    for p in range(2):
                        ins = dve.tensor_tensor(smid_s[:, :, p, :], st_s[:, :, p, :],
                                                eplus[:, s, p, P:P + 8].unsqueeze(2).to_broadcast([P, DEC_B, P]),
                                                ALU.mult)
                        if p == 0:
                            link(dve, ins, dve_step)
                    ins.then_inc(g_smid, 1)
                    dve.wait_ge(g_smid, 2 * t + 1)
                    for c in range(4):
                        ps, free = full(dve, "KV", t, c)
                        dve.tensor_tensor(st_s[:, 2 * c:2 * c + 2, :, :].rearrange("p b g v -> p (b g v)"),
                                          smid_s[:, 2 * c:2 * c + 2, :, :].rearrange("p b g v -> p (b g v)"),
                                          ps, ALU.add).then_inc(free, 1)
                        drained(dve, "KV", t, c)
                        for i in range(2):
                            for p in range(2):
                                b = 2 * c + i
                                ins = dve.tensor_scalar(st_s[:, b, p, :], st_s[:, b, p, :],
                                                        eplus[:, s, p, DEC_T * b + 15:DEC_T * b + 16], None, ALU.mult)
                                if i + p < 2:
                                    link(dve, ins, dve_step)
                        ins.then_inc(g_st, 1)
                sqs, sums, rstd, done = hn["gla"]
                dve.wait_ge(sqs, t + 1)
                dve.tensor_reduce(hn_ss[:, s, 0:4], sq[:, s, :].rearrange("p (h d) -> p h d", h=GH), AX.X, ALU.add)\
                   .then_inc(sums, 1)
                v = og[:, s, :].rearrange("p (h d) -> p h d", h=GH)
                dve.wait_ge(rstd, t + 1)
                link(dve, dve.tensor_tensor(v, v, hn_rs[:, s, 0:4].unsqueeze(2).to_broadcast([P, GH, GV]), ALU.mult),
                     dve_step)
                link(dve, dve.tensor_tensor(v, v, ggla.unsqueeze(1).to_broadcast([P, GH, GV]), ALU.mult), dve_step)
                dve.tensor_tensor(og[:, s, :], og[:, s, :], rr[:, t, :], ALU.mult).then_inc(done, 1)

            full(dve, "ogT", NT - 1)
            for t in range(NT):
                drained(dve, "qT", t)
            link(dve, dve.memset(QB, 0.0), dve_step)
            for o in (0, 64):
                ins = dve.tensor_copy(QB[o:o + 64, :, :, o // 4:o // 4 + DEC_T],
                                      qT[o:o + 64, :, SEQ:T].rearrange("p c (b t) -> p c b t", b=DEC_B))
                if o == 0:
                    link(dve, ins, dve_step)
            ins.then_inc(qb_s, 1)

            def att_max(m):
                kind, a, qt = SMU[m]
                s = m % 2
                if m >= 2:
                    full(dve, "PT" if SMU[m - 2][0] == "p" else "PT2", m - 2)
                ps, free = full(dve, "s", m)
                if kind == "p":
                    n = (qt + 1) * P
                    slot = bias_use[m] % BSLOTS
                    dve.wait_ge(bias_s_[slot], 16 * (bias_use[m] // BSLOTS + 1))
                    dve.scalar_tensor_tensor(out=S_sb[:, s, 0:n], in0=ps[:, 0:n], scalar=AD ** -0.5,
                                             in1=bias_ring[:, slot, 512 - n:512], op0=ALU.mult, op1=ALU.add)\
                       .then_inc(free, 1)
                    drained(dve, "s", m)
                else:
                    n = NEWK
                    dve.scalar_tensor_tensor(out=S_sb[:, s, 0:BANDK], in0=ps, scalar=AD ** -0.5,
                                             in1=bs_sb[:, 0:BANDK], op0=ALU.mult, op1=ALU.add).then_inc(free, 1)
                    ps, free = full(dve, "s2", m)
                    dve.scalar_tensor_tensor(out=S_sb[:, s, BANDK:NEWK], in0=ps[:, 0:DEC_T], scalar=AD ** -0.5,
                                             in1=bs_sb[:, BANDK:NEWK], op0=ALU.mult, op1=ALU.add).then_inc(free, 1)
                    drained(dve, "s", m)
                    drained(dve, "s2", m)
                dve.tensor_reduce(sm_nm[:, s, 0:1], S_sb[:, s, 0:n], AX.X, ALU.max, negate=True)\
                   .then_inc(sm["att"][0], 1)

            def att_norm(m):
                kind, a, qt = SMU[m]
                n = (qt + 1) * P if kind == "p" else NEWK
                s = m % 2
                dve.wait_ge(sm["att"][1], m + 1)
                link(dve, dve.reciprocal(sm_inv[:, s, 0:1], sm_sum[:, s, 0:1]), dve_step)
                dve.tensor_scalar(S_sb[:, s, 0:n], S_sb[:, s, 0:n], sm_inv[:, s, 0:1], None, ALU.mult)\
                   .then_inc(sm["att"][2], 1)

            def att_out(m):
                kind, a, qt = SMU[m]
                ps, free = full(dve, "o", m)
                if kind == "p":
                    o = 64 * (a % 2)
                    dve.tensor_copy(mixT[o:o + 64, a // 2, qt * P:(qt + 1) * P], ps[o:o + 64, 0:P]).then_inc(free, 1)
                else:
                    dve.tensor_copy(mixT[:, 0:4, SEQ + DEC_T * a:SEQ + DEC_T * (a + 1)],
                                    ps[:, 0:64].rearrange("p (c t) -> p c t", c=4)).then_inc(free, 1)

            for m in range(len(SMU) + 3):
                if m < len(SMU):
                    att_max(m)
                if 1 <= m < len(SMU) + 1:
                    att_norm(m - 1)
                if m >= 3:
                    att_out(m - 3)

            def residual(name, u0, ready):
                for t in range(NT):
                    for u in (u0, u0 + 1):
                        ps, free = full(dve, name, u, t)
                        c = (u - u0) * 512
                        ins = dve.tensor_tensor(X[:, t, c:c + 512], X[:, t, c:c + 512], ps, ALU.add)
                        ins.then_inc(free, 1)
                        drained(dve, name, u, t)
                        dve.sem_inc(ready, 1)

            residual("w", 10, x_mix)
            norm_scale("cross")
            head_norm("cq", [(cq_tm[:, t, (u - 12) * 512:(u - 11) * 512], gcq) for u in range(12, 14) for t in range(NT)],
                      2, 256)
            for g in range(2):
                drained(dve, "cqT", NT - 1, g)
            link(dve, dve.memset(QX, 0.0), dve_step)
            dve.tensor_copy(QX[:, :, :, 0:DEC_T], cqT[:, :, SEQ:T].rearrange("p c (b t) -> p c b t", b=DEC_B))\
               .then_inc(qx_s, 1)

            def x_max(m):
                kind, a, qt = XU[m]
                ps, _ = full(dve, "xs", m)
                h = 2 if kind == "p" else 1
                s = m % 2
                link(dve, dve.tensor_reduce(sm_max[:, s, 0:h], ps[:, 0:h * NMEM].rearrange("p (h k) -> p h k", h=h),
                                            AX.X, ALU.max), dve_step)
                dve.tensor_scalar(sm_nm[:, s, 0:h], sm_max[:, s, 0:h], -1.0 / 16, None, ALU.mult)\
                   .then_inc(sm["xat"][0], 1)

            def x_norm(m):
                kind, a, qt = XU[m]
                h = 2 if kind == "p" else 1
                s = m % 2
                drained(dve, "xs", m)
                link(dve, dve.reciprocal(sm_inv[:, s, 0:h], sm_sum[:, s, 0:h]), dve_step)
                v = S_sb[:, s, 0:h * NMEM].rearrange("p (h k) -> p h k", h=h)
                dve.tensor_tensor(v, v, sm_inv[:, s, 0:h].unsqueeze(2).to_broadcast([P, h, NMEM]), ALU.mult)\
                   .then_inc(sm["xat"][2], 1)

            def x_out(m):
                kind, a, qt = XU[m]
                ps, free = full(dve, "xo", m)
                if kind == "p":
                    dve.tensor_copy(hT[:, 4 * a:4 * a + 4, qt * P:(qt + 1) * P], ps.rearrange("p (c t) -> p c t", c=4))\
                       .then_inc(free, 1)
                else:
                    dve.tensor_copy(hT[:, :, SEQ + DEC_T * a:SEQ + DEC_T * (a + 1)],
                                    ps[:, 0:P].rearrange("p (c t) -> p c t", c=8)).then_inc(free, 1)

            for m in range(len(XU) + 3):
                if m < len(XU):
                    x_max(m)
                if 1 <= m < len(XU) + 1:
                    x_norm(m - 1)
                if m >= 3:
                    x_out(m - 3)
            residual("co", 14, x_cross)
            norm_scale("ffn")
            for t in range(NT):
                c = slice(t * P, (t + 1) * P)
                for g in range(2):
                    drained(dve, "Tffn", t, g)
                link(dve, dve.tensor_copy(hhi[:, :, c], hT[:, :, c]), dve_step)
                dve.tensor_tensor(hlo[:, :, c], hT[:, :, c], hhi[:, :, c], ALU.subtract).then_inc(h_split, 1)

            dve.tensor_copy(iota16, iota.unsqueeze(2).to_broadcast([P, NK, OHB]))

            def top16(vals, idx, src, n):
                link(dve, dve.max(vals[:, 0:8], src), dve_step)
                dve.max_index(idx[:, 0:8], vals[:, 0:8], src)
                link(dve, dve.match_replace(srep[:, 0:n], vals[:, 0:8], src, NEG), dve_step)
                link(dve, dve.max(vals[:, 8:16], srep[:, 0:n]), dve_step)
                link(dve, dve.max_index(idx[:, 8:16], vals[:, 8:16], srep[:, 0:n]), dve_step)

            for u in range(16, 20):
                for t in range(NT):
                    ps, free = full(dve, "sc", u, t)
                    dve.tensor_copy(s_ring[:, u % 2, t, :], ps).then_inc(free, 1)
                    drained(dve, "sc", u, t)
                for t in range(NT):
                    for j in range(4):
                        jj = 4 * (u - 16) + j
                        top16(top_v[:, t, jj, :], top_i[:, t, jj * TOPK:(jj + 1) * TOPK],
                              s_ring[:, u % 2, t, j * NK:(j + 1) * NK], NK)
            for t in range(NT):
                v = top_v[:, t].rearrange("p (h two) k -> p h two k", two=2)
                for h in range(PH):
                    link(dve, dve.tensor_tensor(cand[:, h, :].rearrange("p (a b) -> p a b", a=TOPK),
                                                v[:, h, 0, :].unsqueeze(2).to_broadcast([P, TOPK, TOPK]),
                                                v[:, h, 1, :].unsqueeze(1).to_broadcast([P, TOPK, TOPK]), ALU.add),
                         dve_step)
                for h in range(PH):
                    top16(ts[:, h, :], tp[:, h * TOPK:(h + 1) * TOPK], cand[:, h, :], 256)
                link(dve, dve.tensor_tensor(sg.rearrange("p (h k) -> p h k", h=PH), ts,
                                            ts[:, :, 0:1].to_broadcast([P, PH, TOPK]), ALU.subtract), dve_step)
                dve.sem_inc(tk_exp_in, 1)
                link(dve, dve.tensor_scalar(ji[:, 0, :], tp, 4, None, ALU.logical_shift_right), dve_step)
                link(dve, dve.tensor_scalar(ji[:, 1, :], tp, 15, None, ALU.bitwise_and), dve_step)
                link(dve, dve.tensor_copy(jf, ji), dve_step)
                for half in range(2):
                    link(dve, dve.tensor_copy(topif[:, half], top_i[:, t, :].rearrange(
                        "p (h two k) -> p h two k", two=2, k=TOPK)[:, :, half, :]), dve_step)
                for half in range(2):
                    link(dve, dve.tensor_tensor(eq, jf[:, half, :].unsqueeze(2).to_broadcast([P, P, TOPK]),
                                                iota[:, 0:TOPK].unsqueeze(1).to_broadcast([P, P, TOPK]), ALU.is_equal),
                         dve_step)
                    e4 = eq.rearrange("p (h k) j -> p h k j", h=PH)
                    link(dve, dve.tensor_tensor(e4, e4, topif[:, half].unsqueeze(2).to_broadcast([P, PH, TOPK, TOPK]),
                                                ALU.mult), dve_step)
                    link(dve, dve.tensor_reduce(jf[:, half, :], eq, AX.X, ALU.add), dve_step)
                dve.wait_ge(tk_exp, t + 1)
                g = sg.rearrange("p (h k) -> p h k", h=PH)
                link(dve, dve.tensor_reduce(gsum, g, AX.X, ALU.add), dve_step)
                link(dve, dve.reciprocal(gsum, gsum), dve_step)
                dve.tensor_tensor(g, g, gsum.unsqueeze(2).to_broadcast([P, PH, TOPK]), ALU.mult).then_inc(tk_done, 1)
                dve.wait_ge(sel_mm, t + 1)
                c = slice(t * P, (t + 1) * P)
                link(dve, dve.tensor_scalar(sel16[:, 0, c], PS[:, 4, 0:P], USCALE, None, ALU.mult), dve_step)
                link(dve, dve.scalar_tensor_tensor(out=sel16[:, 1, c], in0=PS[:, 4, 0:P], scalar=USCALE,
                                                   in1=sel16[:, 0, c], op0=ALU.mult, op1=ALU.subtract), dve_step)
                link(dve, dve.tensor_copy(sel16[:, 2:4, c], PS[:, 4, P:3 * P].rearrange("p (a b) -> p a b", a=2)),
                     dve_step)
                for j in range(P // OHB):
                    n = t * (P // OHB) + j
                    if n >= 2:
                        dve.wait_ge(wg_mm, 4 * (n - 1))

                    def col(x):
                        return sel16[:, x, t * P + OHB * j:t * P + OHB * (j + 1)].unsqueeze(1)\
                            .to_broadcast([P, NK, OHB])

                    link(dve, dve.tensor_tensor(eqa, iota16, col(2), ALU.is_equal), dve_step)
                    dve.tensor_tensor(oh[:, n % 2, 2], iota16, col(3), ALU.is_equal).then_inc(dve_step, 1)
                    dve.tensor_tensor(oh[:, n % 2, 0], eqa, col(0), ALU.mult).then_inc(dve_step, 1)
                    count[id(dve_step)] += 2
                    link(dve, dve.tensor_tensor(oh[:, n % 2, 1], eqa, col(1), ALU.mult), dve_step)
                    dve.sem_inc(oh_s, 1)

            def u_low(k, n):
                dve.wait_ge(u_hi, n + 1)
                dve.scalar_tensor_tensor(out=u16[:, k, 1, :, :], in0=ust[:, k, :, :], scalar=USCALE,
                                         in1=u16[:, k, 0, :, :], op0=ALU.mult, op1=ALU.subtract).then_inc(u_sp, 1)

            def v_low(k, par, n):
                dve.wait_ge(v_hi, n + 1)
                dve.tensor_tensor(v16[:, EB * par + k, 1, :], vst[:, k, :], v16[:, EB * par + k, 0, :],
                                  ALU.subtract).then_inc(v_sp, 1)

            def gated(k, par, n):
                dve.tensor_tensor(a32[:, k % 2, :].rearrange("p (g t) -> p g t", g=NTG),
                                  gel[:, k % 2, :].rearrange("p (g t) -> p g t", g=NTG), W_sb[:, par, :, k, :],
                                  ALU.mult).then_inc(a_mul, 1)
                dve.wait_ge(a_hi, n + 1)
                dve.tensor_tensor(a16[:, EB * par + k, 1, :], a32[:, k % 2, :], a16[:, EB * par + k, 0, :],
                                  ALU.subtract).then_inc(a_sp, 1)

            def y_tile(par, B, k):
                v_low(k, par, B * EB + k)
                if k == 0:
                    dve.wait_ge(W_in[par], B * 8 + (16 - 8 * par))
                dve.wait_ge(g_in[k % 2], B * 32 + (16 * (k // 2) + 16))
                gated(k, par, B * EB + k)

            def zy_tiles(par, B):
                for k in range(EB):
                    v_low(k, par, B * EB + k)
                    dve.wait_ge(z_ge, B * EB + (k + 1))
                    if k == 0:
                        dve.wait_ge(W_in[par], B * 8 + (16 - 8 * par))
                    gated(k, par, B * EB + k)

            def y_add(par, B, g):
                t, half = g // 2, g % 2
                dve.wait_ge(y_mm, B * (2 * NT) + (g + 1))
                c = slice(half * 512, half * 512 + 512)
                dve.tensor_tensor(X[:, t, c], X[:, t, c], PS[:, 4 + (par * 2 * NT + g) % 4, :], ALU.add)\
                   .then_inc(y_ev, 1)

            def y_pass(par, B):
                for g in range(2 * NT):
                    if g % 2 == 0 and g < 2 * EB:
                        y_tile(1 - par, B + 1, g // 2)
                    y_add(par, B, g)

            def zy_pass(par, B):
                for g in range(2 * NT):
                    if g % 2 == 0 and g < 2 * EB:
                        u_low(g // 2, B * EB + (2 * EB + g // 2))
                    y_add(par, B, g)
                zy_tiles(par, B + 2)

            for k in range(EB):
                y_tile(0, 0, k)
            y_pass(0, 0)
            with dve.Fori(0, AHEAD // 2 - 1) as i:
                for s in range(2):
                    y_pass(1 - s, i * 2 + (1 + s))
            zy_tiles(0, AHEAD)
            with dve.Fori(0, (NBLK - AHEAD) // 2 - 1) as i:
                for s in range(2):
                    zy_pass(1 - s, i * 2 + (AHEAD - 1 + s))
            zy_pass(1, NBLK - 3)
            for B in (NBLK - 2, NBLK - 1):
                for g in range(2 * NT):
                    y_add(B % 2, B, g)


def kernel(**inputs):
    import numpy as np
    import concourse.bacc as _bacc
    from concourse import mybir as _mybir
    from concourse.bass_utils import run_bass_kernel_spmd as _run

    a = {k: np.asarray(v) for k, v in inputs.items()}
    f = np.float32
    x = np.concatenate([a["x_prompt"][0], a["x_sample"].reshape(128, 1024)], axis=0)
    w_in = a["w_in"][0]
    q, m = np.arange(128)[:, None], np.arange(512)[None, :]
    rb = a["rel_bias"][0]
    bias_p = rb[:, np.clip(q + 384 - m, -128, 128) + 128]
    blocked = np.broadcast_to((q < 64) & (m >= 448), bias_p.shape)
    bias_p = np.where(blocked, f(-1e30), bias_p).astype(f)
    i, j = np.arange(16)[:, None], np.arange(528)[None, :]
    bias_s = rb[:, np.clip(512 + i - j, -128, 128) + 128].reshape(128, 528)
    kc = a["cache_att_k"][0][:, 64:].reshape(8, 512, 4, 128).transpose(0, 3, 2, 1)
    vc = a["cache_att_v"][0][:, 64:].reshape(8, 4, 128, 512).transpose(0, 2, 1, 3)
    mkc = a["cache_mem_k"][0].reshape(8, 256, 8, 128).transpose(0, 3, 2, 1)
    mvc = a["cache_mem_v"][0].reshape(8, 2, 128, 1024).transpose(0, 2, 1, 3)
    state = a["state_gla"][0].reshape(8, 2, 128, 128)
    u_t = a["expert_u"][0].reshape(128, 128, 8, 128).transpose(1, 3, 2, 0).reshape(128, 128, 1024)
    v_t = a["expert_v"][0].reshape(128, 128, 1024).transpose(1, 0, 2)
    gcols = np.stack([a[n][0].reshape(8, 128).T for n in ("g_mix", "g_mem", "g_cross", "g_ffn")], axis=1)
    grow = np.concatenate([a[n][0] for n in ("g_q", "g_k", "g_gla_out", "g_cq", "g_ck")])
    grows = np.broadcast_to(grow, (128, 768))
    wg2 = np.concatenate([a["w_gate2"][0], a["b_gate2"]], axis=0)
    keys = np.stack([a["sub_keys1"][0].T, a["sub_keys2"][0].T])
    s, t = np.arange(128)[:, None], np.arange(128)[None, :]

    def tri(L):
        same = (s // L) == (t // L)
        mid = (s // L) * L + L // 2 - 1
        centred = (same & (s <= t)).astype(f) - (same & (s <= mid)).astype(f)
        mids = ((s // L) == np.arange(128 // L)[None, :]).astype(f) * (s <= mid)
        return np.concatenate([centred, mids], axis=1) / 16.0

    def causal(L):
        return (((s // L) == (t // L)) & (s <= t)).astype(f)

    consts = np.concatenate([np.eye(128), np.broadcast_to(np.arange(128), (128, 128)), causal(64), causal(16),
                             tri(64), tri(16), (s // 16) == np.arange(8)[None, :]], axis=1).astype(f)
    arrays = {"x_in": x, "mem_in": a["mem_prompt"][0], "w_in": w_in, "w_gl": w_in[:, 2560:2576], "w_out": a["w_out"][0],
              "w_cq": a["w_cq"][0], "w_ck": a["w_ck"][0], "w_cv": a["w_cv"][0], "w_co": a["w_co"][0],
              "w_pq": a["w_pq"][0], "wg2": wg2, "gcols": gcols, "grows": grows, "bias_p": bias_p, "bias_s": bias_s,
              "kc_t": kc, "v_c": vc, "state_in": state, "mk_c": mkc, "mv_c": mvc, "keys_t": keys, "u_t": u_t,
              "v_t": v_t, "consts": consts}
    arrays = {k: np.ascontiguousarray(v) for k, v in arrays.items()}
    outs = {"y_out": (640, 1024), "k_out": (640, 512), "v_out": (640, 512), "gp_out": (2, 128, 128),
            "gs_out": (8, 2, 128, 128), "mk_out": (256, 1024), "mv_out": (256, 1024)}

    nc = _bacc.Bacc("TRN2", target_bir_lowering=False, num_devices=1)
    F = _mybir.dt.float32
    aps = {k: nc.dram_tensor(k, v.shape, F, kind="ExternalInput").ap() for k, v in arrays.items()}
    aps |= {k: nc.dram_tensor(k, v, F, kind="ExternalOutput").ap() for k, v in outs.items()}
    w_dram = nc.dram_tensor("w_dram", (NBLK, P, NTG, EB * TG), F).ap()
    g_dram = nc.dram_tensor("g_dram", (NA, P, T), F).ap()
    peer_stream_step(nc, w_dram=w_dram, g_dram=g_dram, **aps)
    r = _run(nc, [arrays], core_ids=[0]).results[0]
    y, k, v = r["y_out"], r["k_out"], r["v_out"]
    return (y[:512].reshape(1, 512, 1024), y[512:].reshape(8, 16, 1024),
            k[:512].reshape(1, 1, 512, 8, 64), v[:512].reshape(1, 1, 512, 8, 64),
            r["gp_out"].reshape(1, 1, 4, 64, 128),
            r["mk_out"].reshape(1, 1, 256, 4, 256), r["mv_out"].reshape(1, 1, 256, 4, 256),
            k[512:].reshape(1, 8, 16, 8, 64), v[512:].reshape(1, 8, 16, 8, 64),
            r["gs_out"].reshape(1, 8, 4, 64, 128))
```

```python
from contextlib import ExitStack

import concourse.bass as bass
from concourse import mybir

F32 = mybir.dt.float32
F16 = mybir.dt.float16
U32 = mybir.dt.uint32
ALU = mybir.AluOpType
ACT = mybir.ActivationFunctionType
AX = mybir.AxisListType

P = 128
D = 1024
KT = D // P
SEQ, DEC_B, DEC_T = 512, 8, 16
T = SEQ + DEC_B * DEC_T
NT = T // P
PT_TILES = SEQ // P
AH, AD = 8, 64
GH, GK, GV = 4, 64, 128
BANDK = 512
NEWK = BANDK + DEC_T
XH, NMEM = 4, 256
NK = 128
TOPK = 16
PH = 8
EPS = 1e-6
UNIT = 512
WSLOTS = 2
PASSES = ((0, 0), (0, 1), (1, 0))
SM = 3
BSLOTS = 4
EB = 4
NBLK = NK // EB
TG = 32
NTG = T // TG
USCALE = 1024.0
OHB = 16
AHEAD = 20
NA = AHEAD * EB
TAIL = 2 * EB
LEAD = NA - 12 * NT - TAIL
NEG = -3.0e38
CREDIT = 16


def peer_stream_step(nc, x_in, mem_in, w_in, w_gl, w_out, w_cq, w_ck, w_cv, w_co, w_pq, wg2, gcols, grows,
                     bias_p, bias_s, kc_t, v_c, state_in, mk_c, mv_c, keys_t, u_t, v_t, consts,
                     y_out, k_out, v_out, gp_out, gs_out, mk_out, mv_out, w_dram, g_dram):
    ctx = ExitStack()
    with ctx:
        def sem(name):
            return ctx.enter_context(nc.semaphore(name))

        AR = ctx.enter_context(nc.sbuf_tensor("arena", [P, 53200], F32))
        PS = ctx.enter_context(nc.psum_tensor("banks", [P, 8, 512], F32))

        def at(off, *shape):
            n = 1
            for s in shape:
                n *= s
            v = AR[:, off:off + n]
            if len(shape) == 2:
                v = v.rearrange("p (a b) -> p a b", a=shape[0])
            elif len(shape) == 3:
                v = v.rearrange("p (a b c) -> p a b c", a=shape[0], b=shape[1])
            elif len(shape) == 4:
                v = v.rearrange("p (a b c d) -> p a b c d", a=shape[0], b=shape[1], c=shape[2])
            return v

        X = at(0, NT, D)
        CB = 5120
        ident = AR[:, CB:CB + 128]
        iota = AR[:, CB + 128:CB + 256]
        maskp = AR[:, CB + 256:CB + 384]
        masks = AR[:, CB + 384:CB + 512]
        trip = AR[:, CB + 512:CB + 642]
        tris = AR[:, CB + 642:CB + 778]
        bmask = AR[:, CB + 778:CB + 786]
        NCONST = 786
        gc_sb = at(CB + 786, 4, KT)
        gr_sb = AR[:, CB + 818:CB + 818 + 768]
        wg2_sb = AR[0:17, CB + 1586:CB + 1842]
        bs_sb = AR[:, CB + 1842:CB + 1842 + NEWK]
        eps_sb = AR[:, CB + 2370:CB + 2371]
        gq, gk, ggla = gr_sb[:, 0:64], gr_sb[:, 64:128], gr_sb[:, 128:256]
        gcq, gck = gr_sb[:, 256:512], gr_sb[:, 512:768]
        MM = 7500
        mv_tm = at(MM, 2, D)
        mkT = at(MM + 2048, 2 * XH, NMEM)
        BI = MM + 4096
        smid_p = at(BI, 4, 2, P)
        H16 = MM
        def halves(off, width):
            return AR[:, off:off + KT * width].bitcast(F16).rearrange("p (x k t) -> p x k t", x=2, k=KT)

        h16 = halves(H16, T)
        hhi, hlo = h16[:, 0], h16[:, 1]
        TA = 12620
        hT = halves(TA, T)
        memT = halves(TA, NMEM)
        mk_tm = at(TA + 2048, 2, D)
        glT = AR[0:17, TA + 4096:TA + 4096 + T]
        QZ = at(TA, 2, DEC_B, P)
        bias_ring = at(TA, BSLOTS, 512)
        zz = at(TA + 2048, NT, 256)
        eplus = at(TA + 3328, 2, 2, 136)
        eminus = at(TA + 4736, 2, P)
        TB = 17740
        q_tm = at(TB, NT, 512)
        k_tm = at(TB + 2560, NT, 512)
        mixT = halves(TB, T)
        cq_tm = at(TB, NT, D)
        qry = at(TB, 8, T)
        QX = at(TB, KT, DEC_B, 32)
        V5 = 22860
        v_tm = at(V5, NT, 512)
        sel16 = AR[:, V5:V5 + 1280].bitcast(F16).rearrange("p (x t) -> p x t", x=4)
        G3 = V5 + 2560
        qk_tm = at(G3, NT, 512)
        vg = at(G3 + 2560, NT, 512)
        rr = at(G3 + 5120, NT, 512)
        smid_s = at(G3, DEC_B, 2, P)
        st_s = at(G3 + 2560, DEC_B, 2, P)
        khm = at(G3 + 5120, DEC_B, 256)
        kc_ring = at(G3, 2, 4, 512)
        vc_ring = at(G3 + 4096, 2, 4, 512)
        mkc_ring = at(G3, 2, 2 * XH, NMEM)
        mvc_ring = at(G3 + 4096, 2, 2, D)
        s_ring = at(G3, 2, NT, 4 * NK)
        QK = G3 + 8192
        qT = at(QK, 4, T)
        kT = at(QK + 2560, 4, T)
        cqT = at(QK, KT, T)
        cand = at(QK, PH, 256)
        eq = AR[:, QK + 2048:QK + 3072].bitcast(F16).rearrange("p (a b) -> p a b", b=TOPK)
        jh = AR[:, QK + 3072:QK + 3200].bitcast(F16).rearrange("p (a b) -> p a b", a=2)
        place = AR[:, QK + 3200:QK + 3208].bitcast(F16)
        ts = at(QK + 4096, PH, TOPK)
        tp = AR[:, QK + 4224:QK + 4352].bitcast(U32)
        jf = at(QK + 4352, 2, P)
        ji = at(QK + 4608, 2, P).bitcast(U32)
        WR = QK + 5120
        w16 = [AR[:, o:o + KT * UNIT].bitcast(F16).rearrange("p (x k n) -> p x k n", x=2, k=KT) for o in (WR, QK)]
        raw = at(WR + KT * UNIT, 2, KT // 2, UNIT)
        TM = WR + WSLOTS * 4096
        xn = at(TM, 2, D)
        junk = AR[:, TM + 2048:TM + 3072]
        er = at(TM + 3072, 2, 512)
        sq = at(TM + 4400, 2, 512)
        ATm = at(TM, 2, 2, P)
        kh_tm = at(TM + 1024, 2, 256)
        hats = at(TM + 2048, 2, 4, P)
        ll = at(TM + 2048, NT, 256)
        og = at(TM + 3072, 2, 512)
        S_sb = at(TM, SM, NEWK)
        PT_sb = at(TM + SM * NEWK, SM, 5, P)
        QB = at(BI, 4, DEC_B, 32)
        vn = at(TM + SM * (NEWK + 640), 2, 512)
        topif = AR[:, TM:TM + 128].bitcast(F16).rearrange("p (x h k) -> p x h k", x=2, h=PH)
        top_v = at(TM + 1280, NT, 2 * PH, TOPK)
        top_i = at(TM + 2560, NT, 2 * PH * TOPK).bitcast(U32)
        iota16 = AR[:, V5 + 1280:V5 + 2304].bitcast(F16).rearrange("p (i t) -> p i t", t=OHB)
        oh = AR[:, G3:G3 + 6144].bitcast(F16).rearrange("p (s x i t) -> p s x i t", s=2, x=3, t=OHB)
        eqa = AR[:, G3 + 6144:G3 + 7168].bitcast(F16).rearrange("p (i t) -> p i t", t=OHB)
        stage = at(WR, 2, NK, TG)
        wgl_sb = at(TM + 4096, KT, 16)
        wgl16 = AR[:, TM + 4224:TM + 4352].bitcast(F16).rearrange("p (x k n) -> p x k n", x=2, k=KT)
        sg = at(TM + 512, P)
        gsum = at(TM + 640, PH)
        srep = AR[:, TM + 1024:TM + 1280]
        keys_sb = at(TM + 4096, 2, NK)
        ST = TM + 5424
        hn_ss = at(ST, 2, 8)
        hn_rs = at(ST + 16, 2, 8)
        nrm_ss = at(ST + 32, 2, 1)
        nrm_rs = at(ST + 34, 2, 1)
        sm_nm = at(ST + 40, SM, 2)
        sm_sum = at(ST + 48, SM, 2)
        sm_inv = at(ST + 56, SM, 2)
        sm_max = at(ST + 64, SM, 2)
        S_p = at(TM + 6020, 2, P)
        R1, R2 = TA, G3 - 640
        ust = at(R1, 4, KT, P)
        u16 = AR[:, R1 + 4096:R1 + 8192].bitcast(F16).rearrange("p (s x k e) -> p s x k e", s=4, x=2, k=KT)
        gel = at(R1 + 8192, 2, T)
        vst = at(R2, 4, D)
        v16 = AR[:, R2 + 4096:R2 + 12288].bitcast(F16).rearrange("p (s x d) -> p s x d", s=2 * EB, x=2)
        a16 = AR[:, R2 + 12288:R2 + 17408].bitcast(F16).rearrange("p (s x t) -> p s x t", s=2 * EB, x=2)
        W_sb = at(R2 + 17408, 2, NTG, EB, TG)
        a32 = at(R2 + 22528, 2, T)
        gel_back = at(R2 + 22528 + 2 * T, 2, T)

        bank_full = [sem(f"bank_full{b}") for b in range(8)]
        bank_free = [sem(f"bank_free{b}") for b in range(8)]
        x_in_s = [sem("x_first_tile_loaded"), sem("x_rest_loaded")]
        c_in = sem("consts_loaded")
        gains_in = sem("gains_loaded")
        mem_in_s = [sem(f"mem_loaded{i}") for i in range(2)]
        w_in_s = [sem(f"weights_loaded{i}") for i in range(WSLOTS)]
        bias_s_ = [sem(f"bias_loaded{i}") for i in range(BSLOTS)]
        kc_s = [sem(f"cache_k_loaded{i}") for i in range(2)]
        vc_s = [sem(f"cache_v_loaded{i}") for i in range(2)]
        vn_s = [sem(f"newv_loaded{i}") for i in range(2)]
        mkc_s = [sem(f"memcache_k_loaded{i}") for i in range(2)]
        mvc_s = [sem(f"memcache_v_loaded{i}") for i in range(2)]
        st_s_s = sem("states_loaded")
        keys_s = sem("keys_loaded")
        outs = {n: sem(f"{n}_stored") for n in ("v", "mk", "mv", "gp", "gs")}
        kout_s = sem("k_stored")
        y_s = sem("y_stored")
        dve_step = sem("dve_step")
        act_step = sem("act_step")
        zero_s = sem("tiles_cleared")
        nrm = {n: (sem(f"{n}_rstd"), sem(f"{n}_scaled")) for n in ("mix", "mem", "cross", "ffn")}
        hn = {n: tuple(sem(f"{n}_{w}") for w in ("squares", "sums", "rstd", "normed")) for n in ("qk", "mk", "gla", "cq")}
        r_silu = sem("r_silu")
        g_l = sem("gate_log")
        g_la = sem("log_a")
        g_hat = sem("hats_ready")
        g_smid = sem("state_scaled")
        g_st = sem("state_updated")
        g_khm = sem("khat_masked")
        qb_s = sem("blockq_ready")
        sm = {n: tuple(sem(f"{n}_{w}") for w in ("max", "exp", "prob")) for n in ("att", "xat")}
        qx_s = sem("padded_q_ready")
        x_mix = sem("x_after_mix")
        x_cross = sem("x_after_cross")
        w_split = sem("weights_split")
        wgl_s = sem("gate_weights_split")
        og_hi = sem("gla_out_high")
        w_hi = sem("weights_high")
        tk_exp_in = sem("topk_shifted")
        tk_exp = sem("topk_exp")
        tk_done = sem("topk_selected")
        sel_mm = sem("choices_transposed")
        oh_s = sem("onehots_ready")
        gst = [sem(f"gelu_stored{i}") for i in range(2)]
        g_in = [sem(f"gelu_loaded{i}") for i in range(2)]
        wg_mm = sem("gate_mm_done")
        wg_ev = sem("gate_evacuated")
        wst_s = [sem(f"gate_stored{i}") for i in range(2)]
        u_in = [sem(f"u_loaded{i}") for i in range(4)]
        v_in = [sem(f"v_loaded{i}") for i in range(4)]
        W_in = [sem(f"gates_loaded{i}") for i in range(2)]
        u_hi_only = sem("u_high_before_scaling")
        u_hi = sem("u_high")
        u_sp = sem("u_split")
        v_hi = sem("v_high")
        v_sp = sem("v_split")
        z_mm = sem("z_done")
        z_ge = sem("gelu_done")
        a_mul = sem("act_gated")
        a_hi = sem("act_high")
        a_sp = sem("act_split")
        y_mm = sem("y_done")
        y_ev = sem("y_added")

        groups = {}
        uses = [0] * 8

        def open_group(pe, key):
            b = len(groups) % 8
            if uses[b]:
                pe.wait_ge(bank_free[b], uses[b])
            uses[b] += 1
            groups[key] = (b, uses[b])
            return PS[:, b, :], bank_full[b]

        def full(eng, *key):
            b, n = groups[key]
            eng.wait_ge(bank_full[b], n)
            return PS[:, b, :], bank_free[b]

        def drained(eng, *key):
            b, n = groups[key]
            eng.wait_ge(bank_free[b], n)

        count = {}

        def link(eng, ins, s):
            count[id(s)] = count.get(id(s), 0) + 1
            ins.then_inc(s, 1)
            eng.wait_ge(s, count[id(s)])

        UNITS = ([("in", w_in, c) for c in (0, 512, 1024, 1536, 2048, 2576)]
                 + [("ck", w_ck, c) for c in (0, 512)] + [("cv", w_cv, c) for c in (0, 512)]
                 + [("wo", w_out, c) for c in (0, 512)] + [("cq", w_cq, c) for c in (0, 512)]
                 + [("co", w_co, c) for c in (0, 512)] + [("pq", w_pq, c) for c in (0, 512, 1024, 1536)])
        unit_last = {}

        def spread(prompt):
            lead = len(prompt) // 4
            each = (len(prompt) - lead) // DEC_B
            order = prompt[:lead]
            for b in range(DEC_B):
                n = lead + b * each
                order += [("s", b, 0)] + prompt[n:(n + each if b + 1 < DEC_B else len(prompt))]
            return order

        SMU = spread([("p", h, qt) for qt in range(PT_TILES) for h in range(AH)])
        XU = spread([("p", hp, qt) for qt in range(PT_TILES) for hp in range(2)])
        bias_use = {m: n for n, m in enumerate(m for m, unit in enumerate(SMU) if unit[0] == "p")}

        NORMS = {"mix": (0, NT, lambda t: X[:, t, :], hT),
                 "mem": (1, 2, lambda t: mk_tm[:, t, :], memT),
                 "cross": (2, NT, lambda t: X[:, t, :], hT),
                 "ffn": (3, NT, lambda t: X[:, t, :], h16)}

        block = ctx.enter_context(nc.Block())

        @block.tensor
        def _(pe):
            def norm_transposes(name, *tiles):
                for t in tiles:
                    pe.wait_ge(nrm[name][1], t + 1)
                    for g in range(2):
                        ps, done = open_group(pe, ("T" + name, t, g))
                        for j in range(4):
                            mm = pe.transpose(ps[:, j * P:(j + 1) * P], xn[:, t % 2, (4 * g + j) * P:(4 * g + j + 1) * P],
                                              ident)
                        mm.then_inc(done, 1)

            def project(u, rows, name, t):
                pe.wait_ge(w_split, 2 * u + 2)
                ps, done = open_group(pe, (name, u, t))
                for k in range(KT):
                    for a, b in PASSES:
                        mm = pe.matmul(ps, rows[:, a, k, t * P:(t + 1) * P], w16[u % 2][:, b, k, :],
                                       start=(k == 0 and a + b == 0), stop=(k == KT - 1 and a == 1))
                mm.then_inc(done, 1)
                unit_last[u] = (name, u, t)

            def project_normed(u, rows, name, norm, t):
                for g in range(2):
                    drained(pe, "T" + norm, t, g)
                project(u, rows, name, t)

            pe.wait_ge(c_in, 16 * 3)
            norm_transposes("mix", 0)
            for t in range(NT):
                if t + 1 < NT:
                    norm_transposes("mix", t + 1)
                project_normed(0, hT, "z", "mix", t)
            for u in range(1, 6):
                for t in range(NT):
                    project(u, hT, "z", t)
            pe.wait_ge(wgl_s, 1)
            for i in range(2):
                ps, done = open_group(pe, ("gl", i))
                for k in range(KT):
                    for a, b in PASSES:
                        mm = pe.matmul(ps[0:16, 0:320], wgl16[:, a, k, :], hT[:, b, k, 320 * i:320 * i + 320],
                                       start=(k == 0 and a + b == 0), stop=(k == KT - 1 and a == 1))
                mm.then_inc(done, 1)
            norm_transposes("mem", 0, 1)
            for u in range(6, 10):
                for t in range(2):
                    if u == 6:
                        for g in range(2):
                            drained(pe, "Tmem", t, g)
                    project(u, memT, "m", t)
            for t in range(2):
                pe.wait_ge(hn["mk"][3], 4)
                for g in range(2):
                    ps, done = open_group(pe, ("mkT", t, g))
                    for j in range(4):
                        mm = pe.transpose(ps[:, j * P:(j + 1) * P], mk_tm[:, t, (4 * g + j) * P:(4 * g + j + 1) * P],
                                          ident)
                    mm.then_inc(done, 1)

            def gla_gate(t):
                ps, done = open_group(pe, ("z2", t))
                pe.matmul(ps[:, 0:256], glT[:, t * P:(t + 1) * P], wg2_sb, start=True, stop=True).then_inc(done, 1)

            drained(pe, "gl", 0)
            drained(pe, "gl", 1)
            for t in range(NT):
                gla_gate(t)
            for t in range(NT):
                for which, tm in (("q", q_tm), ("k", k_tm)):
                    pe.wait_ge(hn["qk"][3], 2 * NT if which == "k" else NT + 1)
                    ps, done = open_group(pe, (which + "T", t))
                    for c in range(4):
                        mm = pe.transpose(ps[:, c * P:(c + 1) * P], tm[:, t, c * P:(c + 1) * P], ident)
                    mm.then_inc(done, 1)
            def gla_decay(t):
                tri = trip if t < PT_TILES else tris
                W = 130 if t < PT_TILES else 136
                ps, done = open_group(pe, ("gT", t))
                for c in range(4):
                    mm = pe.transpose(ps[:, c * P:(c + 1) * P], qk_tm[:, t, c * P:(c + 1) * P], ident)
                mm.then_inc(done, 1)
                pe.wait_ge(g_la, 1)
                ps, done = open_group(pe, ("cum", t))
                for p in range(2):
                    mm = pe.matmul(ps[:, 256 * p:256 * p + W], zz[:, t, p * P:(p + 1) * P], tri,
                                   start=True, stop=True)
                mm.then_inc(done, 1)

            def gla_tile(t):
                qh = hats[:, t % 2, 0:2, :]
                kh = hats[:, t % 2, 2:4, :]
                pe.wait_ge(g_hat, t + 1)
                ps, done = open_group(pe, ("kh", t))
                for p in range(2):
                    mm = pe.transpose(ps[:, p * P:(p + 1) * P], kh[:, p, :], ident)
                mm.then_inc(done, 1)
                for par in range(2):
                    o = 64 * par
                    ps, done = open_group(pe, ("A", t, par))
                    for p in range(2):
                        mm = pe.matmul(ps[:, p * P:(p + 1) * P], kh[o:o + 64, p, :], qh[o:o + 64, p, :],
                                       start=True, stop=True)
                    mm.then_inc(done, 1)
                drained(pe, "kh", t)
                if t < PT_TILES:
                    for c in range(2):
                        ps, done = open_group(pe, ("KV", t, c))
                        for h in range(GH):
                            o = 64 * (h % 2)
                            mm = pe.matmul(ps[o:o + 64, (h // 2) * P:(h // 2 + 1) * P],
                                           kh_tm[64 * c:64 * c + 64, t % 2, h * 64:h * 64 + 64],
                                           vg[64 * c:64 * c + 64, t, h * P:(h + 1) * P], start=True, stop=True)
                        mm.then_inc(done, 1)
                else:
                    pe.wait_ge(g_khm, 1)
                    for c in range(4):
                        ps, done = open_group(pe, ("KV", t, c))
                        for i in range(2):
                            for h in range(GH):
                                o = 64 * (h % 2)
                                mm = pe.matmul(ps[o:o + 64, i * 256 + (h // 2) * P:i * 256 + (h // 2 + 1) * P],
                                               khm[:, 2 * c + i, h * 64:h * 64 + 64],
                                               vg[:, t, h * P:(h + 1) * P], start=True, stop=True)
                        mm.then_inc(done, 1)
                drained(pe, "A", t, 0)
                drained(pe, "A", t, 1)
                pe.wait_ge(g_smid, 2 * t + 2 if t < PT_TILES else 2 * t + 1)
                for par in range(2):
                    o = 64 * par
                    ps, done = open_group(pe, ("go", t, par))
                    for p in range(2):
                        out = ps[:, p * P:(p + 1) * P]
                        h = 2 * p + par
                        pe.matmul(out, ATm[:, par, p, :], vg[:, t, h * P:(h + 1) * P], start=True, stop=False)
                        if t < PT_TILES:
                            for c in range(2):
                                mm = pe.matmul(out[64 * c:64 * c + 64, :], qh[o:o + 64, p, 64 * c:64 * c + 64],
                                               smid_p[o:o + 64, 2 * (t % 2) + c, p, :], start=False, stop=True)
                        else:
                            for b in range(DEC_B):
                                mm = pe.matmul(out, QZ[o:o + 64, p, b, :], smid_s[o:o + 64, b, p, :],
                                               start=False, stop=(b == DEC_B - 1))
                    mm.then_inc(done, 1)

            def gla_out(t):
                pe.wait_ge(hn["gla"][3], t + 1)
                ps, done = open_group(pe, ("ogT", t))
                for c in range(4):
                    mm = pe.transpose(ps[:, c * P:(c + 1) * P], og[:, t % 2, c * P:(c + 1) * P], ident)
                mm.then_inc(done, 1)

            gla_decay(0)
            for t in range(NT):
                if t + 1 < NT:
                    gla_decay(t + 1)
                gla_tile(t)
                if t:
                    gla_out(t - 1)
            gla_out(NT - 1)

            def att_scores(m):
                kind, a, qt = SMU[m]
                if kind == "p":
                    for t in range(qt + 1):
                        drained(pe, "qT", t)
                        drained(pe, "kT", t)
                    o, n = 64 * (a % 2), (qt + 1) * P
                    ps, done = open_group(pe, ("s", m))
                    pe.matmul(ps[:, 0:n], qT[o:o + 64, a // 2, qt * P:(qt + 1) * P], kT[o:o + 64, a // 2, 0:n],
                              start=True, stop=True).then_inc(done, 1)
                else:
                    pe.wait_ge(qb_s, 1)
                    drained(pe, "kT", NT - 1)
                    pe.wait_ge(kc_s[a % 2], 16 * (a // 2 + 1))
                    for part in range(2):
                        ps, done = open_group(pe, ("s", m) if part == 0 else ("s2", m))
                        for p in range(4):
                            rhs = (kc_ring[:, a % 2, p, :] if part == 0
                                   else kT[:, p, SEQ + DEC_T * a:SEQ + DEC_T * (a + 1)])
                            out = ps[32 * p:32 * p + 32, 0:BANDK if part == 0 else DEC_T]
                            mm = pe.matmul(out, QB[:, p, a, :], rhs, start=True, stop=True,
                                           tile_position=(0, 32 * p))
                        mm.then_inc(done, 1)

            def att_probs(m):
                kind, a, qt = SMU[m]
                pe.wait_ge(sm["att"][2], m + 1)
                ps, done = open_group(pe, ("PT", m))
                for k in range(qt + 1 if kind == "p" else 4):
                    mm = pe.transpose(ps[:, k * P:(k + 1) * P], S_sb[:, m % SM, k * P:(k + 1) * P], ident)
                mm.then_inc(done, 1)
                if kind == "s":
                    ps, done = open_group(pe, ("PT2", m))
                    pe.transpose(ps[0:DEC_T, 0:P], S_sb[:, m % SM, BANDK:NEWK], ident).then_inc(done, 1)

            def att_values(m):
                kind, a, qt = SMU[m]
                drained(pe, "PT", m)
                if kind == "p":
                    o = 64 * (a % 2)
                    ps, done = open_group(pe, ("o", m))
                    for k in range(qt + 1):
                        mm = pe.matmul(ps[o:o + 64, 0:P], v_tm[:, k, a * 64:(a + 1) * 64], PT_sb[:, m % SM, k, :],
                                       start=(k == 0), stop=(k == qt))
                    mm.then_inc(done, 1)
                else:
                    drained(pe, "PT2", m)
                    pe.wait_ge(vc_s[a % 2], 16 * (a // 2 + 1))
                    pe.wait_ge(vn_s[a % 2], 16 * (a // 2 + 1))
                    ps, done = open_group(pe, ("o", m))
                    for h in range(AH):
                        o = 64 * (h % 2)
                        out = ps[o:o + 64, (h // 2) * DEC_T:(h // 2 + 1) * DEC_T]
                        for k in range(4):
                            pe.matmul(out, vc_ring[:, a % 2, k, h * 64:(h + 1) * 64],
                                      PT_sb[:, m % SM, k, DEC_T * h:DEC_T * (h + 1)], start=(k == 0), stop=False)
                        mm = pe.matmul(out, vn[0:DEC_T, a % 2, h * 64:(h + 1) * 64],
                                       PT_sb[0:DEC_T, m % SM, 4, DEC_T * h:DEC_T * (h + 1)], start=False, stop=True)
                    mm.then_inc(done, 1)

            for m in range(len(SMU) + 3):
                if m < len(SMU):
                    att_scores(m)
                if 2 <= m < len(SMU) + 2:
                    att_probs(m - 2)
                if m >= 3:
                    att_values(m - 3)
            for t in range(NT):
                drained(pe, "ogT", t)
                for m, (kind, a, qt) in enumerate(SMU):
                    if (qt == t and kind == "p") or (kind == "s" and t == NT - 1):
                        drained(pe, "o", m)
                project(10, mixT, "w", t)

            def project_then_norm(u, rows, name, norm):
                for t in range(NT):
                    project(u, rows, name, t)
                    if t >= 2:
                        norm_transposes(norm, t - 2)

            project_then_norm(11, mixT, "w", "cross")
            norm_transposes("cross", NT - 2)
            project_normed(12, hT, "cq", "cross", 0)
            norm_transposes("cross", NT - 1)
            for t in range(1, NT):
                project_normed(12, hT, "cq", "cross", t)
            for t in range(NT):
                project(13, hT, "cq", t)
            for t in range(NT):
                pe.wait_ge(hn["cq"][3], NT + t + 1)
                for g in range(2):
                    ps, done = open_group(pe, ("cqT", t, g))
                    for j in range(4):
                        mm = pe.transpose(ps[:, j * P:(j + 1) * P], cq_tm[:, t, (4 * g + j) * P:(4 * g + j + 1) * P],
                                          ident)
                    mm.then_inc(done, 1)

            def x_scores(m):
                kind, a, qt = XU[m]
                ps, done = open_group(pe, ("xs", m))
                if kind == "p":
                    drained(pe, "cqT", qt, a)
                    if m == 0:
                        for t in range(2):
                            for g in range(2):
                                drained(pe, "mkT", t, g)
                    for i in range(2):
                        for d in range(2):
                            mm = pe.matmul(ps[:, i * NMEM:(i + 1) * NMEM], cqT[:, 4 * a + 2 * i + d, qt * P:(qt + 1) * P],
                                           mkT[:, 4 * a + 2 * i + d, :], start=(d == 0), stop=(d == 1))
                else:
                    pe.wait_ge(qx_s, 1)
                    pe.wait_ge(mkc_s[a % 2], 16 * (a // 2 + 1))
                    for h in range(XH):
                        for d in range(2):
                            mm = pe.matmul(ps[32 * h:32 * h + 32, 0:NMEM], QX[:, 2 * h + d, a, :],
                                           mkc_ring[:, a % 2, 2 * h + d, :], start=(d == 0), stop=(d == 1),
                                           tile_position=(0, 32 * h))
                mm.then_inc(done, 1)

            def x_probs(m):
                kind, a, qt = XU[m]
                pe.wait_ge(sm["xat"][2], m + 1)
                ps, done = open_group(pe, ("xPT", m))
                for k in range(4 if kind == "p" else 2):
                    mm = pe.transpose(ps[:, k * P:(k + 1) * P], S_sb[:, m % SM, k * P:(k + 1) * P], ident)
                mm.then_inc(done, 1)

            def x_values(m):
                kind, a, qt = XU[m]
                drained(pe, "xPT", m)
                ps, done = open_group(pe, ("xo", m))
                if kind == "p":
                    if m == 0:
                        for u in range(8, 10):
                            for t in range(2):
                                drained(pe, "m", u, t)
                    for i in range(2):
                        for d in range(2):
                            c = (4 * a + 2 * i + d) * P
                            for k in range(2):
                                mm = pe.matmul(ps[:, (2 * i + d) * P:(2 * i + d + 1) * P], mv_tm[:, k, c:c + P],
                                               PT_sb[:, m % SM, 2 * i + k, :], start=(k == 0), stop=(k == 1))
                else:
                    pe.wait_ge(mvc_s[a % 2], 16 * (a // 2 + 1))
                    for j in range(2 * XH):
                        for k in range(2):
                            mm = pe.matmul(ps[:, j * DEC_T:(j + 1) * DEC_T], mvc_ring[:, a % 2, k, j * P:(j + 1) * P],
                                           PT_sb[:, m % SM, k, 32 * (j // 2):32 * (j // 2) + DEC_T],
                                           start=(k == 0), stop=(k == 1))
                mm.then_inc(done, 1)

            for m in range(len(XU) + 3):
                if m < len(XU):
                    x_scores(m)
                if 2 <= m < len(XU) + 2:
                    x_probs(m - 2)
                if m >= 3:
                    x_values(m - 3)
            for t in range(NT):
                for m, (kind, a, qt) in enumerate(XU):
                    if (qt == t and kind == "p") or (kind == "s" and t == NT - 1):
                        drained(pe, "xo", m)
                project(14, hT, "co", t)
            project_then_norm(15, hT, "co", "ffn")
            norm_transposes("ffn", NT - 2)
            pe.wait_ge(keys_s, 32)
            for u in range(16, 20):
                pe.wait_ge(w_split, 2 * u + 2)
                for j in range(4):
                    for i in range(2):
                        if u == 16 and j == 0:
                            if i == 1:
                                norm_transposes("ffn", NT - 1)
                            for t in range(NT if i else 3):
                                for g in range(2):
                                    drained(pe, "Tffn", t, g)
                        ps, done = open_group(pe, ("pq", u, j, i))
                        for k in range(KT):
                            for a, b in PASSES:
                                mm = pe.matmul(ps[:, 0:320], w16[u % 2][:, a, k, j * P:(j + 1) * P],
                                               h16[:, b, k, 320 * i:320 * i + 320],
                                               start=(k == 0 and a + b == 0), stop=(k == KT - 1 and a == 1))
                        mm.then_inc(done, 1)
                        unit_last[u] = ("pq", u, j, i)
                for j in range(4):
                    for i in range(2):
                        drained(pe, "pq", u, j, i)
                for t in range(NT):
                    ps, done = open_group(pe, ("sc", u, t))
                    for j in range(4):
                        mm = pe.matmul(ps[:, j * NK:(j + 1) * NK], qry[:, 4 * (u % 2) + j, t * P:(t + 1) * P],
                                       keys_sb[:, j % 2, :], start=True, stop=True)
                    mm.then_inc(done, 1)

            for b in range(8):
                pe.wait_ge(bank_free[b], uses[b])

            def z_tile(k, n, first=False):
                pe.wait_ge(u_sp, n + 1)
                if not first:
                    pe.wait_ge(z_ge, n - 1)
                for i in range(2):
                    for kk in range(KT):
                        for x, (a, b) in enumerate(((0, hhi), (0, hlo), (1, hhi))):
                            mm = pe.matmul(PS[:, 2 * (k % 2) + i, 0:320], u16[:, k % 4, a, kk, :],
                                           b[:, kk, 320 * i:320 * i + 320], start=(kk == 0 and x == 0),
                                           stop=(kk == KT - 1 and x == 2))
                mm.then_inc(z_mm, 1)

            def y_block(par, B, first=False):
                pe.wait_ge(a_sp, B * EB + EB)
                pe.wait_ge(v_sp, B * EB + EB)
                for g in range(2 * NT):
                    if not (first and g < 4):
                        pe.wait_ge(y_ev, B * (2 * NT) + (g - 3))
                    t, half = g // 2, g % 2
                    bank = 4 + (par * 2 * NT + g) % 4
                    for e in range(EB):
                        s = EB * par + e
                        for x, (a, b) in enumerate(((0, 0), (0, 1), (1, 0))):
                            mm = pe.matmul(PS[:, bank, :], a16[:, s, a, t * P:(t + 1) * P],
                                           v16[:, s, b, half * 512:(half + 1) * 512], start=(e == 0 and x == 0),
                                           stop=(e == EB - 1 and x == 2))
                    mm.then_inc(y_mm, 1)

            def gate_batch(slot, n):
                pe.wait_ge(oh_s, n + 1)
                for q in range(4):
                    pe.wait_ge(wg_ev, n * 4 + (CREDIT + q - 3))
                    for j in range(4):
                        for x in range(2):
                            mm = pe.matmul(PS[:, 4 + q, j * P:(j + 1) * P], oh[:, slot, x, :, 4 * q + j],
                                           oh[:, slot, 2, :, 4 * q + j], start=(x == 0), stop=(x == 1))
                    mm.then_inc(wg_mm, 1)

            for k in range(LEAD):
                z_tile(k, k, k < 2)
            with pe.Fori(0, NT) as i:
                for k in range(12):
                    z_tile(k % 4, i * 12 + (LEAD + k))
                    if k == 3:
                        pe.wait_ge(tk_done, i + 1)
                        pe.wait_ge(wg_ev, i * 32 + CREDIT)
                        pe.transpose(PS[:, 4, 0:P], sg, ident)
                        pe.transpose(PS[:, 4, P:2 * P], jf[:, 0, :], ident)
                        pe.transpose(PS[:, 4, 2 * P:3 * P], jf[:, 1, :], ident).then_inc(sel_mm, 1)
                    if k >= 4:
                        gate_batch(k % 2, i * 8 + (k - 4))
            for k in range(TAIL):
                z_tile(k, NA - TAIL + k)
            pe.wait_ge(wg_ev, CREDIT + T // 4)
            y_block(0, 0, True)
            with pe.Fori(0, AHEAD // 2 - 1) as i:
                for s in range(2):
                    y_block(1 - s, i * 2 + (1 + s))
            for k in range(EB):
                z_tile(k, NA + k)
            with pe.Fori(0, (NBLK - AHEAD) // 2 - 1) as i:
                for s in range(2):
                    y_block(1 - s, i * 2 + (AHEAD - 1 + s))
                    for k in range(EB):
                        z_tile(k, i * (2 * EB) + (EB * (AHEAD + 1 + s) + k))
            y_block(1, NBLK - 3)
            for k in range(EB):
                z_tile(k, NK - EB + k)
            y_block(0, NBLK - 2)
            y_block(1, NBLK - 1)

        @block.sync
        def _(sp):
            def unit(u):
                name, w, c = UNITS[u]
                for h in range(2):
                    if u:
                        sp.wait_ge(w_split, 2 * (u - 1) + h + 1)
                    sp.dma_start(raw[:, h], w.rearrange("(h k p) n -> h p k n", h=2, p=P)[h, :, :, c:c + UNIT])\
                      .then_inc(w_in_s[h], 16)

            sp.dma_start(X[:, 0, :], x_in[0:P, :]).then_inc(x_in_s[0], 16)
            sp.dma_start(AR[:, CB:CB + NCONST], consts).then_inc(c_in, 16)
            sp.dma_start(gc_sb, gcols).then_inc(c_in, 16)
            unit(0)
            sp.dma_start(X[:, 1:NT, :], x_in[P:T, :].rearrange("(t p) d -> p t d", p=P)).then_inc(x_in_s[1], 16)
            sp.dma_start(gr_sb, grows).then_inc(gains_in, 16)
            sp.dma_start(wg2_sb, wg2).then_inc(gains_in, 16)
            sp.dma_start(bs_sb, bias_s).then_inc(gains_in, 16)
            sp.dma_start(wgl_sb, w_gl.rearrange("(k p) n -> p k n", p=P)).then_inc(gains_in, 16)
            for u in range(1, len(UNITS)):
                unit(u)
                if u == 7:
                    for b in range(2):
                        if b == 0:
                            full(sp, "gl", 1)
                        sp.dma_start(mk_tm[:, b, :], mem_in[b * P:(b + 1) * P, :]).then_inc(mem_in_s[b], 16)

            def load_u(k, n, first=False):
                if not first:
                    sp.wait_ge(u_sp, n - 3)
                sp.dma_start(ust[:, k % 4, :, :], u_t[bass.ds(n, 1)].rearrange("e p n -> p (e n)"))\
                  .then_inc(u_in[k % 4], 16)

            def load_v(k, n, first=False):
                if not first:
                    sp.wait_ge(v_sp, n - 3)
                sp.dma_start(vst[:, k % 4, :], v_t[bass.ds(n, 1)].rearrange("e p n -> p (e n)"))\
                  .then_inc(v_in[k % 4], 16)

            def load_gelu(k, n, first=False):
                if not first:
                    sp.wait_ge(a_mul, n - 1)
                sp.dma_start(gel_back[:, k % 2, :], g_dram[bass.ds(n, 1)].rearrange("e p n -> p (e n)"))\
                  .then_inc(g_in[k % 2], 16)

            def load_gates(par, B, first=False):
                if not first:
                    sp.wait_ge(a_mul, B * EB - EB)
                sp.dma_start(W_sb[:, par, :, :, :], w_dram[bass.ds(B, 1)].rearrange("b p g n -> p (b g n)"))\
                  .then_inc(W_in[par], 16)

            def store_gelu(k, n):
                sp.wait_ge(z_ge, n + 1)
                sp.dma_start(g_dram[bass.ds(n, 1)].rearrange("e p n -> p (e n)"), gel[:, k % 2, :])\
                  .then_inc(gst[k % 2], 16)

            full(sp, "co", 15, NT - 1)
            for k in range(EB):
                load_u(k, k, True)
            for k in range(LEAD):
                load_u(k, EB + k)
                store_gelu(k, k)
            for s in range(2):
                sp.sem_inc(wst_s[s], CREDIT)
            with sp.Fori(0, NT) as i:
                for k in range(12):
                    load_u(k, i * 12 + (LEAD + EB + k))
                    store_gelu(k, i * 12 + (LEAD + k))
                    if k >= 4 and k % 2:
                        j = (k - 4) // 2
                        sp.wait_ge(wg_ev, i * 32 + (CREDIT + 8 * (j + 1)))
                        sp.dma_start(w_dram[:, :, bass.ds(i * 4 + j, 1), :].rearrange("b p g n -> p b (g n)"),
                                     stage[:, j % 2, :, :].rearrange("p (b e) t -> p b (e t)", e=EB))\
                          .then_inc(wst_s[j % 2], 16)
            for k in range(EB):
                load_u(k, NA - EB + k)
            store_gelu(0, NA - 8)
            for s in range(2):
                sp.wait_ge(wst_s[s], CREDIT + 16 * (NTG // 2))
                sp.wait_ge(gst[s], 16 * ((NA - TAIL) // 2))
            load_v(0, 0, True)
            load_gates(0, 0, True)
            load_gelu(0, 0, True)
            load_v(1, 1, True)
            load_gelu(1, 1, True)
            load_v(2, 2, True)
            load_v(3, 3, True)
            store_gelu(1, NA - 7)
            load_gates(1, 1, True)
            load_u(0, NA)
            load_gelu(2, 2)
            load_gelu(3, 3)
            store_gelu(2, NA - 6)
            load_u(1, NA + 1)
            load_v(4, 4)
            store_gelu(3, NA - 5)
            load_u(2, NA + 2)
            load_v(5, 5)
            store_gelu(4, NA - 4)
            load_u(3, NA + 3)
            for k in range(3):
                store_gelu(5 + k, NA - 3 + k)
            for s in range(2):
                sp.wait_ge(gst[s], 16 * (NA // 2))

            def feed_y(par, B):
                load_gates(1 - par, B + 1)
                for k in range(EB):
                    load_v(k + 2, B * EB + (k + 2))
                    load_gelu(k, B * EB + k)

            def feed_zy(par, B):
                load_gates(1 - par, B + 1)
                for k in range(EB):
                    load_u(k, B * EB + (k + 4))
                    load_v(k + 2, B * EB + (k + 2))

            with sp.Fori(0, AHEAD // 2 - 1) as i:
                for s in range(2):
                    feed_y(1 - s, i * 2 + (1 + s))
            feed_y(1, AHEAD - 1)
            with sp.Fori(0, (NBLK - AHEAD) // 2 - 1) as i:
                for s in range(2):
                    feed_zy(s, i * 2 + (AHEAD + s))
            feed_zy(0, NBLK - 2)
            load_v(2, NK - 2)
            load_v(3, NK - 1)
            for t in range(NT):
                sp.wait_ge(y_ev, (NBLK - 1) * 2 * NT + 2 * (t + 1))
                sp.dma_start(y_out[t * P:(t + 1) * P, :], X[:, t, :]).then_inc(y_s, 16)
            sp.wait_ge(y_s, 16 * NT)
            sp.wait_ge(kout_s, 16)
            for stored in outs.values():
                sp.wait_ge(stored, 16)

        @block.gpsimd
        def _(pool):
            def split(u):
                for h in range(2):
                    pool.wait_ge(w_hi, 2 * u + h + 1)
                    w = w16[u % 2][:, :, 4 * h:4 * h + 4, :].rearrange("p x k n -> p x (k n)")
                    pool.tensor_tensor(w[:, 1], raw[:, h].rearrange("p k n -> p (k n)"), w[:, 0], ALU.subtract)\
                        .then_inc(w_split, 1)

            for u in range(4):
                split(u)
            pool.wait_ge(hn["qk"][3], 2 * NT)
            pool.dma_start(k_out.rearrange("(t p) n -> p t n", p=P), k_tm).then_inc(kout_s, 16)
            split(4)
            for t in range(NT):
                drained(pool, "z", 2, t)
            pool.dma_start(v_out.rearrange("(t p) n -> p t n", p=P), v_tm).then_inc(outs["v"], 16)
            for u in range(5, 10):
                split(u)
            pool.wait_ge(hn["mk"][3], 4)
            pool.dma_start(mk_out.rearrange("(t p) n -> p t n", p=P), mk_tm).then_inc(outs["mk"], 16)
            for u in range(8, 10):
                for t in range(2):
                    drained(pool, "m", u, t)
            pool.dma_start(mv_out.rearrange("(t p) n -> p t n", p=P), mv_tm).then_inc(outs["mv"], 16)
            split(10)
            full(pool, "go", PT_TILES - 1, 1)
            pool.dma_start(st_s, state_in.rearrange("b g p v -> p b g v")).then_inc(st_s_s, 16)
            pool.wait_ge(g_st, 2 * PT_TILES)
            pool.dma_start(gp_out.rearrange("g p v -> p g v"), S_p).then_inc(outs["gp"], 16)
            full(pool, "go", NT - 1, 1)
            def load_bias(n):
                h = n % AH
                pool.dma_start(bias_ring[:, n % BSLOTS, :], bias_p[h]).then_inc(bias_s_[n % BSLOTS], 16)

            def load_keys(b):
                pool.dma_start(kc_ring[:, b % 2, :, :], kc_t[b]).then_inc(kc_s[b % 2], 16)

            def load_values(b):
                pool.dma_start(vc_ring[:, b % 2, :, :], v_c[b]).then_inc(vc_s[b % 2], 16)
                pool.dma_start(vn[0:DEC_T, b % 2, :], v_tm[DEC_T * b:DEC_T * (b + 1), NT - 1, :])\
                    .then_inc(vn_s[b % 2], 16)

            for n in range(BSLOTS):
                load_bias(n)
            pool.wait_ge(g_st, 2 * PT_TILES + 4)
            pool.dma_start(gs_out.rearrange("b g p v -> p b g v"), st_s).then_inc(outs["gs"], 16)
            for m in range(len(SMU) + 3):
                if m == 2:
                    pool.wait_ge(outs["gs"], 16)
                    pool.wait_ge(hn["gla"][3], NT)
                if m in (2, 4):
                    load_keys(m // 2 - 1)
                    load_values(m // 2 - 1)
                if m < len(SMU):
                    kind, b, _ = SMU[m]
                    if kind == "p" and bias_use[m] + BSLOTS < len(bias_use):
                        pool.wait_ge(sm["att"][0], m + 1)
                        load_bias(bias_use[m] + BSLOTS)
                    if kind == "s" and b + 2 < DEC_B:
                        full(pool, "s", m)
                        load_keys(b + 2)
                if m >= 3 and SMU[m - 3][0] == "s" and SMU[m - 3][1] + 2 < DEC_B:
                    full(pool, "o", m - 3)
                    load_values(SMU[m - 3][1] + 2)

            full(pool, "s", len(SMU) - 1)
            split(11)

            def load_memkeys(b):
                pool.dma_start(mkc_ring[:, b % 2, :, :], mk_c[b]).then_inc(mkc_s[b % 2], 16)

            def load_memvalues(b):
                pool.dma_start(mvc_ring[:, b % 2, :, :], mv_c[b]).then_inc(mvc_s[b % 2], 16)

            for b in range(2):
                full(pool, "o", SMU.index(("s", DEC_B - 2 + b, 0)))
                load_memkeys(b)
                load_memvalues(b)
            for u in range(12, 15):
                split(u)
            for m in range(len(XU) + 3):
                if m < len(XU) and XU[m][0] == "s" and XU[m][1] + 2 < DEC_B:
                    full(pool, "xs", m)
                    load_memkeys(XU[m][1] + 2)
                if m >= 3 and XU[m - 3][0] == "s" and XU[m - 3][1] + 2 < DEC_B:
                    full(pool, "xo", m - 3)
                    load_memvalues(XU[m - 3][1] + 2)
            full(pool, "xs", len(XU) - 1)
            split(15)
            full(pool, "xo", len(XU) - 1)
            for i in range(2):
                pool.dma_start(keys_sb[:, i, :], keys_t[i]).then_inc(keys_s, 16)
            for u in range(16, 20):
                split(u)
            def u_low(k, n):
                pool.wait_ge(u_hi, n + 1)
                pool.tensor_tensor(u16[:, k, 1, :, :].rearrange("p k e -> p (k e)"),
                                   ust[:, k, :, :].rearrange("p k e -> p (k e)"),
                                   u16[:, k, 0, :, :].rearrange("p k e -> p (k e)"), ALU.subtract).then_inc(u_sp, 1)

            with pool.Fori(0, AHEAD + 1) as i:
                for k in range(EB):
                    u_low(k, i * EB + k)

        @block.scalar
        def _(act):
            def split_half(u, h):
                act.wait_ge(w_in_s[h], 16 * (u + 1))
                if h == 0 and u >= 2:
                    full(act, *unit_last[u - 2])
                link(act, act.activation(w16[u % 2][:, 0, 4 * h:4 * h + 4, :], raw[:, h], ACT.Copy, scale=USCALE), act_step)
                act.activation(raw[:, h], raw[:, h], ACT.Copy, scale=USCALE).then_inc(w_hi, 1)

            def ahead(u, t):
                if t < 2:
                    split_half(u + 1, t)

            def norm_stats(name, ready):
                _, n, src, _ = NORMS[name]
                for t in range(n):
                    ready(t)
                    link(act, act.activation(junk, src(t), ACT.Square, accum_out=nrm_ss[:, t % 2, :]), act_step)
                    if t >= 2:
                        act.wait_ge(nrm[name][1], t - 1)
                    act.activation(nrm_rs[:, t % 2, :], nrm_ss[:, t % 2, :], ACT.Sqrt, scale=1.0 / D, bias=eps_sb)\
                       .then_inc(nrm[name][0], 1)

            def head_norm(name, items, heads, width):
                sqs, sums, rstd, _ = hn[name]
                for m in range(len(items) + 1):
                    if m < len(items):
                        key, dst, slot_free = items[m]
                        slot_free()
                        ps, free = full(act, *key)
                        act.activation(dst, ps, ACT.Copy, scale=1.0 / USCALE).then_inc(free, 1)
                        drained(act, *key)
                        if m >= 2:
                            act.wait_ge(sums, m - 1)
                        act.activation(sq[:, m % 2, :], dst, ACT.Square).then_inc(sqs, 1)
                    if m:
                        act.wait_ge(sums, m)
                        s = (m - 1) % 2
                        act.activation(hn_rs[:, s, 0:heads], hn_ss[:, s, 0:heads], ACT.Sqrt, scale=1.0 / width,
                                       bias=eps_sb).then_inc(rstd, 1)

            def copy_out(dst, *key, scale=1.0):
                ps, free = full(act, *key)
                n = 1
                for s in dst.shape[1:]:
                    n *= s
                if len(dst.shape) == 3:
                    ps = ps[0:dst.shape[0], 0:n].rearrange("p (a b) -> p a b", a=dst.shape[1])
                else:
                    ps = ps[0:dst.shape[0], 0:n]
                act.activation(dst, ps, ACT.Copy, scale=scale).then_inc(free, 1)

            act.wait_ge(c_in, 16 * 3)
            def mix_ready(t):
                if t == 1:
                    split_half(0, 0)
                    split_half(0, 1)
                act.wait_ge(x_in_s[min(t, 1)], 16)

            norm_stats("mix", mix_ready)
            head_norm("qk", [(("z", u, t), (q_tm, k_tm)[u][:, t, :], lambda u=u, t=t: ahead(u, t)) for u in range(2) for t in range(NT)], 8, 64)
            for u, dst in ((2, v_tm), (3, qk_tm), (4, vg)):
                for t in range(NT):
                    ahead(u, t)
                    copy_out(dst[:, t, :], "z", u, t, scale=1.0 / USCALE)
            for t in range(NT):
                ahead(5, t)
                ps, free = full(act, "z", 5, t)
                link(act, act.activation(rr[:, t, :], ps, ACT.Copy, scale=1.0 / USCALE), act_step)
                if t >= 2:
                    act.wait_ge(r_silu, t - 1)
                act.activation(er[:, t % 2, :], ps, ACT.Exp, scale=-1.0 / USCALE).then_inc(free, 1)
            act.wait_ge(zero_s, 1)
            for i in range(2):
                copy_out(glT[0:16, 320 * i:320 * i + 320], "gl", i, scale=1.0 / USCALE)
            norm_stats("mem", lambda t: act.wait_ge(mem_in_s[t], 16))
            def mk_free(u, t):
                ahead(u, t)
                act.wait_ge(nrm["mem"][1], 2)
            head_norm("mk", [(("m", u, t), mk_tm[:, t, (u - 6) * 512:(u - 5) * 512], lambda u=u, t=t: mk_free(u, t))
                             for u in range(6, 8) for t in range(2)], 2, 256)
            for u in range(8, 10):
                for t in range(2):
                    ahead(u, t)
                    copy_out(mv_tm[:, t, (u - 8) * 512:(u - 7) * 512], "m", u, t, scale=1.0 / USCALE)
            for t in range(2):
                for g in range(2):
                    copy_out(mkT[:, 4 * g:4 * g + 4, t * P:(t + 1) * P], "mkT", t, g)
            act.wait_ge(outs["mk"], 16)
            for t in range(NT):
                ps, free = full(act, "z2", t)
                act.activation(zz[:, t, :], ps[:, 0:256], ACT.Copy).then_inc(free, 1)
                drained(act, "z2", t)
                link(act, act.activation(ll[:, t, :], zz[:, t, :], ACT.Abs), act_step)
            link(act, act.activation(ll, ll, ACT.Exp, scale=-1.0), act_step)
            act.activation(ll, ll, ACT.Ln, bias=1.0).then_inc(g_l, 1)

            for t in range(NT):
                for which, dst in (("q", qT), ("k", kT)):
                    copy_out(dst[:, :, t * P:(t + 1) * P], which + "T", t)

            def decays(t):
                W = 130 if t < PT_TILES else 136
                ps, free = full(act, "cum", t)
                psv = ps.rearrange("p (a b) -> p a b", a=2)
                if t >= 2:
                    act.wait_ge(g_st, 2 * (t - 1))
                link(act, act.activation(eplus[:, t % 2, :, 0:W], psv[:, :, 0:W], ACT.Exp), act_step)
                if t:
                    act.wait_ge(g_hat, t)
                act.activation(eminus, psv[:, :, 0:P], ACT.Exp, scale=-1.0).then_inc(free, 1)

            def out_high(t):
                ps, _ = full(act, "ogT", t)
                act.activation(mixT[:, 0, 4:8, t * P:(t + 1) * P], ps.rearrange("p (a b) -> p a b", a=4), ACT.Copy)\
                   .then_inc(og_hi, 1)

            decays(0)
            for t in range(NT):
                if t + 1 < NT:
                    decays(t + 1)
                copy_out(kh_tm[:, t % 2, :], "kh", t)
                sqs, sums, rstd, done = hn["gla"]
                if t >= 2:
                    full(act, "ogT", t - 2)
                if t == 0:
                    act.wait_ge(r_silu, NT)
                for par in range(2):
                    ps, free = full(act, "go", t, par)
                    act.activation(og[:, t % 2, :].rearrange("p (g par d) -> p g par d", g=2, par=2)[:, :, par, :],
                                   ps[:, 0:256].rearrange("p (g d) -> p g d", g=2), ACT.Copy).then_inc(free, 1)
                for par in range(2):
                    drained(act, "go", t, par)
                act.activation(sq[:, t % 2, :], og[:, t % 2, :], ACT.Square).then_inc(sqs, 1)
                act.wait_ge(sums, t + 1)
                act.activation(hn_rs[:, t % 2, 0:4], hn_ss[:, t % 2, 0:4], ACT.Sqrt, scale=1.0 / GV, bias=eps_sb)\
                   .then_inc(rstd, 1)
                if t == 0:
                    act.wait_ge(kout_s, 16)
                if t:
                    out_high(t - 1)
            out_high(NT - 1)

            def softmax_exp(m):
                kind, a, qt = SMU[m]
                n = (qt + 1) * P if kind == "p" else NEWK
                act.wait_ge(sm["att"][0], m + 1)
                act.activation(S_sb[:, m % SM, 0:n], S_sb[:, m % SM, 0:n], ACT.Exp, bias=sm_nm[:, m % SM, 0:1],
                               accum_out=sm_sum[:, m % SM, 0:1]).then_inc(sm["att"][1], 1)

            def probs_out(m):
                kind, a, qt = SMU[m]
                if m >= SM:
                    full(act, "o", m - SM)
                copy_out(PT_sb[:, m % SM, 0:(qt + 1 if kind == "p" else 4), :], "PT", m)
                if kind == "s":
                    copy_out(PT_sb[0:DEC_T, m % SM, 4, :], "PT2", m)

            for m in range(len(SMU) + 2):
                if m < len(SMU):
                    softmax_exp(m)
                if m >= 2:
                    probs_out(m - 2)
                if m >= len(SMU):
                    full(act, "s", len(SMU) - 1)
                    split_half(11, m - len(SMU))
            for h in range(2):
                split_half(12, h)
            norm_stats("cross", lambda t: act.wait_ge(x_mix, NT + t + 1))
            def cq_free(u, t):
                ahead(u, t)
                full(act, "w", 11, NT - 1)
            head_norm("cq", [(("cq", u, t), cq_tm[:, t, (u - 12) * 512:(u - 11) * 512], lambda u=u, t=t: cq_free(u, t))
                             for u in range(12, 14) for t in range(NT)], 2, 256)
            for t in range(NT):
                for g in range(2):
                    copy_out(cqT[:, 4 * g:4 * g + 4, t * P:(t + 1) * P], "cqT", t, g)

            def x_exp(m):
                kind, a, qt = XU[m]
                ps, free = full(act, "xs", m)
                act.wait_ge(sm["xat"][0], m + 1)
                if m >= SM:
                    full(act, "xPT", m - SM)
                for i in range(2 if kind == "p" else 1):
                    ins = act.activation(S_sb[:, m % SM, i * NMEM:(i + 1) * NMEM], ps[:, i * NMEM:(i + 1) * NMEM],
                                         ACT.Exp, bias=sm_nm[:, m % SM, i:i + 1], scale=1.0 / 16,
                                         accum_out=sm_sum[:, m % SM, i:i + 1])
                    if kind == "p" and i == 0:
                        link(act, ins, act_step)
                ins.then_inc(free, 1)

            for m in range(len(XU) + 2):
                if m < len(XU):
                    x_exp(m)
                if m >= 2:
                    if m >= SM + 2:
                        full(act, "xo", m - 2 - SM)
                    copy_out(PT_sb[:, (m - 2) % SM, 0:(4 if XU[m - 2][0] == "p" else 2), :], "xPT", m - 2)
            full(act, "xs", len(XU) - 1)
            for u in (15, 16):
                for h in range(2):
                    split_half(u, h)
            norm_stats("ffn", lambda t: act.wait_ge(x_cross, NT + t + 1))
            for u in range(16, 20):
                for j in range(4):
                    for i in range(2):
                        if u < 19 and j == 0:
                            ahead(u, i)
                        if u >= 18 and j == 0 and i == 0:
                            full(act, "sc", u - 2, NT - 1)
                        copy_out(qry[:, 4 * (u % 2) + j, 320 * i:320 * i + 320], "pq", u, j, i,
                                 scale=1.0 / USCALE)

            def v_high(k, par, B, early=False):
                act.wait_ge(v_in[k], B * 16 + 16)
                if not early:
                    act.wait_ge(y_mm, B * (2 * NT) - 2 * NT)
                act.activation(v16[:, EB * par + k, 0, :], vst[:, k, :], ACT.Copy).then_inc(v_hi, 1)

            def gelu(k, n):
                act.activation(gel[:, k % 2, :].rearrange("p (i t) -> p i t", i=2),
                               PS[:, 2 * (k % 2):2 * (k % 2) + 2, 0:320], ACT.Gelu, scale=1.0 / USCALE)\
                   .then_inc(z_ge, 1)

            def gated_high(k, par, n):
                act.wait_ge(a_mul, n + 1)
                act.activation(a16[:, EB * par + k, 0, :], a32[:, k % 2, :], ACT.Copy).then_inc(a_hi, 1)

            for k in range(EB):
                if k == 0 or k == EB - 1:
                    full(act, "sc", 18 if k == 0 else 19, NT - 1)
                act.wait_ge(u_in[k], 16)
                act.activation(u16[:, k, 0, :, :], ust[:, k, :, :], ACT.Copy, scale=USCALE).then_inc(u_hi_only, 1)
                act.wait_ge(u_hi_only, k + 1)
                act.activation(ust[:, k, :, :], ust[:, k, :, :], ACT.Copy, scale=USCALE).then_inc(u_hi, 1)

            def early_tile(k, n, stored):
                act.wait_ge(z_mm, n + 1)
                if stored is not None:
                    act.wait_ge(gst[k % 2], stored)
                gelu(k, n)
                act.wait_ge(u_in[k % 4], n * 4 + (32 - 4 * (k % 4)))
                act.activation(u16[:, k % 4, 0, :, :], ust[:, k % 4, :, :], ACT.Copy, scale=USCALE).then_inc(u_hi_only, 1)
                act.wait_ge(u_hi_only, n + 5)
                act.activation(ust[:, k % 4, :, :], ust[:, k % 4, :, :], ACT.Copy, scale=USCALE).then_inc(u_hi, 1)

            for k in range(LEAD):
                early_tile(k, k, None if k < 2 else 16 * (k // 2))
            act.sem_inc(wg_ev, CREDIT)
            with act.Fori(0, NT) as i:
                for k in range(12):
                    early_tile(k, i * 12 + (LEAD + k), i * 96 + (8 * LEAD + 16 * (k // 2)))
                    if k == 2:
                        act.wait_ge(tk_exp_in, i + 1)
                        act.activation(sg, sg, ACT.Exp).then_inc(tk_exp, 1)
                    if k >= 4:
                        j = k - 4
                        if j % 2 == 0:
                            act.wait_ge(wst_s[(j // 2) % 2], i * 32 + (CREDIT + 16 * (j // 4)))
                        for q in range(4):
                            act.wait_ge(wg_mm, i * 32 + (4 * j + q + 1))
                            c = OHB * (j % 2) + 4 * q
                            act.activation(stage[:, (j // 2) % 2, :, c:c + 4].rearrange("p e t -> p t e"),
                                           PS[:, 4 + q, :].rearrange("p (t e) -> p t e", t=4), ACT.Copy,
                                           scale=1.0 / USCALE).then_inc(wg_ev, 1)

            def y_steps(par, B, early=False):
                for k in range(EB):
                    v_high(k, par, B, early)
                    gated_high(k, par, B * EB + k)

            def zy_steps(par, B):
                for k in range(EB):
                    v_high(k, par, B)
                    act.wait_ge(z_mm, B * EB + (k + 1))
                    act.wait_ge(a_mul, B * EB + (k - 1))
                    gelu(k, B * EB + k)
                    gated_high(k, par, B * EB + k)

            def u_steps(B):
                for k in range(EB):
                    act.wait_ge(u_in[k], B * 16 + 16)
                    act.wait_ge(z_mm, B * EB + (k - 3))
                    act.activation(u16[:, k, 0, :, :], ust[:, k, :, :], ACT.Copy, scale=USCALE).then_inc(u_hi, 1)

            for k in range(TAIL):
                early_tile(k, NA - TAIL + k, 8 * (NA - TAIL) + 16 * (k // 2))
                for y in {2: (0, 1), 3: (2, 3)}.get(k, ()):
                    v_high(y, 0, 0, True)
                    gated_high(y, 0, y)
            y_steps(1, 1, True)
            with act.Fori(0, AHEAD // 2 - 1) as i:
                for s in range(2):
                    y_steps(s, i * 2 + (2 + s))
            zy_steps(0, AHEAD)
            with act.Fori(0, (NBLK - AHEAD) // 2 - 1) as i:
                for s in range(2):
                    B = i * 2 + (AHEAD + 1 + s)
                    u_steps(B)
                    zy_steps(1 - s, B)
            u_steps(NBLK - 1)
            zy_steps(1, NBLK - 1)

        @block.vector
        def _(dve):
            link(dve, dve.memset(eps_sb, EPS), dve_step)
            dve.sem_inc(c_in, 16)

            def norm_step(name, t):
                gi, n, src, dst = NORMS[name]
                if t < n:
                    dve.wait_ge(nrm[name][0], t + 1)
                    link(dve, dve.reciprocal(nrm_rs[:, t % 2, :], nrm_rs[:, t % 2, :]), dve_step)
                    dve.tensor_scalar(xn[:, t % 2, :], src(t), nrm_rs[:, t % 2, :], None, ALU.mult)\
                       .then_inc(nrm[name][1], 1)
                if t:
                    for g in range(2):
                        ps, free = full(dve, "T" + name, t - 1, g)
                        if t >= 2:
                            drained(dve, "T" + name, t - 2, g)
                        h = er[:, g, :].rearrange("p (a b) -> p a b", a=4)
                        f, c = slice(4 * g, 4 * g + 4), slice((t - 1) * P, t * P)
                        link(dve, dve.tensor_tensor(h, ps.rearrange("p (a b) -> p a b", a=4),
                                                    gc_sb[:, gi, f].unsqueeze(2).to_broadcast([P, 4, P]), ALU.mult),
                             dve_step)
                        link(dve, dve.tensor_copy(dst[:, 0, f, c], h), dve_step)
                        dve.tensor_tensor(dst[:, 1, f, c], h, dst[:, 0, f, c], ALU.subtract).then_inc(free, 1)

            def norm_scale(name):
                for t in range(NORMS[name][1] + 1):
                    norm_step(name, t)

            def head_norm(name, items, heads, width):
                sqs, sums, rstd, done = hn[name]
                for m in range(len(items) + 1):
                    if m < len(items):
                        dve.wait_ge(sqs, m + 1)
                        dve.tensor_reduce(hn_ss[:, m % 2, 0:heads],
                                          sq[:, m % 2, :].rearrange("p (h d) -> p h d", h=heads), AX.X, ALU.add)\
                           .then_inc(sums, 1)
                    if m:
                        dst, gain = items[m - 1]
                        v = dst.rearrange("p (h d) -> p h d", h=heads)
                        dve.wait_ge(rstd, m)
                        root = hn_rs[:, (m - 1) % 2, 0:heads]
                        link(dve, dve.reciprocal(root, root), dve_step)
                        rs = hn_rs[:, (m - 1) % 2, 0:heads].unsqueeze(2).to_broadcast([P, heads, width])
                        link(dve, dve.tensor_tensor(v, v, rs, ALU.mult), dve_step)
                        dve.tensor_tensor(v, v, gain.unsqueeze(1).to_broadcast([P, heads, width]), ALU.mult)\
                           .then_inc(done, 1)

            dve.wait_ge(c_in, 16 * 3)
            norm_scale("mix")
            dve.wait_ge(gains_in, 16 * 4)
            link(dve, dve.tensor_scalar(wgl16[:, 0], wgl_sb, USCALE, None, ALU.mult), dve_step)
            dve.scalar_tensor_tensor(out=wgl16[:, 1], in0=wgl_sb, scalar=USCALE, in1=wgl16[:, 0], op0=ALU.mult,
                                     op1=ALU.subtract).then_inc(wgl_s, 1)
            head_norm("qk", [((q_tm, k_tm)[u][:, t, :], (gq, gk)[u]) for u in range(2) for t in range(NT)], 8, 64)
            for t in range(NT):
                drained(dve, "z", 5, t)
                s = t % 2
                link(dve, dve.tensor_scalar(er[:, s, :], er[:, s, :], 1.0, None, ALU.add), dve_step)
                link(dve, dve.reciprocal(er[:, s, :], er[:, s, :]), dve_step)
                dve.tensor_tensor(rr[:, t, :], rr[:, t, :], er[:, s, :], ALU.mult).then_inc(r_silu, 1)
            full(dve, "gl", 1)
            dve.memset(glT, 1.0).then_inc(zero_s, 1)
            norm_scale("mem")
            head_norm("mk", [(mk_tm[:, t, (u - 6) * 512:(u - 5) * 512], gck) for u in range(6, 8) for t in range(2)],
                      2, 256)
            dve.wait_ge(outs["mk"], 16)
            full(dve, "mkT", 1, 1)
            link(dve, dve.memset(QZ, 0.0), dve_step)
            link(dve, dve.memset(S_p, 0.0), dve_step)

            dve.wait_ge(g_l, 1)
            dve.scalar_tensor_tensor(out=zz, in0=zz, scalar=0.0, in1=ll, op0=ALU.min, op1=ALU.subtract).then_inc(g_la, 1)

            def scaled(dst, src, t, col, inc):
                for p in range(2):
                    ins = dve.tensor_scalar(dst[:, p, :], src[:, p, :], eplus[:, t % 2, p, col:col + 1], None, ALU.mult)
                    if p == 0:
                        ins.then_inc(dve_step, 1)
                        count[id(dve_step)] += 1
                ins.then_inc(inc, 1)

            def out_low(t):
                c = slice(t * P, (t + 1) * P)
                ps, free = full(dve, "ogT", t)
                dve.wait_ge(og_hi, t + 1)
                dve.tensor_tensor(mixT[:, 1, 4:8, c], ps.rearrange("p (a b) -> p a b", a=4), mixT[:, 0, 4:8, c],
                                  ALU.subtract).then_inc(free, 1)

            def put_halves(dst, rows, features, cols, src, free):
                link(dve, dve.tensor_copy(dst[rows, 0, features, cols], src), dve_step)
                dve.tensor_tensor(dst[rows, 1, features, cols], src, dst[rows, 0, features, cols], ALU.subtract)\
                   .then_inc(free, 1)

            def decayed(t):
                s = t % 2
                ps, free = full(dve, "gT", t)
                psv = ps.rearrange("p (a b) -> p a b", a=4)
                drained(dve, "cum", t)
                link(dve, dve.scalar_tensor_tensor(out=hats[:, s, 0:2, :], in0=psv[:, 0:2, :], scalar=GK ** -0.5,
                                                   in1=eplus[:, s, :, 0:P], op0=ALU.mult, op1=ALU.mult), dve_step)
                dve.tensor_tensor(hats[:, s, 2:4, :], psv[:, 2:4, :], eminus, ALU.mult).then_inc(free, 1)
                drained(dve, "gT", t)
                if t == NT - 1:
                    for b in range(DEC_B):
                        link(dve, dve.tensor_copy(QZ[:, :, b, DEC_T * b:DEC_T * (b + 1)],
                                                  hats[:, s, 0:2, DEC_T * b:DEC_T * (b + 1)]), dve_step)
                dve.sem_inc(g_hat, 1)

            dve.wait_ge(g_la, 1)
            decayed(0)
            for t in range(NT):
                s = t % 2
                if t:
                    full(dve, "go", t - 1, 1)
                if t + 1 < NT:
                    decayed(t + 1)
                mask = maskp if t < PT_TILES else masks
                for par in range(2):
                    ps, free = full(dve, "A", t, par)
                    dve.tensor_tensor(ATm[:, par], ps[:, 0:256].rearrange("p (h t) -> p h t", h=2),
                                      mask.unsqueeze(1).to_broadcast([P, 2, P]), ALU.mult).then_inc(free, 1)
                if t < PT_TILES:
                    for c in range(2):
                        scaled(smid_p[:, 2 * s + c], S_p, t, P + c, g_smid)
                        dve.wait_ge(g_smid, 2 * t + c + 1)
                        ps, free = full(dve, "KV", t, c)
                        dve.tensor_tensor(S_p, smid_p[:, 2 * s + c], ps[:, 0:256].rearrange("p (a b) -> p a b", a=2),
                                          ALU.add).then_inc(free, 1)
                        drained(dve, "KV", t, c)
                        scaled(S_p, S_p, t, 64 * c + 63, g_st)
                        dve.wait_ge(g_st, 2 * t + c + 1)
                else:
                    drained(dve, "kh", t)
                    dve.wait_ge(hn["gla"][3], t)
                    dve.tensor_tensor(khm, kh_tm[:, s, :].unsqueeze(1).to_broadcast([P, DEC_B, 256]),
                                      bmask.unsqueeze(2).to_broadcast([P, DEC_B, 256]), ALU.mult).then_inc(g_khm, 1)
                    dve.wait_ge(st_s_s, 16)
                    for p in range(2):
                        ins = dve.tensor_tensor(smid_s[:, :, p, :], st_s[:, :, p, :],
                                                eplus[:, s, p, P:P + 8].unsqueeze(2).to_broadcast([P, DEC_B, P]),
                                                ALU.mult)
                        if p == 0:
                            link(dve, ins, dve_step)
                    ins.then_inc(g_smid, 1)
                    dve.wait_ge(g_smid, 2 * t + 1)
                    for c in range(4):
                        ps, free = full(dve, "KV", t, c)
                        dve.tensor_tensor(st_s[:, 2 * c:2 * c + 2, :, :].rearrange("p b g v -> p (b g v)"),
                                          smid_s[:, 2 * c:2 * c + 2, :, :].rearrange("p b g v -> p (b g v)"),
                                          ps, ALU.add).then_inc(free, 1)
                        drained(dve, "KV", t, c)
                        for i in range(2):
                            for p in range(2):
                                b = 2 * c + i
                                ins = dve.tensor_scalar(st_s[:, b, p, :], st_s[:, b, p, :],
                                                        eplus[:, s, p, DEC_T * b + 15:DEC_T * b + 16], None, ALU.mult)
                                if i + p < 2:
                                    link(dve, ins, dve_step)
                        ins.then_inc(g_st, 1)
                sqs, sums, rstd, done = hn["gla"]
                dve.wait_ge(sqs, t + 1)
                dve.tensor_reduce(hn_ss[:, s, 0:4], sq[:, s, :].rearrange("p (h d) -> p h d", h=GH), AX.X, ALU.add)\
                   .then_inc(sums, 1)
                v = og[:, s, :].rearrange("p (h d) -> p h d", h=GH)
                dve.wait_ge(rstd, t + 1)
                link(dve, dve.reciprocal(hn_rs[:, s, 0:4], hn_rs[:, s, 0:4]), dve_step)
                link(dve, dve.tensor_tensor(v, v, hn_rs[:, s, 0:4].unsqueeze(2).to_broadcast([P, GH, GV]), ALU.mult),
                     dve_step)
                link(dve, dve.tensor_tensor(v, v, ggla.unsqueeze(1).to_broadcast([P, GH, GV]), ALU.mult), dve_step)
                dve.tensor_tensor(og[:, s, :], og[:, s, :], rr[:, t, :], ALU.mult).then_inc(done, 1)
                if t:
                    out_low(t - 1)
            out_low(NT - 1)

            for t in range(NT):
                drained(dve, "qT", t)
            link(dve, dve.memset(QB, 0.0), dve_step)
            for o in (0, 64):
                ins = dve.tensor_copy(QB[o:o + 64, :, :, o // 4:o // 4 + DEC_T],
                                      qT[o:o + 64, :, SEQ:T].rearrange("p c (b t) -> p c b t", b=DEC_B))
                if o == 0:
                    link(dve, ins, dve_step)
            ins.then_inc(qb_s, 1)

            def att_max(m):
                kind, a, qt = SMU[m]
                s = m % SM
                if m >= SM:
                    full(dve, "PT" if SMU[m - SM][0] == "p" else "PT2", m - SM)
                ps, free = full(dve, "s", m)
                if kind == "p":
                    n = (qt + 1) * P
                    slot = bias_use[m] % BSLOTS
                    dve.wait_ge(bias_s_[slot], 16 * (bias_use[m] // BSLOTS + 1))
                    dve.scalar_tensor_tensor(out=S_sb[:, s, 0:n], in0=ps[:, 0:n], scalar=AD ** -0.5,
                                             in1=bias_ring[:, slot, 512 - n:512], op0=ALU.mult, op1=ALU.add)\
                       .then_inc(free, 1)
                    drained(dve, "s", m)
                else:
                    n = NEWK
                    dve.scalar_tensor_tensor(out=S_sb[:, s, 0:BANDK], in0=ps, scalar=AD ** -0.5,
                                             in1=bs_sb[:, 0:BANDK], op0=ALU.mult, op1=ALU.add).then_inc(free, 1)
                    ps, free = full(dve, "s2", m)
                    dve.scalar_tensor_tensor(out=S_sb[:, s, BANDK:NEWK], in0=ps[:, 0:DEC_T], scalar=AD ** -0.5,
                                             in1=bs_sb[:, BANDK:NEWK], op0=ALU.mult, op1=ALU.add).then_inc(free, 1)
                    drained(dve, "s", m)
                    drained(dve, "s2", m)
                dve.tensor_reduce(sm_nm[:, s, 0:1], S_sb[:, s, 0:n], AX.X, ALU.max, negate=True)\
                   .then_inc(sm["att"][0], 1)

            def att_norm(m):
                kind, a, qt = SMU[m]
                n = (qt + 1) * P if kind == "p" else NEWK
                s = m % SM
                dve.wait_ge(sm["att"][1], m + 1)
                link(dve, dve.reciprocal(sm_inv[:, s, 0:1], sm_sum[:, s, 0:1]), dve_step)
                dve.tensor_scalar(S_sb[:, s, 0:n], S_sb[:, s, 0:n], sm_inv[:, s, 0:1], None, ALU.mult)\
                   .then_inc(sm["att"][2], 1)

            def att_out(m):
                kind, a, qt = SMU[m]
                ps, free = full(dve, "o", m)
                if kind == "p":
                    o = 64 * (a % 2)
                    put_halves(mixT, slice(o, o + 64), a // 2, slice(qt * P, (qt + 1) * P), ps[o:o + 64, 0:P], free)
                else:
                    put_halves(mixT, slice(0, P), slice(0, 4), slice(SEQ + DEC_T * a, SEQ + DEC_T * (a + 1)),
                               ps[:, 0:64].rearrange("p (c t) -> p c t", c=4), free)

            for m in range(len(SMU) + 3):
                if m < len(SMU):
                    att_max(m)
                if 1 <= m < len(SMU) + 1:
                    att_norm(m - 1)
                if m >= 3:
                    att_out(m - 3)

            def residual(name, u0, ready, norm):
                for u in (u0, u0 + 1):
                    for t in range(NT):
                        ps, free = full(dve, name, u, t)
                        c = slice((u - u0) * 512, (u - u0 + 1) * 512)
                        dve.scalar_tensor_tensor(out=X[:, t, c], in0=ps, scalar=1.0 / USCALE, in1=X[:, t, c],
                                                 op0=ALU.mult, op1=ALU.add).then_inc(free, 1)
                        drained(dve, name, u, t)
                        dve.sem_inc(ready, 1)
                        if u > u0 and t:
                            norm_step(norm, t - 1)
                for t in (NT - 1, NT):
                    norm_step(norm, t)

            residual("w", 10, x_mix, "cross")
            head_norm("cq", [(cq_tm[:, t, (u - 12) * 512:(u - 11) * 512], gcq) for u in range(12, 14) for t in range(NT)],
                      2, 256)
            for g in range(2):
                drained(dve, "cqT", NT - 1, g)
            link(dve, dve.memset(QX, 0.0), dve_step)
            dve.tensor_copy(QX[:, :, :, 0:DEC_T], cqT[:, :, SEQ:T].rearrange("p c (b t) -> p c b t", b=DEC_B))\
               .then_inc(qx_s, 1)

            def x_max(m):
                kind, a, qt = XU[m]
                ps, _ = full(dve, "xs", m)
                h = 2 if kind == "p" else 1
                s = m % SM
                link(dve, dve.tensor_reduce(sm_max[:, s, 0:h], ps[:, 0:h * NMEM].rearrange("p (h k) -> p h k", h=h),
                                            AX.X, ALU.max), dve_step)
                dve.tensor_scalar(sm_nm[:, s, 0:h], sm_max[:, s, 0:h], -1.0 / 16, None, ALU.mult)\
                   .then_inc(sm["xat"][0], 1)

            def x_norm(m):
                kind, a, qt = XU[m]
                h = 2 if kind == "p" else 1
                s = m % SM
                drained(dve, "xs", m)
                link(dve, dve.reciprocal(sm_inv[:, s, 0:h], sm_sum[:, s, 0:h]), dve_step)
                v = S_sb[:, s, 0:h * NMEM].rearrange("p (h k) -> p h k", h=h)
                dve.tensor_tensor(v, v, sm_inv[:, s, 0:h].unsqueeze(2).to_broadcast([P, h, NMEM]), ALU.mult)\
                   .then_inc(sm["xat"][2], 1)

            def x_out(m):
                kind, a, qt = XU[m]
                ps, free = full(dve, "xo", m)
                if kind == "p":
                    put_halves(hT, slice(0, P), slice(4 * a, 4 * a + 4), slice(qt * P, (qt + 1) * P),
                               ps.rearrange("p (c t) -> p c t", c=4), free)
                else:
                    put_halves(hT, slice(0, P), slice(0, KT), slice(SEQ + DEC_T * a, SEQ + DEC_T * (a + 1)),
                               ps[:, 0:P].rearrange("p (c t) -> p c t", c=KT), free)

            for m in range(len(XU) + 3):
                if m < len(XU):
                    x_max(m)
                if 1 <= m < len(XU) + 1:
                    x_norm(m - 1)
                if m >= 3:
                    x_out(m - 3)
            residual("co", 14, x_cross, "ffn")
            dve.tensor_copy(iota16, iota.unsqueeze(2).to_broadcast([P, NK, OHB]))

            def top16(vals, idx, src, n):
                link(dve, dve.max(vals[:, 0:8], src), dve_step)
                dve.max_index(idx[:, 0:8], vals[:, 0:8], src)
                link(dve, dve.match_replace(srep[:, 0:n], vals[:, 0:8], src, NEG), dve_step)
                link(dve, dve.max(vals[:, 8:16], srep[:, 0:n]), dve_step)
                link(dve, dve.max_index(idx[:, 8:16], vals[:, 8:16], srep[:, 0:n]), dve_step)

            def take_scores(u):
                for t in range(NT):
                    ps, free = full(dve, "sc", u, t)
                    dve.tensor_copy(s_ring[:, u % 2, t, :], ps).then_inc(free, 1)
                    drained(dve, "sc", u, t)

            take_scores(16)
            for u in range(16, 20):
                for t in range(NT):
                    if t == NT - 1 and u < 19:
                        take_scores(u + 1)
                    for j in range(4):
                        jj = 4 * (u - 16) + j
                        top16(top_v[:, t, jj, :], top_i[:, t, jj * TOPK:(jj + 1) * TOPK],
                              s_ring[:, u % 2, t, j * NK:(j + 1) * NK], NK)
            link(dve, dve.tensor_copy(place, iota[:, 0:TOPK]), dve_step)
            for t in range(NT):
                v = top_v[:, t].rearrange("p (h two) k -> p h two k", two=2)
                for h in range(PH):
                    link(dve, dve.tensor_tensor(cand[:, h, :].rearrange("p (a b) -> p a b", a=TOPK),
                                                v[:, h, 0, :].unsqueeze(2).to_broadcast([P, TOPK, TOPK]),
                                                v[:, h, 1, :].unsqueeze(1).to_broadcast([P, TOPK, TOPK]), ALU.add),
                         dve_step)
                for h in range(PH):
                    top16(ts[:, h, :], tp[:, h * TOPK:(h + 1) * TOPK], cand[:, h, :], 256)
                link(dve, dve.tensor_tensor(sg.rearrange("p (h k) -> p h k", h=PH), ts,
                                            ts[:, :, 0:1].to_broadcast([P, PH, TOPK]), ALU.subtract), dve_step)
                dve.sem_inc(tk_exp_in, 1)
                link(dve, dve.tensor_scalar(ji[:, 0, :], tp, 4, None, ALU.logical_shift_right), dve_step)
                link(dve, dve.tensor_scalar(ji[:, 1, :], tp, 15, None, ALU.bitwise_and), dve_step)
                link(dve, dve.tensor_copy(jh, ji), dve_step)
                for half in range(2):
                    link(dve, dve.tensor_copy(topif[:, half], top_i[:, t, :].rearrange(
                        "p (h two k) -> p h two k", two=2, k=TOPK)[:, :, half, :]), dve_step)
                for half in range(2):
                    link(dve, dve.tensor_tensor(eq, jh[:, half, :].unsqueeze(2).to_broadcast([P, P, TOPK]),
                                                place.unsqueeze(1).to_broadcast([P, P, TOPK]), ALU.is_equal),
                         dve_step)
                    e4 = eq.rearrange("p (h k) j -> p h k j", h=PH)
                    link(dve, dve.tensor_tensor(e4, e4, topif[:, half].unsqueeze(2).to_broadcast([P, PH, TOPK, TOPK]),
                                                ALU.mult), dve_step)
                    link(dve, dve.tensor_reduce(jf[:, half, :], eq, AX.X, ALU.add), dve_step)
                dve.wait_ge(tk_exp, t + 1)
                g = sg.rearrange("p (h k) -> p h k", h=PH)
                link(dve, dve.tensor_reduce(gsum, g, AX.X, ALU.add), dve_step)
                link(dve, dve.reciprocal(gsum, gsum), dve_step)
                dve.tensor_tensor(g, g, gsum.unsqueeze(2).to_broadcast([P, PH, TOPK]), ALU.mult).then_inc(tk_done, 1)
                dve.wait_ge(sel_mm, t + 1)
                c = slice(t * P, (t + 1) * P)
                link(dve, dve.tensor_scalar(sel16[:, 0, c], PS[:, 4, 0:P], USCALE, None, ALU.mult), dve_step)
                link(dve, dve.scalar_tensor_tensor(out=sel16[:, 1, c], in0=PS[:, 4, 0:P], scalar=USCALE,
                                                   in1=sel16[:, 0, c], op0=ALU.mult, op1=ALU.subtract), dve_step)
                link(dve, dve.tensor_copy(sel16[:, 2:4, c], PS[:, 4, P:3 * P].rearrange("p (a b) -> p a b", a=2)),
                     dve_step)
                for j in range(P // OHB):
                    n = t * (P // OHB) + j
                    if n >= 2:
                        dve.wait_ge(wg_mm, 4 * (n - 1))

                    def col(x):
                        return sel16[:, x, t * P + OHB * j:t * P + OHB * (j + 1)].unsqueeze(1)\
                            .to_broadcast([P, NK, OHB])

                    link(dve, dve.tensor_tensor(eqa, iota16, col(2), ALU.is_equal), dve_step)
                    dve.tensor_tensor(oh[:, n % 2, 2], iota16, col(3), ALU.is_equal).then_inc(dve_step, 1)
                    dve.tensor_tensor(oh[:, n % 2, 0], eqa, col(0), ALU.mult).then_inc(dve_step, 1)
                    count[id(dve_step)] += 2
                    link(dve, dve.tensor_tensor(oh[:, n % 2, 1], eqa, col(1), ALU.mult), dve_step)
                    dve.sem_inc(oh_s, 1)

            def u_low(k, n):
                dve.wait_ge(u_hi, n + 1)
                dve.scalar_tensor_tensor(out=u16[:, k, 1, :, :], in0=ust[:, k, :, :], scalar=USCALE,
                                         in1=u16[:, k, 0, :, :], op0=ALU.mult, op1=ALU.subtract).then_inc(u_sp, 1)

            def v_low(k, par, n):
                dve.wait_ge(v_hi, n + 1)
                dve.tensor_tensor(v16[:, EB * par + k, 1, :], vst[:, k, :], v16[:, EB * par + k, 0, :],
                                  ALU.subtract).then_inc(v_sp, 1)

            def gated(k, par, n, gel):
                dve.tensor_tensor(a32[:, k % 2, :].rearrange("p (g t) -> p g t", g=NTG),
                                  gel[:, k % 2, :].rearrange("p (g t) -> p g t", g=NTG), W_sb[:, par, :, k, :],
                                  ALU.mult).then_inc(a_mul, 1)
                dve.wait_ge(a_hi, n + 1)
                dve.tensor_tensor(a16[:, EB * par + k, 1, :], a32[:, k % 2, :], a16[:, EB * par + k, 0, :],
                                  ALU.subtract).then_inc(a_sp, 1)

            def y_tile(par, B, k):
                v_low(k, par, B * EB + k)
                if k == 0:
                    dve.wait_ge(W_in[par], B * 8 + (16 - 8 * par))
                dve.wait_ge(g_in[k % 2], B * 32 + (16 * (k // 2) + 16))
                gated(k, par, B * EB + k, gel_back)

            def zy_tiles(par, B):
                for k in range(EB):
                    v_low(k, par, B * EB + k)
                    dve.wait_ge(z_ge, B * EB + (k + 1))
                    if k == 0:
                        dve.wait_ge(W_in[par], B * 8 + (16 - 8 * par))
                    gated(k, par, B * EB + k, gel)

            def y_add(par, B, g):
                t, half = g // 2, g % 2
                dve.wait_ge(y_mm, B * (2 * NT) + (g + 1))
                c = slice(half * 512, half * 512 + 512)
                dve.tensor_tensor(X[:, t, c], X[:, t, c], PS[:, 4 + (par * 2 * NT + g) % 4, :], ALU.add)\
                   .then_inc(y_ev, 1)

            def y_pass(par, B):
                for g in range(2 * NT):
                    if g % 2 == 0 and g < 2 * EB:
                        y_tile(1 - par, B + 1, g // 2)
                    y_add(par, B, g)

            def zy_pass(par, B):
                for g in range(2 * NT):
                    if g % 2 == 0 and g < 2 * EB:
                        u_low(g // 2, B * EB + (2 * EB + g // 2))
                    y_add(par, B, g)
                zy_tiles(par, B + 2)

            for k in range(EB):
                y_tile(0, 0, k)
            y_pass(0, 0)
            with dve.Fori(0, AHEAD // 2 - 1) as i:
                for s in range(2):
                    y_pass(1 - s, i * 2 + (1 + s))
            zy_tiles(0, AHEAD)
            with dve.Fori(0, (NBLK - AHEAD) // 2 - 1) as i:
                for s in range(2):
                    zy_pass(1 - s, i * 2 + (AHEAD - 1 + s))
            zy_pass(1, NBLK - 3)
            for B in (NBLK - 2, NBLK - 1):
                for g in range(2 * NT):
                    y_add(B % 2, B, g)


def kernel(**inputs):
    import numpy as np
    import concourse.bacc as _bacc
    from concourse import mybir as _mybir
    from concourse.bass_utils import run_bass_kernel_spmd as _run

    a = {k: np.asarray(v) for k, v in inputs.items()}
    f = np.float32
    x = np.concatenate([a["x_prompt"][0], a["x_sample"].reshape(128, 1024)], axis=0)
    w_in = a["w_in"][0]
    q, m = np.arange(128)[:, None], np.arange(512)[None, :]
    rb = a["rel_bias"][0]
    bias_p = rb[:, np.clip(q + 384 - m, -128, 128) + 128]
    blocked = np.broadcast_to((q < 64) & (m >= 448), bias_p.shape)
    bias_p = np.where(blocked, f(-1e30), bias_p).astype(f)
    i, j = np.arange(16)[:, None], np.arange(528)[None, :]
    bias_s = rb[:, np.clip(512 + i - j, -128, 128) + 128].reshape(128, 528)
    kc = a["cache_att_k"][0][:, 64:].reshape(8, 512, 4, 128).transpose(0, 3, 2, 1)
    vc = a["cache_att_v"][0][:, 64:].reshape(8, 4, 128, 512).transpose(0, 2, 1, 3)
    mkc = a["cache_mem_k"][0].reshape(8, 256, 8, 128).transpose(0, 3, 2, 1)
    mvc = a["cache_mem_v"][0].reshape(8, 2, 128, 1024).transpose(0, 2, 1, 3)
    state = a["state_gla"][0].reshape(8, 2, 128, 128)
    u_t = a["expert_u"][0].reshape(128, 128, 8, 128).transpose(1, 3, 2, 0).reshape(128, 128, 1024)
    v_t = a["expert_v"][0].reshape(128, 128, 1024).transpose(1, 0, 2)
    gcols = np.stack([a[n][0].reshape(8, 128).T for n in ("g_mix", "g_mem", "g_cross", "g_ffn")], axis=1)
    grow = np.concatenate([a[n][0] for n in ("g_q", "g_k", "g_gla_out", "g_cq", "g_ck")])
    grows = np.broadcast_to(grow, (128, 768))
    wg2 = np.concatenate([a["w_gate2"][0], a["b_gate2"]], axis=0)
    keys = np.stack([a["sub_keys1"][0].T, a["sub_keys2"][0].T])
    s, t = np.arange(128)[:, None], np.arange(128)[None, :]

    def tri(L):
        same = (s // L) == (t // L)
        mid = (s // L) * L + L // 2 - 1
        centred = (same & (s <= t)).astype(f) - (same & (s <= mid)).astype(f)
        mids = ((s // L) == np.arange(128 // L)[None, :]).astype(f) * (s <= mid)
        return np.concatenate([centred, mids], axis=1) / 16.0

    def causal(L):
        return (((s // L) == (t // L)) & (s <= t)).astype(f)

    consts = np.concatenate([np.eye(128), np.broadcast_to(np.arange(128), (128, 128)), causal(64), causal(16),
                             tri(64), tri(16), (s // 16) == np.arange(8)[None, :]], axis=1).astype(f)
    arrays = {"x_in": x, "mem_in": a["mem_prompt"][0], "w_in": w_in, "w_gl": w_in[:, 2560:2576], "w_out": a["w_out"][0],
              "w_cq": a["w_cq"][0], "w_ck": a["w_ck"][0], "w_cv": a["w_cv"][0], "w_co": a["w_co"][0],
              "w_pq": a["w_pq"][0], "wg2": wg2, "gcols": gcols, "grows": grows, "bias_p": bias_p, "bias_s": bias_s,
              "kc_t": kc, "v_c": vc, "state_in": state, "mk_c": mkc, "mv_c": mvc, "keys_t": keys, "u_t": u_t,
              "v_t": v_t, "consts": consts}
    arrays = {k: np.ascontiguousarray(v) for k, v in arrays.items()}
    outs = {"y_out": (640, 1024), "k_out": (640, 512), "v_out": (640, 512), "gp_out": (2, 128, 128),
            "gs_out": (8, 2, 128, 128), "mk_out": (256, 1024), "mv_out": (256, 1024)}

    nc = _bacc.Bacc("TRN2", target_bir_lowering=False, num_devices=1)
    F = _mybir.dt.float32
    aps = {k: nc.dram_tensor(k, v.shape, F, kind="ExternalInput").ap() for k, v in arrays.items()}
    aps |= {k: nc.dram_tensor(k, v, F, kind="ExternalOutput").ap() for k, v in outs.items()}
    w_dram = nc.dram_tensor("w_dram", (NBLK, P, NTG, EB * TG), F).ap()
    g_dram = nc.dram_tensor("g_dram", (NA, P, T), F).ap()
    peer_stream_step(nc, w_dram=w_dram, g_dram=g_dram, **aps)
    r = _run(nc, [arrays], core_ids=[0]).results[0]
    y, k, v = r["y_out"], r["k_out"], r["v_out"]
    return (y[:512].reshape(1, 512, 1024), y[512:].reshape(8, 16, 1024),
            k[:512].reshape(1, 1, 512, 8, 64), v[:512].reshape(1, 1, 512, 8, 64),
            r["gp_out"].reshape(1, 1, 4, 64, 128),
            r["mk_out"].reshape(1, 1, 256, 4, 256), r["mv_out"].reshape(1, 1, 256, 4, 256),
            k[512:].reshape(1, 8, 16, 8, 64), v[512:].reshape(1, 8, 16, 8, 64),
            r["gs_out"].reshape(1, 8, 4, 64, 128))
```
